# Optimizing a Trainium2 kernel written in Bass

```python
import jax, jax.numpy as jnp
from jax import lax
import numpy as np

'''One inference step of a hybrid streaming encoder (Hymba-style parallel head groups).

Each layer: h = h + W_out [ silu(g_A) * ChunkBandAttn(...) ; silu(g_B) * RWKV7(...) ]
with ONE combined input projection of RMSNorm(h) partitioned among the two head groups.

Inputs:
  x_prompt          (BATCH, SEQ, D_MODEL)           first SEQ frames of BATCH new streams
  x_sample          (DEC_BATCH, DEC_SEQ, D_MODEL)   next DEC_SEQ frames of DEC_BATCH running streams
  cache_attn_k/v    (DEPTH, DEC_BATCH, ATT_HEADS, min(LEFT_CONTEXT, PAST_LEN), HEAD_DIM)
                    QK-normed keys / values of the newest visible past rows (chunk band)
  state_rwkv_wkv    (DEPTH, DEC_BATCH, RWKV_HEADS, HEAD_DIM, HEAD_DIM)  RWKV-7 matrix state S[v, k]
  state_rwkv_shift  (DEPTH, DEC_BATCH, 1, RWKV_SHIFT_COLS)  last projected row (token-shift buffer)
  followed by the layer weights (leading DEPTH axis).
Output tuple:
  (y_prompt (BATCH, SEQ, D_MODEL),
   y_sample (DEC_BATCH, DEC_SEQ, D_MODEL),
   k_prompt_new (DEPTH, BATCH, ATT_HEADS, min(LEFT_CONTEXT, SEQ), HEAD_DIM),
   v_prompt_new (same),
   k_sample_new (DEPTH, DEC_BATCH, ATT_HEADS, DEC_SEQ, HEAD_DIM),
   v_sample_new (same),
   wkv_prompt_new (DEPTH, BATCH, RWKV_HEADS, HEAD_DIM, HEAD_DIM),
   wkv_sample_new (DEPTH, DEC_BATCH, RWKV_HEADS, HEAD_DIM, HEAD_DIM),
   shift_prompt_new (DEPTH, BATCH, 1, RWKV_SHIFT_COLS),
   shift_sample_new (DEPTH, DEC_BATCH, 1, RWKV_SHIFT_COLS))
'''

D_MODEL = 1024
BATCH = 1
SEQ = 2048
DEPTH = 1
DEC_BATCH = 8
DEC_SEQ = 16
PAST_LEN = 256

CHUNK = 64
LEFT_CHUNKS = 8
LEFT_CONTEXT = LEFT_CHUNKS * CHUNK
MIX_WIDTH = D_MODEL
HEAD_DIM = 64
ATT_WIDTH = MIX_WIDTH // 2
RWKV_WIDTH = MIX_WIDTH - ATT_WIDTH
ATT_HEADS = ATT_WIDTH // HEAD_DIM
RWKV_HEADS = RWKV_WIDTH // HEAD_DIM
MAX_REL_DIST = 128
DECAY_LORA = 64
ICLR_LORA = 64
RMS_EPS = 1e-6
GN_EPS = 64e-5
ATT_COLS = 4 * ATT_WIDTH
RWKV_SHIFT_COLS = 3 * RWKV_WIDTH + DECAY_LORA + ICLR_LORA
IN_COLS = ATT_COLS + RWKV_SHIFT_COLS + RWKV_WIDTH

kernel_name = 'hymba_chunkattn_rwkv7_stream_step'

F32 = jnp.float32

def rms_norm(x, g):
    xf = x.astype(F32)
    y = xf * lax.rsqrt(jnp.mean(xf * xf, axis=-1, keepdims=True) + RMS_EPS)
    return (y * g.astype(F32)).astype(x.dtype)

def rel_bias(table, q_pos, k_pos):
    rel = jnp.clip(q_pos[:, None] - k_pos[None, :], -MAX_REL_DIST, MAX_REL_DIST) + MAX_REL_DIST
    return table.astype(F32)[:, rel]

def split_projection(proj):
    att = proj[..., :ATT_COLS]
    rcols = proj[..., ATT_COLS:ATT_COLS + RWKV_SHIFT_COLS]
    g_r = proj[..., ATT_COLS + RWKV_SHIFT_COLS:]
    return att, rcols, g_r

def attn_qkv(att, q_gain, k_gain):
    B, T, _ = att.shape
    q, k, v, g = jnp.split(att, 4, axis=-1)
    q = rms_norm(q.reshape(B, T, ATT_HEADS, HEAD_DIM), q_gain)
    k = rms_norm(k.reshape(B, T, ATT_HEADS, HEAD_DIM), k_gain)
    v = v.reshape(B, T, ATT_HEADS, HEAD_DIM)
    return q, k, v, g

def chunk_band_attention(q, k, v, table):
    B, T, H, Dh = q.shape
    nc = T // CHUNK
    pad = ((0, 0), (LEFT_CONTEXT, 0), (0, 0), (0, 0))
    kp = jnp.pad(k, pad).reshape(B, nc + LEFT_CHUNKS, CHUNK, H, Dh)
    vp = jnp.pad(v, pad).reshape(B, nc + LEFT_CHUNKS, CHUNK, H, Dh)
    kb = jnp.concatenate([kp[:, j:j + nc] for j in range(LEFT_CHUNKS + 1)], axis=2)
    vb = jnp.concatenate([vp[:, j:j + nc] for j in range(LEFT_CHUNKS + 1)], axis=2)
    qc = q.reshape(B, nc, CHUNK, H, Dh)
    s = jnp.einsum('bnqhd,bnkhd->bnhqk', qc.astype(F32), kb.astype(F32)) * (Dh ** -0.5)
    q_off = jnp.arange(CHUNK, dtype=jnp.int32)
    k_off = jnp.arange((LEFT_CHUNKS + 1) * CHUNK, dtype=jnp.int32) - LEFT_CONTEXT
    s = s + rel_bias(table, q_off, k_off)[None, None]
    valid = (jnp.arange(nc, dtype=jnp.int32)[:, None] * CHUNK + k_off[None, :]) >= 0
    s = jnp.where(valid[None, :, None, None, :], s, jnp.finfo(F32).min)
    p = jax.nn.softmax(s, axis=-1)
    o = jnp.einsum('bnhqk,bnkhd->bnqhd', p, vb.astype(F32))
    return o.reshape(B, T, H * Dh)

def cached_band_attention(q, k_new, v_new, cache_k, cache_v, table):
    B, Tn, H, Dh = q.shape
    W = cache_k.shape[2]
    kc = jnp.concatenate([cache_k.astype(F32), k_new.transpose(0, 2, 1, 3).astype(F32)], axis=2)
    vc = jnp.concatenate([cache_v.astype(F32), v_new.transpose(0, 2, 1, 3).astype(F32)], axis=2)
    s = jnp.einsum('bqhd,bhkd->bhqk', q.astype(F32), kc) * (Dh ** -0.5)
    q_off = jnp.arange(Tn, dtype=jnp.int32)
    k_off = jnp.arange(W + Tn, dtype=jnp.int32) - W
    s = s + rel_bias(table, q_off, k_off)[None]
    p = jax.nn.softmax(s, axis=-1)
    o = jnp.einsum('bhqk,bhkd->bqhd', p, vc)
    return o.reshape(B, Tn, H * Dh)

def wkv_scan(r, decay, k, v, kk, a, state0):
    def step(S, inp):
        r_t, w_t, k_t, v_t, kk_t, a_t = inp
        sa = jnp.einsum('bhij,bhj->bhi', S, -kk_t)
        S = (S * w_t[:, :, None, :] + sa[..., None] * (kk_t * a_t)[:, :, None, :]
             + v_t[..., None] * k_t[:, :, None, :])
        y = jnp.einsum('bhij,bhj->bhi', S, r_t)
        return S, y
    xs = tuple(jnp.moveaxis(t, 1, 0) for t in (r, decay, k, v, kk, a))
    S, ys = lax.scan(step, state0.astype(F32), xs)
    return jnp.moveaxis(ys, 0, 1), S

def rwkv_branch(cur, prev, state0, g, mix, w0, w_up, a0, a_up, k_k, k_a, r_k, gn_g, gn_b):
    B, T, _ = cur.shape
    xs = cur + (prev - cur) * mix
    r, k, v, wd, ad = jnp.split(xs, [RWKV_WIDTH, 2 * RWKV_WIDTH, 3 * RWKV_WIDTH,
                                     3 * RWKV_WIDTH + DECAY_LORA], axis=-1)
    w = -jax.nn.softplus(-(w0 + jnp.tanh(wd) @ w_up).astype(F32)) - 0.5
    decay = jnp.exp(-jnp.exp(w))
    a = jax.nn.sigmoid((a0 + ad @ a_up).astype(F32))
    heads = lambda t: t.astype(F32).reshape(B, T, RWKV_HEADS, HEAD_DIM)
    kk = heads(k * k_k)
    kk = kk * lax.rsqrt(jnp.maximum(jnp.sum(kk * kk, axis=-1, keepdims=True), 1e-24))
    k = k.astype(F32) * (1.0 + (a - 1.0) * k_a.astype(F32))
    r, k, v, a, decay = heads(r), heads(k), heads(v), heads(a), heads(decay)
    y, S = wkv_scan(r, decay, k, v, kk, a, state0)
    mu = jnp.mean(y, axis=-1, keepdims=True)
    var = jnp.mean(jnp.square(y - mu), axis=-1, keepdims=True)
    y = ((y - mu) * lax.rsqrt(var + GN_EPS)).reshape(B, T, RWKV_WIDTH) * gn_g.astype(F32) + gn_b.astype(F32)
    y = y + (jnp.sum(r * k * r_k.astype(F32), axis=-1, keepdims=True) * v).reshape(B, T, RWKV_WIDTH)
    return y * jax.nn.silu(g.astype(F32)), S

def merge_out(o_a, g_a, o_r, w_out, dtype):
    z = jnp.concatenate([o_a * jax.nn.silu(g_a.astype(F32)), o_r], axis=-1)
    return (z.astype(dtype) @ w_out).astype(dtype)

def setup_inputs(seed: int = 0) -> dict:
    key = jax.random.key(seed)
    ks = jax.random.split(key, 24)
    n = lambda i, shape: jax.random.normal(ks[i], shape, F32)
    win = min(LEFT_CONTEXT, PAST_LEN)
    return {
        'x_prompt': n(0, (BATCH, SEQ, D_MODEL)),
        'x_sample': n(1, (DEC_BATCH, DEC_SEQ, D_MODEL)),
        'cache_attn_k': n(2, (DEPTH, DEC_BATCH, ATT_HEADS, win, HEAD_DIM)),
        'cache_attn_v': n(3, (DEPTH, DEC_BATCH, ATT_HEADS, win, HEAD_DIM)),
        'state_rwkv_wkv': 0.1 * n(4, (DEPTH, DEC_BATCH, RWKV_HEADS, HEAD_DIM, HEAD_DIM)),
        'state_rwkv_shift': n(5, (DEPTH, DEC_BATCH, 1, RWKV_SHIFT_COLS)),
        'norm_gain': 1.0 + 0.05 * n(6, (DEPTH, D_MODEL)),
        'w_in': n(7, (DEPTH, D_MODEL, IN_COLS)) * D_MODEL ** -0.5,
        'q_norm_gain': 1.0 + 0.05 * n(8, (DEPTH, HEAD_DIM)),
        'k_norm_gain': 1.0 + 0.05 * n(9, (DEPTH, HEAD_DIM)),
        'rel_pos_bias': 0.1 * n(10, (DEPTH, ATT_HEADS, 2 * MAX_REL_DIST + 1)),
        'shift_mix': jax.random.uniform(ks[11], (DEPTH, RWKV_SHIFT_COLS), F32),
        'decay_base': jax.random.uniform(ks[12], (DEPTH, RWKV_WIDTH), F32, -6.0, -1.0),
        'decay_lora_up': 0.1 * n(13, (DEPTH, DECAY_LORA, RWKV_WIDTH)),
        'iclr_base': 0.1 * n(14, (DEPTH, RWKV_WIDTH)),
        'iclr_lora_up': n(15, (DEPTH, ICLR_LORA, RWKV_WIDTH)) * ICLR_LORA ** -0.5,
        'key_remove_scale': 0.85 + 0.05 * n(16, (DEPTH, RWKV_WIDTH)),
        'key_iclr_scale': 1.0 + 0.05 * n(17, (DEPTH, RWKV_WIDTH)),
        'bonus_scale': 0.1 * n(18, (DEPTH, RWKV_HEADS, HEAD_DIM)),
        'out_norm_gain': 1.0 + 0.05 * n(19, (DEPTH, RWKV_WIDTH)),
        'out_norm_bias': 0.01 * n(20, (DEPTH, RWKV_WIDTH)),
        'w_out': n(21, (DEPTH, MIX_WIDTH, D_MODEL)) * MIX_WIDTH ** -0.5,
    }

def reference(x_prompt, x_sample, cache_attn_k, cache_attn_v, state_rwkv_wkv, state_rwkv_shift,
              norm_gain, w_in, q_norm_gain, k_norm_gain, rel_pos_bias, shift_mix,
              decay_base, decay_lora_up, iclr_base, iclr_lora_up, key_remove_scale,
              key_iclr_scale, bonus_scale, out_norm_gain, out_norm_bias, w_out):
    h_p, h_s = x_prompt, x_sample
    kp_l, vp_l, ks_l, vs_l, sp_l, ss_l, shp_l, shs_l = [], [], [], [], [], [], [], []
    for l in range(DEPTH):
        rw = (shift_mix[l], decay_base[l], decay_lora_up[l], iclr_base[l], iclr_lora_up[l],
              key_remove_scale[l], key_iclr_scale[l], bonus_scale[l], out_norm_gain[l], out_norm_bias[l])
        B, T, _ = h_p.shape
        proj = rms_norm(h_p, norm_gain[l]) @ w_in[l]
        att, rcols, g_r = split_projection(proj)
        q, k, v, g_a = attn_qkv(att, q_norm_gain[l], k_norm_gain[l])
        o_a = chunk_band_attention(q, k, v, rel_pos_bias[l])
        prev = jnp.concatenate([jnp.zeros_like(rcols[:, :1]), rcols[:, :-1]], axis=1)
        o_r, S_p = rwkv_branch(rcols, prev, jnp.zeros((B, RWKV_HEADS, HEAD_DIM, HEAD_DIM), F32), g_r, *rw)
        h_p = h_p + merge_out(o_a, g_a, o_r, w_out[l], h_p.dtype)
        win = min(LEFT_CONTEXT, T)
        kp_l.append(k[:, T - win:].transpose(0, 2, 1, 3))
        vp_l.append(v[:, T - win:].transpose(0, 2, 1, 3))
        sp_l.append(S_p)
        shp_l.append(rcols[:, -1:])
        proj = rms_norm(h_s, norm_gain[l]) @ w_in[l]
        att, rcols, g_r = split_projection(proj)
        q, k, v, g_a = attn_qkv(att, q_norm_gain[l], k_norm_gain[l])
        o_a = cached_band_attention(q, k, v, cache_attn_k[l], cache_attn_v[l], rel_pos_bias[l])
        prev = jnp.concatenate([state_rwkv_shift[l].astype(rcols.dtype), rcols[:, :-1]], axis=1)
        o_r, S_s = rwkv_branch(rcols, prev, state_rwkv_wkv[l], g_r, *rw)
        h_s = h_s + merge_out(o_a, g_a, o_r, w_out[l], h_s.dtype)
        ks_l.append(k.transpose(0, 2, 1, 3))
        vs_l.append(v.transpose(0, 2, 1, 3))
        ss_l.append(S_s)
        shs_l.append(rcols[:, -1:])
    return (h_p, h_s, jnp.stack(kp_l), jnp.stack(vp_l), jnp.stack(ks_l), jnp.stack(vs_l),
            jnp.stack(sp_l), jnp.stack(ss_l), jnp.stack(shp_l), jnp.stack(shs_l))


_drawn_inputs = setup_inputs


def setup_inputs(seed=0):
    import zlib

    import numpy as np

    out = dict(_drawn_inputs(seed))
    spreads = {}
    factors = {'q_norm_gain': 8.0, 'rel_pos_bias': 8.0, 'out_norm_gain': 3.085, 'out_norm_bias': 23.124}
    for name, (base, spread) in spreads.items():
        noise = np.random.default_rng([zlib.crc32(name.encode()), seed]).standard_normal(out[name].shape)
        drawn = base * np.exp(spread * noise) if base else spread * noise
        out[name] = __import__('jax').numpy.asarray(drawn.astype(out[name].dtype))
    for name, factor in factors.items():
        out[name] = (out[name] * factor).astype(out[name].dtype)
    return out
```

```python
from contextlib import ExitStack

import concourse.bass as bass
from concourse import mybir

F32 = mybir.dt.float32
F32R = mybir.dt.float32r
ACT = mybir.ActivationFunctionType
ALU = mybir.AluOpType
AX_X = mybir.AxisListType.X

P = 128
D = 1024
KT = D // P
HD = 64
H = 8
PAIRS = H // 2
AW = H * HD
TILES = 16
DEC = TILES
NS, SL = 8, 16
PAST = 256
SLOTS = 5
WIN = SLOTS * P
NEAR = 2 * P
FAR = WIN - NEAR
MAXREL = 128
CH = 64
MASKED = -3.0e38
SCALE = HD ** -0.5
EPS = 1e-6
SHIFT_COLS = 3 * AW + 128
ACT_TABLES = "natural_log_exp_and_others"


def wait(eng, sem, value):
    if isinstance(value, int) and value <= 0:
        return
    eng.wait_ge(sem, value)


def t_known(t):
    return isinstance(t, int)


def rows_of(dram, width):
    return dram.rearrange("b s d -> (b s) d")


def prompt_steps(eng, step):
    for t in range(4):
        step(t, t % 2)
    with eng.Fori(4, 12, 2) as t:
        step(t, 0)
        step(t + 1, 1)
    for t in range(12, TILES):
        step(t, t % 2)


def clear_semaphores(nc, held):
    with nc.Block() as block:
        @block.gpsimd
        def _(pool):
            for sem in held:
                pool.sem_clear(sem)


def attention_phase(nc, io):
    with ExitStack() as ctx:
        def sb(name, shape, dt=F32):
            return ctx.enter_context(nc.sbuf_tensor(name, shape, dt))

        held = []

        def sem(name):
            held.append(ctx.enter_context(nc.semaphore(name)))
            return held[-1]

        QKV = 3 * AW
        w_hi = sb("a_w_hi", [P, KT, QKV], F32R)
        w_lo = sb("a_w_lo", [P, KT, QKV], F32R)
        w_raw = [sb(f"a_w_raw{i}", [P, KT, P]) for i in range(2)]
        x_tok = [sb(f"a_x{i}", [P, D]) for i in range(2)]
        xT = sb("a_xT", [P, KT, P])
        x_hi = [sb(f"a_x_hi{i}", [P, KT, P], F32R) for i in range(2)]
        x_lo = [sb(f"a_x_lo{i}", [P, KT, P], F32R) for i in range(2)]
        ident = sb("a_ident", [P, P])
        gainT = sb("a_gainT", [P, KT])
        qk_gain = sb("a_qk_gain", [P, 2, HD])
        near_bias = sb("a_near_bias", [P, H, NEAR])
        far_mask = sb("a_far_mask", [P, FAR])
        far_value = sb("a_far_value", [P, H])
        qk = sb("a_qk", [P, 2, AW])
        qk_n = sb("a_qk_n", [P, 2, AW])
        qT = sb("a_qT", [P, PAIRS, P])
        kT = [sb(f"a_kT{i}", [P, PAIRS, WIN]) for i in range(2)]
        v = [sb(f"a_v{i}", [P, SLOTS, AW]) for i in range(2)]
        probs = [sb(f"a_probs{i}", [P, WIN]) for i in range(2)]
        pT = [sb(f"a_pT{i}", [P, WIN]) for i in range(2)]
        o_tok = sb("a_o", [P, H, HD])
        small = sb("a_small", [P, 64])
        sumsq, rstd, logms = small[:, 0:1], small[:, 1:2], small[:, 2:3]
        neg_max = [small[:, 3:4], small[:, 4:5]]
        row_sum = small[:, 8:16]
        row_inv = small[:, 16:24]
        qk_ss, qk_rstd, eps = small[:, 24:40], small[:, 40:56], small[:, 5:6]

        ps_proj = [ctx.enter_context(nc.psum_tensor(f"a_ps_proj{i}", [P, 512], F32)) for i in range(2)]
        ps_score = [ctx.enter_context(nc.psum_tensor(f"a_ps_score{i}", [P, 1024], F32)) for i in range(2)]
        ps_turn = ctx.enter_context(nc.psum_tensor("a_ps_turn", [P, 512], F32))
        ps_out = ctx.enter_context(nc.psum_tensor("a_ps_out", [P, 512], F32))

        consts_loaded = sem("a_consts_loaded")
        ident_zero, ident_ready = sem("a_ident_zero"), sem("a_ident_ready")
        eps_ready = sem("a_eps_ready")
        rev_zero, rev_ready, table_stored = sem("a_rev_zero"), sem("a_rev_ready"), sem("a_table_stored")
        bias_loaded, bias_near, bias_ready = sem("a_bias_loaded"), sem("a_bias_near"), sem("a_bias_ready")
        w_loaded = [sem(f"a_w_loaded{i}") for i in range(2)]
        w_hi_ready, w_lo_ready = sem("a_w_hi_ready"), sem("a_w_lo_ready")
        x_loaded = [sem(f"a_x_loaded{i}") for i in range(2)]
        x_sumsq, x_logms, x_rstd, x_scaled = sem("a_x_sumsq"), sem("a_x_logms"), sem("a_x_rstd"), sem("a_x_scaled")
        x_turned, xT_ready, xT_stored = sem("a_x_turned"), sem("a_xT_ready"), sem("a_xT_stored")
        x_hi_ready, x_lo_ready = sem("a_x_hi_ready"), sem("a_x_lo_ready")
        proj_ready, proj_read = sem("a_proj_ready"), sem("a_proj_read")
        qk_sq, qk_summed, qk_logms = sem("a_qk_sq"), sem("a_qk_summed"), sem("a_qk_logms")
        qk_rstd_ready, qk_scaled, qk_normed = sem("a_qk_rstd"), sem("a_qk_scaled"), sem("a_qk_normed")
        qk_turned, qkT_ready, shifted = sem("a_qk_turned"), sem("a_qkT_ready"), sem("a_shifted")
        score_ready, biased, max_ready = sem("a_score_ready"), sem("a_biased"), sem("a_max_ready")
        p_ready, p_turned, pT_ready, pv_done = sem("a_p_ready"), sem("a_p_turned"), sem("a_pT_ready"), sem("a_pv_done")
        inv_ready, out_ready, out_stored = sem("a_inv_ready"), sem("a_out_ready"), sem("a_out_stored")
        kv_stored = sem("a_kv_stored")

        xp, xs = rows_of(io["x_prompt"], D), rows_of(io["x_sample"], D)
        w_in = io["w_in"][0].rearrange("(k p) n -> p k n", p=P)
        table = io["rel_pos_bias"][0]
        rev = w_raw[0][0:H, :, :].rearrange("h a b -> h (a b)")[:, 0:3 * P]
        tab = w_raw[1][0:H, :, :].rearrange("h a b -> h (a b)")[:, 0:2 * MAXREL + 1]
        rev_d = io["rev_table"]
        WB = QKV // P

        PAR = [0]

        def half_count(n, u):
            return 8 * n + 16 - 8 * u

        ctx.callback(clear_semaphores, nc, held)
        block = ctx.enter_context(nc.Block())

        def x_rows(t):
            return xs if isinstance(t, int) and t == DEC else xp[bass.ds(t * P, P), :]

        def first_slot(t):
            return SLOTS - 1 - t if isinstance(t, int) and t < SLOTS - 1 else 0

        @block.sync
        def _(sp):
            sp.dma_start(tab, table).then_inc(consts_loaded, 16)
            sp.dma_start(x_tok[0][:], x_rows(0)).then_inc(x_loaded[0], 16)
            sp.dma_start(x_tok[1][:], x_rows(1)).then_inc(x_loaded[1], 16)
            sp.dma_start(gainT[:], io["norm_gain"][0].rearrange("(k p) -> p k", p=P),
                         allow_slow_non_contiguous=True).then_inc(consts_loaded, 16)
            sp.dma_start(qk_gain[:, 0, :], io["q_norm_gain"][0].partition_broadcast(P)).then_inc(consts_loaded, 16)
            sp.dma_start(qk_gain[:, 1, :], io["k_norm_gain"][0].partition_broadcast(P)).then_inc(consts_loaded, 16)
            sp.wait_ge(rev_ready, 2)
            sp.dma_start(rev_d, rev.rearrange("h (o n) -> h o n", o=1).broadcast_to([H, P, 3 * P])).then_inc(table_stored, 16)
            sp.wait_ge(table_stored, 16)
            for h in range(H):
                src = bass.AP(rev_d.tensor, h * P * 3 * P + P - 1, [[3 * P - 1, P], [1, NEAR]])
                sp.dma_start(near_bias[:, h, :], src).then_inc(bias_loaded, 16)
            sp.dma_start(far_value[:], bass.AP(rev_d.tensor, 0, [[0, P], [P * 3 * P, H]]),
                         allow_slow_non_contiguous=True).then_inc(bias_loaded, 16)
            def store_xT(n):
                sp.wait_ge(xT_ready, 2 * n + 2)
                sp.dma_start(io["xT"][bass.ds(n, 1)].rearrange("a p k n -> (a p) k n"), xT[:]).then_inc(xT_stored, 16)

            for b in range(WB):
                if b == 2:
                    store_xT(0)
                    store_xT(1)
                if b >= 2:
                    sp.wait_ge(w_lo_ready, b - 1)
                sp.dma_start(w_raw[b % 2][:], w_in[:, :, b * P:(b + 1) * P]).then_inc(w_loaded[b % 2], 16)

            def step(t, u):
                if t_known(t) and t >= 12:
                    rows = slice((t - 12) * P, (t - 11) * P)
                    sp.wait_ge(qk_normed, t + 1)
                    sp.dma_start(io["k_prompt_new"][0, 0, :, rows, :].rearrange("h s d -> s h d"),
                                 qk_n[:, 1, :].rearrange("p (h d) -> p h d", h=H)).then_inc(kv_stored, 16)
                    sp.wait_ge(proj_read, 3 * (t + 1))
                    sp.dma_start(io["v_prompt_new"][0, 0, :, rows, :].rearrange("h s d -> s h d"),
                                 v[u][:, SLOTS - 1, :].rearrange("p (h d) -> p h d", h=H)).then_inc(kv_stored, 16)
                if not (t_known(t) and t + 2 > DEC):
                    sp.wait_ge(x_turned, 2 * t + 2)
                    sp.dma_start(x_tok[u][:], x_rows(t + 2)).then_inc(x_loaded[u], 16)
                    store_xT(t + 2)
                sp.wait_ge(out_ready, t + 1)
                sp.dma_start(io["o_att"][bass.ds(t * P, P), :],
                             o_tok[:].rearrange("p h d -> p (h d)")).then_inc(out_stored, 16)

            prompt_steps(sp, step)
            sp.wait_ge(qk_normed, DEC + 1)
            sp.wait_ge(proj_read, 3 * (DEC + 1))
            for b in range(NS):
                rows = slice(b * SL, (b + 1) * SL)
                sp.dma_start(io["k_sample_new"][0, b].rearrange("h s d -> s h d"),
                             qk_n[rows, 1, :].rearrange("p (h d) -> p h d", h=H)).then_inc(kv_stored, 16)
                sp.dma_start(io["v_sample_new"][0, b].rearrange("h s d -> s h d"),
                             v[0][rows, SLOTS - 1, :].rearrange("p (h d) -> p h d", h=H)).then_inc(kv_stored, 16)
            sp.wait_ge(qkT_ready, 2 * (DEC + 1))
            sp.dma_start(io["qT_new"], qT[:]).then_inc(kv_stored, 16)
            sp.dma_start(io["kT_new"], kT[0][:, :, FAR + P:WIN]).then_inc(kv_stored, 16)
            sp.dma_start(io["v_new"], v[0][:, SLOTS - 1, :]).then_inc(kv_stored, 16)
            sp.wait_ge(kv_stored, 16 * (2 * 4 + 2 * NS + 3))
            sp.wait_ge(xT_stored, 16 * (TILES + 1))
            sp.wait_ge(out_stored, 16 * TILES)

        @block.gpsimd
        def _(pool):
            nc.gpsimd.memset(ident[:], 0.0).then_inc(ident_zero, 1)
            pool.wait_ge(ident_zero, 1)
            nc.gpsimd.affine_select(out=ident[:], in_=ident[:], compare_op=ALU.not_equal, fill=1.0, base=0,
                                    pattern=[[-1, P]], channel_multiplier=1).then_inc(ident_ready, 1)

            def split_lo(n, u):
                pool.wait_ge(x_hi_ready, n + 1)
                wait(pool, proj_ready, 3 * (n - 1))
                nc.gpsimd.tensor_tensor(x_lo[u][:], xT[:], x_hi[u][:].bitcast(F32), ALU.subtract).then_inc(x_lo_ready, 1)

            def apply_gain(n):
                pool.wait_ge(qk_scaled, n + 1)
                gain = qk_gain[:].rearrange("p g (o d) -> p g o d", o=1).broadcast_to([P, 2, H, HD])
                nc.gpsimd.tensor_tensor(qk_n[:].rearrange("p g (h d) -> p g h d", h=H),
                                        qk[:].rearrange("p g (h d) -> p g h d", h=H), gain,
                                        ALU.mult).then_inc(qk_normed, 1)

            pool.wait_ge(consts_loaded, 64)
            split_lo(0, 0)
            split_lo(1, 1)
            apply_gain(0)

            def step(t, u):
                if not t_known(t) or t < TILES - 1:
                    split_lo(t + 2, u)
                apply_gain(t + 1)

            prompt_steps(pool, step)

        @block.scalar
        def _(act):
            act.preload_act_table_set(ACT_TABLES)

            def norm_stats(n, u):
                act.wait_ge(x_loaded[u], half_count(n, u))
                wait(act, xT_ready, 2 * n)
                wait(act, x_lo_ready, n)
                wait(act, xT_stored, 16 * n)
                nc.scalar.activation(xT[:].rearrange("p k n -> p (k n)"), x_tok[u][:], ACT.Square,
                                     accum_out=sumsq).then_inc(x_sumsq, 1)
                act.wait_ge(x_sumsq, n + 1)
                act.wait_ge(eps_ready, 1)
                nc.scalar.activation(logms, sumsq, ACT.Ln, scale=1.0 / D, bias=eps).then_inc(x_logms, 1)
                act.wait_ge(x_logms, n + 1)
                wait(act, x_scaled, n)
                nc.scalar.activation(rstd, logms, ACT.Exp, scale=-0.5).then_inc(x_rstd, 1)

            def split_hi(n, u):
                act.wait_ge(xT_ready, 2 * n + 2)
                wait(act, proj_ready, 3 * (n - 1))
                nc.scalar.activation(x_hi[u][:], xT[:], ACT.Copy).then_inc(x_hi_ready, 1)

            def read_qk(n, g):
                act.wait_ge(proj_ready, 3 * n + g + 1)
                wait(act, qk_normed, n)
                nc.scalar.activation(qk[:, g, :], ps_proj[(n + g) % 2 if t_known(n) else g ^ PAR[0]][:], ACT.Copy).then_inc(proj_read, 1)

            def read_v(n, u):
                act.wait_ge(proj_ready, 3 * n + 3)
                wait(act, pv_done, H * (n - 1))
                wait(act, shifted, 2 * (n - 1))
                nc.scalar.activation(v[u][:, SLOTS - 1, :], ps_proj[u][:], ACT.Copy).then_inc(proj_read, 1)

            def square_qk(n):
                act.wait_ge(proj_read, 3 * n + 2)
                wait(act, qk_turned, 2 * n)
                if t_known(n) and n > 12:
                    act.wait_ge(kv_stored, 32 * (n - 12))
                nc.scalar.activation(qk_n[:], qk[:], ACT.Square).then_inc(qk_sq, 1)

            def qk_stats(n):
                act.wait_ge(qk_summed, n + 1)
                nc.scalar.activation(qk_rstd, qk_ss, ACT.Ln, scale=1.0 / HD, bias=eps).then_inc(qk_logms, 1)
                act.wait_ge(qk_logms, n + 1)
                nc.scalar.activation(qk_rstd, qk_rstd, ACT.Exp, scale=-0.5).then_inc(qk_rstd_ready, 1)

            def read_qT(n):
                act.wait_ge(qk_turned, 2 * n + 1)
                wait(act, score_ready, H * n)
                nc.scalar.activation(qT[:], ps_turn[:].rearrange("p (g n) -> p g n", g=PAIRS), ACT.Copy).then_inc(qkT_ready, 1)

            def read_kT(n, u):
                act.wait_ge(qk_turned, 2 * n + 2)
                wait(act, shifted, 2 * (n - 1))
                nc.scalar.activation(kT[u][:, :, FAR + P:WIN], ps_turn[:].rearrange("p (g n) -> p g n", g=PAIRS),
                                     ACT.Copy).then_inc(qkT_ready, 1)

            def exps(t, h, lo):
                act.wait_ge(max_ready, H * t + h + 1)
                if h == 0:
                    wait(act, inv_ready, t)
                nc.scalar.activation(probs[h % 2][:, lo * P:WIN], probs[h % 2][:, lo * P:WIN], ACT.Exp,
                                     bias=neg_max[h % 2], accum_out=row_sum[:, h:h + 1]).then_inc(p_ready, 1)

            def read_pT(t, h, lo):
                act.wait_ge(p_turned, H * t + h + 1)
                wait(act, pv_done, H * t + h - 1)
                nc.scalar.activation(pT[h % 2][:, lo * P:WIN], ps_score[h % 2][:, lo * P:WIN], ACT.Copy).then_inc(pT_ready, 1)

            norm_stats(0, 0)
            split_hi(0, 0)
            norm_stats(1, 1)
            split_hi(1, 1)
            for b in range(WB):
                act.wait_ge(w_loaded[b % 2], 16 * (b // 2 + 1))
                nc.scalar.activation(w_hi[:, :, b * P:(b + 1) * P], w_raw[b % 2][:], ACT.Copy).then_inc(w_hi_ready, 1)
            PAR[0] = 0
            read_qk(0, 0)
            read_qk(0, 1)
            square_qk(0)
            qk_stats(0)
            read_v(0, 0)
            read_qT(0)
            read_kT(0, 0)

            def step(t, u):
                PAR[0] = 1 - u
                lo = first_slot(t)
                more = not t_known(t) or t < TILES - 1
                for h in range(H):
                    if h >= 1:
                        read_pT(t, h - 1, lo)
                    exps(t, h, lo)
                    if h == 2:
                        read_qk(t + 1, 0)
                        if more:
                            norm_stats(t + 2, u)
                    if h == 5:
                        read_qk(t + 1, 1)
                        square_qk(t + 1)
                    if h == 6:
                        if more:
                            split_hi(t + 2, u)
                        qk_stats(t + 1)
                read_v(t + 1, 1 - u)
                read_qT(t + 1)
                read_pT(t, H - 1, lo)
                read_kT(t + 1, 1 - u)

            prompt_steps(act, step)

        @block.vector
        def _(dve):
            def norm_x(n, u):
                dve.wait_ge(x_rstd, n + 1)
                nc.vector.tensor_scalar(x_tok[u][:], x_tok[u][:], rstd, None, ALU.mult).then_inc(x_scaled, 1)

            def read_xT(n, j):
                dve.wait_ge(x_turned, 2 * n + j + 1)
                gain = gainT[:, 4 * j:4 * j + 4].rearrange("p (k o) -> p k o", o=1).broadcast_to([P, 4, P])
                nc.vector.tensor_tensor(xT[:, 4 * j:4 * j + 4, :], ps_turn[:].rearrange("p (k n) -> p k n", k=4),
                                        gain, ALU.mult).then_inc(xT_ready, 1)

            def sum_qk(n):
                dve.wait_ge(qk_sq, n + 1)
                nc.vector.tensor_reduce(qk_ss, qk_n[:].rearrange("p g (h d) -> p (g h) d", h=H), AX_X,
                                        ALU.add).then_inc(qk_summed, 1)

            def scale_qk(n):
                dve.wait_ge(qk_rstd_ready, n + 1)
                r = qk_rstd.rearrange("p (g o) -> p g o", o=1).broadcast_to([P, 2 * H, HD])
                x = qk[:].rearrange("p g (h d) -> p (g h) d", h=H)
                nc.vector.tensor_tensor(x, x, r, ALU.mult).then_inc(qk_scaled, 1)

            def bias_and_max(t, h, lo):
                dve.wait_ge(score_ready, H * t + h + 1)
                wait(dve, p_turned, H * t + h - 1)
                s, out = ps_score[h % 2], probs[h % 2]
                if lo * P < FAR:
                    nc.vector.scalar_tensor_tensor(out=out[:, lo * P:FAR], in0=s[:, lo * P:FAR], scalar=SCALE,
                                                   in1=far_mask[:, lo * P:FAR], op0=ALU.mult, op1=ALU.add)
                near = max(lo * P, FAR)
                nc.vector.scalar_tensor_tensor(out=out[:, near:WIN], in0=s[:, near:WIN], scalar=SCALE,
                                               in1=near_bias[:, h, near - FAR:NEAR], op0=ALU.mult,
                                               op1=ALU.add).then_inc(biased, 1)
                dve.wait_ge(biased, H * t + h + 1)
                nc.vector.tensor_reduce(neg_max[h % 2], out[:, lo * P:WIN], AX_X, ALU.max,
                                        negate=True).then_inc(max_ready, 1)

            def shift_window(n, u):
                lo = first_slot(n)
                dve.wait_ge(qkT_ready, 2 * n)
                wait(dve, score_ready, H * (n - 1))
                wait(dve, shifted, 2 * (n - 1))
                nc.vector.tensor_copy(kT[u][:, :, lo * P:FAR + P], kT[1 - u][:, :, (lo + 1) * P:WIN]).then_inc(shifted, 1)
                dve.wait_ge(proj_read, 3 * n)
                wait(dve, pv_done, H * (n - 1))
                nc.vector.tensor_copy(v[u][:, lo:SLOTS - 1, :], v[1 - u][:, lo + 1:SLOTS, :]).then_inc(shifted, 1)

            nc.vector.memset(eps, EPS).then_inc(eps_ready, 1)
            dve.wait_ge(consts_loaded, 64)
            last = tab[:, 2 * MAXREL:2 * MAXREL + 1]
            nc.vector.tensor_copy(rev[:, 0:P], last.broadcast_to([H, P])).then_inc(rev_ready, 1)
            nc.vector.tensor_copy(rev[:, P:3 * P], tab[:, 0:2 * MAXREL][:, ::-1]).then_inc(rev_ready, 1)
            nc.vector.memset(far_mask[:], 0.0).then_inc(rev_zero, 1)
            dve.wait_ge(rev_zero, 1)
            nc.vector.memset(far_mask[CH:P, 0:CH], MASKED).then_inc(bias_near, 1)
            norm_x(0, 0)
            read_xT(0, 0)
            read_xT(0, 1)
            norm_x(1, 1)
            wait(dve, x_lo_ready, 1)
            wait(dve, xT_stored, 16)
            read_xT(1, 0)
            read_xT(1, 1)
            dve.wait_ge(bias_loaded, 16 * (H + 1))
            far = far_value[:].rearrange("p (h o) -> p h o", o=1).broadcast_to([P, H, NEAR])
            nc.vector.tensor_tensor(near_bias[:], near_bias[:], far, ALU.subtract).then_inc(bias_near, 1)
            dve.wait_ge(bias_near, 2)
            nc.vector.memset(near_bias[0:CH, :, NEAR - CH:NEAR], MASKED).then_inc(bias_ready, 1)
            for b in range(WB):
                dve.wait_ge(w_hi_ready, b + 1)
                nc.vector.tensor_tensor(w_lo[:, :, b * P:(b + 1) * P], w_raw[b % 2][:],
                                        w_hi[:, :, b * P:(b + 1) * P].bitcast(F32), ALU.subtract).then_inc(w_lo_ready, 1)
            sum_qk(0)
            scale_qk(0)
            dve.wait_ge(bias_ready, 1)

            def step(t, u):
                lo = first_slot(t)
                more = not t_known(t) or t < TILES - 1
                for h in range(H):
                    bias_and_max(t, h, lo)
                    if h == 1 and more:
                        shift_window(t + 1, 1 - u)
                    if h == 3 and more:
                        norm_x(t + 2, u)
                    if more and h in (4, 5):
                        read_xT(t + 2, h - 4)
                    if h == 6:
                        sum_qk(t + 1)
                    if h == 7:
                        scale_qk(t + 1)
                dve.wait_ge(p_ready, H * (t + 1))
                nc.vector.reciprocal(row_inv, row_sum).then_inc(inv_ready, 1)
                dve.wait_ge(inv_ready, t + 1)
                dve.wait_ge(pv_done, H * (t + 1))
                wait(dve, out_stored, 16 * t)
                inv = row_inv.rearrange("p (h o) -> p h o", o=1).broadcast_to([P, H, HD])
                nc.vector.tensor_tensor(o_tok[:], ps_out[:].rearrange("p (h d) -> p h d", h=H), inv,
                                        ALU.mult).then_inc(out_ready, 1)

            prompt_steps(dve, step)

        @block.tensor
        def _(pe):
            def turn_x(n, u, j):
                pe.wait_ge(x_scaled, n + 1)
                if j == 0:
                    wait(pe, qkT_ready, 2 * (n - 1))
                wait(pe, xT_ready, 2 * n + j)
                for k in range(4):
                    last = nc.tensor.transpose(ps_turn[:, k * P:(k + 1) * P],
                                               x_tok[u][:, (4 * j + k) * P:(4 * j + k + 1) * P], ident[:])
                last.then_inc(x_turned, 1)

            def projection(n, u):
                for g in range(3):
                    out = ps_proj[(u + g) % 2]
                    for k in range(KT):
                        for i, (a, w) in enumerate(((x_hi, w_hi), (x_hi, w_lo), (x_lo, w_hi))):
                            if k == 0 and i == 0:
                                if g == 0:
                                    pe.wait_ge(x_hi_ready, n + 1)
                                    pe.wait_ge(x_lo_ready, n + 1)
                                wait(pe, proj_read, 3 * n + g - 1)
                                if t_known(n) and n == 0:
                                    pe.wait_ge(w_lo_ready, 4 * (g + 1))
                            mm = nc.tensor.matmul(out[:], a[u][:, k, :], w[:, k, g * AW:(g + 1) * AW],
                                                  start=(k == 0 and i == 0), stop=(k == KT - 1 and i == 2))
                            if k == KT - 1 and i == 2:
                                mm.then_inc(proj_ready, 1)
                            yield

            def turn_qk(n, g):
                if g == 0:
                    pe.wait_ge(qk_normed, n + 1)
                    pe.wait_ge(xT_ready, 2 * (DEC + 1) if t_known(n) and n == DEC else 2 * n + 4)
                wait(pe, qkT_ready, 2 * n + g)
                for c in range(PAIRS):
                    last = nc.tensor.transpose(ps_turn[:, c * P:(c + 1) * P], qk_n[:, g, c * P:(c + 1) * P], ident[:])
                last.then_inc(qk_turned, 1)

            def scores(t, u, h, lo):
                c, o = h // 2, HD * (h % 2)
                if h == 0:
                    pe.wait_ge(qkT_ready, 2 * t + 2)
                    wait(pe, shifted, 2 * t - 1)
                wait(pe, pT_ready, H * t + h - 1)
                for a, b in ((lo * P, 512), (512, WIN)):
                    if a < b:
                        mm = nc.tensor.matmul(ps_score[h % 2][:, a:b], qT[o:o + HD, c, :], kT[u][o:o + HD, c, a:b],
                                              start=True, stop=True)
                mm.then_inc(score_ready, 1)

            def turn_probs(t, h, lo):
                pe.wait_ge(p_ready, H * t + h + 1)
                for s in range(lo, SLOTS):
                    last = nc.tensor.transpose(ps_score[h % 2][:, s * P:(s + 1) * P], probs[h % 2][:, s * P:(s + 1) * P],
                                               ident[:])
                last.then_inc(p_turned, 1)

            def weigh_values(t, u, h, lo):
                pe.wait_ge(pT_ready, H * t + h + 1)
                if h == 0:
                    wait(pe, out_ready, t)
                    wait(pe, shifted, 2 * t)
                    pe.wait_ge(proj_read, 3 * (t + 1))
                for s in range(lo, SLOTS):
                    mm = nc.tensor.matmul(ps_out[:, h * HD:(h + 1) * HD], pT[h % 2][:, s * P:(s + 1) * P],
                                          v[u][:, s, h * HD:(h + 1) * HD], start=(s == lo), stop=(s == SLOTS - 1))
                mm.then_inc(pv_done, 1)

            pe.wait_ge(ident_ready, 1)
            for n in (0, 1):
                turn_x(n, n, 0)
                turn_x(n, n, 1)
            for _ in projection(0, 0):
                pass
            turn_qk(0, 0)
            turn_qk(0, 1)

            def step(t, u):
                lo = first_slot(t)
                more = not t_known(t) or t < TILES - 1
                ahead = projection(t + 1, 1 - u)

                def fill(n):
                    for _ in range(n):
                        next(ahead, None)

                for h in range(H):
                    scores(t, u, h, lo)
                    fill(3)
                    if h >= 1:
                        turn_probs(t, h - 1, lo)
                    fill(3)
                    if h >= 1:
                        weigh_values(t, u, h - 1, lo)
                    fill(3)
                    if more and h in (4, 5):
                        turn_x(t + 2, u, h - 4)
                turn_qk(t + 1, 0)
                turn_probs(t, H - 1, lo)
                turn_qk(t + 1, 1)
                weigh_values(t, u, H - 1, lo)

            prompt_steps(pe, step)


def cached_attention_phase(nc, io):
    with ExitStack() as ctx:
        def sb(name, shape, dt=F32):
            return ctx.enter_context(nc.sbuf_tensor(name, shape, dt))

        held = []

        def sem(name):
            held.append(ctx.enter_context(nc.semaphore(name)))
            return held[-1]

        DK = PAST // P
        DW = PAST + P
        BW = DW + P - SL
        G2 = 2 * SL
        k_c = [sb(f"c_k{i}", [P, DK, AW]) for i in range(2)]
        v_c = [sb(f"c_v{i}", [P, DK, AW]) for i in range(2)]
        kcT = [sb(f"c_kT{i}", [P, DK, PAIRS, P]) for i in range(2)]
        q_blocks = [sb(f"c_q{i}", [P, PAIRS, 2, SL]) for i in range(2)]
        qT, knT, v_n = sb("c_qT", [P, PAIRS, P]), sb("c_knT", [P, PAIRS, P]), sb("c_vn", [P, AW])
        bias = sb("c_bias", [P, BW])
        probs = [sb(f"c_probs{i}", [P, DW]) for i in range(2)]
        pT = [sb(f"c_pT{i}", [P, DK + 1, P]) for i in range(2)]
        oT, o_tok = sb("c_oT", [P, PAIRS, P]), sb("c_o", [P, AW])
        ident = sb("c_ident", [P, P])
        small = sb("c_small", [P, 8])
        ps_k = ctx.enter_context(nc.psum_tensor("c_ps_k", [P, DK * AW], F32))
        ps_s = [ctx.enter_context(nc.psum_tensor(f"c_ps_s{i}", [P, 512], F32)) for i in range(2)]
        ps_p = [ctx.enter_context(nc.psum_tensor(f"c_ps_p{i}", [P, 512], F32)) for i in range(2)]
        ps_o = [ctx.enter_context(nc.psum_tensor(f"c_ps_o{i}", [P, 512], F32)) for i in range(2)]

        new_loaded, bias_loaded = sem("c_new_loaded"), sem("c_bias_loaded")
        kv_loaded = [sem(f"c_kv_loaded{i}") for i in range(2)]
        ident_zero, ident_ready, bias_masked, q_zero = sem("c_ident_zero"), sem("c_ident_ready"), sem("c_bias_masked"), sem("c_q_zero")
        q_ready, k_turned, kcT_ready = sem("c_q_ready"), sem("c_k_turned"), sem("c_kcT_ready")
        score_ready, biased, max_ready, p_exp = sem("c_score_ready"), sem("c_biased"), sem("c_max_ready"), sem("c_p_exp")
        inv_ready, p_ready, p_turned, pT_ready = sem("c_inv_ready"), sem("c_p_ready"), sem("c_p_turned"), sem("c_pT_ready")
        pv_done, oT_ready, o_turned, o_ready, o_stored = sem("c_pv_done"), sem("c_oT_ready"), sem("c_o_turned"), sem("c_o_ready"), sem("c_o_stored")

        ctx.callback(clear_semaphores, nc, held)
        block = ctx.enter_context(nc.Block())

        def streams(eng, first, second):
            for half in (first, second):
                half(0, 0)
                half(1, 1)
            with eng.Fori(1, NS // 2) as i:
                for half in (first, second):
                    half(i * 2, 0)
                    half(i * 2 + 1, 1)

        @block.sync
        def _(sp):
            sp.dma_start(qT[:], io["qT_new"]).then_inc(new_loaded, 16)
            sp.dma_start(knT[:], io["kT_new"]).then_inc(new_loaded, 16)
            sp.dma_start(v_n[:], io["v_new"]).then_inc(new_loaded, 16)
            rev = io["rev_table"].tensor
            sp.wait_ge(bias_masked, 1)
            for h in range(H):
                rows = slice(h * SL, (h + 1) * SL)
                sp.dma_start(bias[rows, 0:P], bass.AP(rev, h * P * 3 * P, [[0, SL], [1, P]])).then_inc(bias_loaded, 16)
                sp.dma_start(bias[rows, P:PAST], bass.AP(rev, h * P * 3 * P + P - 1, [[3 * P - 1, SL], [1, P]])).then_inc(bias_loaded, 16)
                sp.dma_start(bias[rows, DW - SL:DW], bass.AP(rev, h * P * 3 * P + PAST - 1, [[3 * P - 1, SL], [1, SL]])).then_inc(bias_loaded, 16)

            def load(b, u):
                wait(sp, pv_done, b - u)
                for s in range(DK):
                    for buf, cache in ((k_c, "cache_attn_k"), (v_c, "cache_attn_v")):
                        src = io[cache][0, bass.ds(b, 1), :, s * P:(s + 1) * P, :].rearrange("o h s d -> s (o h) d")
                        sp.dma_start(buf[u][:, s, :].rearrange("p (h d) -> p h d", h=H), src).then_inc(kv_loaded[u], 16)

            streams(sp, load, lambda b, u: None)
            sp.wait_ge(o_ready, 1)
            sp.dma_start(io["o_att"][DEC * P:(DEC + 1) * P, :], o_tok[:]).then_inc(o_stored, 16)
            sp.wait_ge(o_stored, 16)

        @block.gpsimd
        def _(pool):
            nc.gpsimd.memset(bias[:], MASKED).then_inc(bias_masked, 1)
            nc.gpsimd.memset(q_blocks[0][:], 0.0).then_inc(q_zero, 1)
            nc.gpsimd.memset(q_blocks[1][:], 0.0).then_inc(q_zero, 1)
            nc.gpsimd.memset(ident[:], 0.0).then_inc(ident_zero, 1)
            pool.wait_ge(ident_zero, 1)
            nc.gpsimd.affine_select(out=ident[:], in_=ident[:], compare_op=ALU.not_equal, fill=1.0, base=0,
                                    pattern=[[-1, P]], channel_multiplier=1).then_inc(ident_ready, 1)

        @block.scalar
        def _(act):
            act.preload_act_table_set(ACT_TABLES)

            def keys_and_exp(b, u):
                act.wait_ge(k_turned, b + 1)
                wait(act, score_ready, b - u)
                nc.scalar.activation(kcT[u][:], ps_k[:].rearrange("p (s c n) -> p s c n", s=DK, c=PAIRS),
                                     ACT.Copy).then_inc(kcT_ready, 1)
                act.wait_ge(max_ready, b + 1)
                nc.scalar.activation(probs[u][:], probs[u][:], ACT.Exp, bias=small[:, u:u + 1],
                                     accum_out=small[:, 2 + u:3 + u]).then_inc(p_exp, 1)

            def read_pT(b, u):
                act.wait_ge(p_turned, b + 1)
                wait(act, pv_done, b - u)
                nc.scalar.activation(pT[u][:], ps_p[u][:, 0:DW].rearrange("p (s n) -> p s n", n=P),
                                     ACT.Copy).then_inc(pT_ready, 1)

            streams(act, keys_and_exp, read_pT)
            act.wait_ge(o_turned, 1)
            nc.scalar.activation(o_tok[:], ps_p[0][:], ACT.Copy).then_inc(o_ready, 1)

        @block.vector
        def _(dve):
            dve.wait_ge(new_loaded, 48)
            dve.wait_ge(q_zero, 2)
            dve.wait_ge(bias_loaded, 16 * 3 * H)

            def queries_and_max(b, u):
                wait(dve, score_ready, b - u)
                for i in range(2):
                    nc.vector.tensor_copy(q_blocks[u][i * HD:(i + 1) * HD, :, i, :],
                                          qT[i * HD:(i + 1) * HD, :, bass.ds(b * SL, SL)]).then_inc(q_ready, 1)
                dve.wait_ge(score_ready, b + 1)
                wait(dve, p_turned, b - u)
                nc.vector.scalar_tensor_tensor(out=probs[u][:, 0:PAST], in0=ps_s[u][:, 0:PAST], scalar=SCALE,
                                               in1=bias[:, 0:PAST], op0=ALU.mult, op1=ALU.add)
                nc.vector.scalar_tensor_tensor(out=probs[u][:, PAST:DW], in0=ps_s[u][:, PAST:DW], scalar=SCALE,
                                               in1=bias[:, bass.ds(DW - SL - b * SL, P)], op0=ALU.mult,
                                               op1=ALU.add).then_inc(biased, 1)
                dve.wait_ge(biased, b + 1)
                nc.vector.tensor_reduce(small[:, u:u + 1], probs[u][:], AX_X, ALU.max, negate=True).then_inc(max_ready, 1)

            def normalise_and_keep(b, u):
                dve.wait_ge(p_exp, b + 1)
                nc.vector.reciprocal(small[:, 4 + u:5 + u], small[:, 2 + u:3 + u]).then_inc(inv_ready, 1)
                dve.wait_ge(inv_ready, b + 1)
                nc.vector.tensor_scalar(probs[u][:], probs[u][:], small[:, 4 + u:5 + u], None, ALU.mult).then_inc(p_ready, 1)
                dve.wait_ge(pv_done, b + 1)
                for i in range(2):
                    half = slice(i * HD, (i + 1) * HD)
                    src = ps_o[u][half, 0:P].rearrange("p (c i q) -> p c i q", c=PAIRS, i=2)[:, :, i, :]
                    nc.vector.tensor_copy(oT[half, :, bass.ds(b * SL, SL)], src).then_inc(oT_ready, 1)

            streams(dve, queries_and_max, normalise_and_keep)

        @block.tensor
        def _(pe):
            pe.wait_ge(ident_ready, 1)
            pe.wait_ge(new_loaded, 48)

            def turn_and_score(b, u):
                pe.wait_ge(kv_loaded[u], 32 * b + (64 - 32 * u))
                wait(pe, kcT_ready, b)
                for s in range(DK):
                    for c in range(PAIRS):
                        last = nc.tensor.transpose(ps_k[:, (s * PAIRS + c) * P:(s * PAIRS + c + 1) * P],
                                                   k_c[u][:, s, c * P:(c + 1) * P], ident[:])
                last.then_inc(k_turned, 1)
                pe.wait_ge(q_ready, 2 * b + 2)
                wait(pe, biased, b - u)
                pe.wait_ge(kcT_ready, b + 1)
                for c in range(PAIRS):
                    lhs = q_blocks[u][:, c, :, :].rearrange("p i q -> p (i q)")
                    nc.tensor.matmul(ps_s[u][c * G2:(c + 1) * G2, 0:PAST], lhs, kcT[u][:, :, c, :], start=True, stop=True)
                    last = nc.tensor.matmul(ps_s[u][c * G2:(c + 1) * G2, PAST:DW], lhs, knT[:, c, :], start=True, stop=True)
                last.then_inc(score_ready, 1)

            def turn_and_weigh(b, u):
                wait(pe, pT_ready, b - u)
                pe.wait_ge(p_ready, b + 1)
                for s in range(DK + 1):
                    last = nc.tensor.transpose(ps_p[u][:, s * P:(s + 1) * P], probs[u][:, s * P:(s + 1) * P], ident[:])
                last.then_inc(p_turned, 1)
                wait(pe, oT_ready, 2 * (b - u))
                pe.wait_ge(pT_ready, b + 1)
                for c in range(PAIRS):
                    cols = slice(c * P, (c + 1) * P)
                    for s in range(DK + 1):
                        vs = v_c[u][:, s, cols] if s < DK else v_n[:, cols]
                        last = nc.tensor.matmul(ps_o[u][:, c * G2:(c + 1) * G2], vs, pT[u][:, s, c * G2:(c + 1) * G2],
                                                start=(s == 0), stop=(s == DK))
                last.then_inc(pv_done, 1)

            streams(pe, turn_and_score, turn_and_weigh)
            pe.wait_ge(oT_ready, 2 * NS)
            pe.wait_ge(pT_ready, NS)
            for c in range(PAIRS):
                last = nc.tensor.transpose(ps_p[0][:, c * P:(c + 1) * P], oT[:, c, :], ident[:])
            last.then_inc(o_turned, 1)


def shape_constants():
    import numpy as np

    p = np.arange(P)[:, None]
    c = np.arange(P)[None, :]
    c64 = np.arange(CH)[None, :]
    out = {"ident": p == c, "ident_c": p % CH == c64, "head_ones": p // HD == c // HD, "head_of": p // HD == np.arange(2)[None, :],
           "stream_of": p // SL == np.arange(NS)[None, :]}
    for mode, size in (("p", CH), ("s", SL)):
        same = p // size == c // size
        out[f"lower_{mode}"] = same & (p > c)
        out[f"upper_{mode}"] = np.concatenate([same & (p < c), same & (p <= c)], 1)
        levels = []
        w = 2
        while w <= size:
            i = p % CH
            levels.append((i // w == c64 // w) & (i % w < w // 2) & (c64 % w >= w // 2))
            w *= 2
        out[f"levels_{mode}"] = np.concatenate(levels, 1)
        out[f"run_{mode}"] = np.broadcast_to(np.arange(PAIRS * P)[None, :] % size != 0, (P, PAIRS * P))
    return {k: np.ascontiguousarray(v, np.float32) for k, v in out.items()}


CONST_AT, CONST_W = {}, 0
for _name, _v in shape_constants().items():
    CONST_AT[_name] = (CONST_W, _v.shape[1])
    CONST_W += _v.shape[1]


SHIFT_TILES = SHIFT_COLS // P
GT = 4


def rwkv_projection_phase(nc, io):
    with ExitStack() as ctx:
        def sb(name, shape, dt=F32):
            return ctx.enter_context(nc.sbuf_tensor("j_" + name, shape, dt))

        held = []

        def sem(name):
            held.append(ctx.enter_context(nc.semaphore("j_" + name)))
            return held[-1]

        w_hi, w_lo = sb("w_hi", [P, KT, SHIFT_COLS], F32R), sb("w_lo", [P, KT, SHIFT_COLS], F32R)
        w_raw = [sb(f"w_raw{i}", [P, KT, P]) for i in range(2)]
        xT = sb("xT", [P, GT, KT, P])
        x_hi, x_lo = sb("x_hi", [P, KT, GT, P], F32R), sb("x_lo", [P, KT, GT, P], F32R)
        out = [sb(f"out{i}", [P, GT * P]) for i in range(2)]
        ps = [ctx.enter_context(nc.psum_tensor(f"j_ps{i}", [P, GT * P], F32)) for i in range(2)]

        w_loaded = [sem(f"w_loaded{i}") for i in range(2)]
        w_hi_ready, w_lo_ready = sem("w_hi_ready"), sem("w_lo_ready")
        x_loaded, x_hi_ready, x_lo_ready = sem("x_loaded"), sem("x_hi_ready"), sem("x_lo_ready")
        projected, copied, stored = ([sem(f"{n}{i}") for i in range(2)] for n in ("projected", "copied", "stored"))

        w_in = io["w_in"][0].rearrange("(k p) n -> p k n", p=P)
        COL0 = 4 * AW
        GROUPS = TILES // GT
        OF = (SHIFT_TILES - SHIFT_TILES // 2, SHIFT_TILES // 2)
        ctx.callback(clear_semaphores, nc, held)
        block = ctx.enter_context(nc.Block())

        def groups(eng, step):
            step(0, GT)
            with eng.Fori(1, GROUPS) as g:
                step(g, GT)
            step(GROUPS, 1)

        def blocks(g):
            for c in range(SHIFT_TILES):
                yield c, c % 2, g * OF[c % 2] + c // 2

        @block.sync
        def _(sp):
            def load_w(b):
                sp.dma_start(w_raw[b % 2][:], w_in[:, :, COL0 + b * P:COL0 + (b + 1) * P]).then_inc(w_loaded[b % 2], 16)

            def load_x(g, n):
                src = io["xT"][bass.ds(g * GT, n)].rearrange("a p k n -> p a (k n)")
                sp.dma_start(xT[:, 0:n].rearrange("p a k n -> p a (k n)"), src).then_inc(x_loaded, 16)

            load_w(0)
            load_x(0, GT)
            load_w(1)

            def step(g, n):
                if not (t_known(g) and g == GROUPS):
                    sp.wait_ge(x_lo_ready, g + 1)
                    load_x(g + 1, GT) if not (t_known(g) and g == GROUPS - 1) else load_x(GROUPS, 1)
                for c, j, i in blocks(g):
                    if t_known(g) and g == 0 and c + 2 < SHIFT_TILES:
                        sp.wait_ge(w_lo_ready, c + 1)
                        load_w(c + 2)
                    sp.wait_ge(copied[j], i + 1)
                    sp.dma_start(io["proj_T"][c, :, bass.ds(1 + g * (GT * P), n * P)], out[j][:, 0:n * P]).then_inc(stored[j], 16)

            step(0, GT)
            with sp.Fori(1, GROUPS - 1) as g:
                step(g, GT)
            step(GROUPS - 1, GT)
            step(GROUPS, 1)
            for j in range(2):
                sp.wait_ge(stored[j], 16 * OF[j] * (GROUPS + 1))

        @block.scalar
        def _(act):
            def split(g, n):
                act.wait_ge(x_loaded, 16 * (g + 1))
                wait(act, projected[0], OF[0] * g)
                wait(act, projected[1], OF[1] * g)
                nc.scalar.activation(x_hi[:, :, 0:n, :].rearrange("p k a n -> p a k n"), xT[:, 0:n], ACT.Copy).then_inc(x_hi_ready, 1)

            act.wait_ge(w_loaded[0], 16)
            nc.scalar.activation(w_hi[:, :, 0:P], w_raw[0][:], ACT.Copy).then_inc(w_hi_ready, 1)
            split(0, GT)
            for b in range(1, SHIFT_TILES):
                act.wait_ge(w_loaded[b % 2], 16 * (b // 2 + 1))
                nc.scalar.activation(w_hi[:, :, b * P:(b + 1) * P], w_raw[b % 2][:], ACT.Copy).then_inc(w_hi_ready, 1)
            with act.Fori(1, GROUPS) as g:
                split(g, GT)
            split(GROUPS, 1)

        @block.vector
        def _(dve):
            def split_w(b):
                dve.wait_ge(w_hi_ready, b + 1)
                nc.vector.tensor_tensor(w_lo[:, :, b * P:(b + 1) * P], w_raw[b % 2][:],
                                        w_hi[:, :, b * P:(b + 1) * P].bitcast(F32), ALU.subtract).then_inc(w_lo_ready, 1)

            def split(g, n):
                dve.wait_ge(x_hi_ready, g + 1)
                nc.vector.tensor_tensor(x_lo[:, :, 0:n, :].rearrange("p k a n -> p a k n"), xT[:, 0:n],
                                        x_hi[:, :, 0:n, :].rearrange("p k a n -> p a k n").bitcast(F32),
                                        ALU.subtract).then_inc(x_lo_ready, 1)

            split_w(0)

            def step(g, n):
                split(g, n)
                for c, j, i in blocks(g):
                    if t_known(g) and g == 0 and c + 1 < SHIFT_TILES:
                        split_w(c + 1)
                    dve.wait_ge(projected[j], i + 1)
                    wait(dve, stored[j], 16 * i)
                    nc.vector.tensor_copy(out[j][:, 0:n * P], ps[j][:, 0:n * P]).then_inc(copied[j], 1)

            groups(dve, step)

        @block.tensor
        def _(pe):
            def step(g, n):
                pe.wait_ge(x_hi_ready, g + 1)
                pe.wait_ge(x_lo_ready, g + 1)
                for c, j, i in blocks(g):
                    wait(pe, copied[j], i)
                    if t_known(g) and g == 0:
                        pe.wait_ge(w_lo_ready, c + 1)
                    cols = slice(c * P, (c + 1) * P)
                    for k in range(KT):
                        for m, (w, x) in enumerate(((w_hi, x_hi), (w_lo, x_hi), (w_hi, x_lo))):
                            mm = nc.tensor.matmul(ps[j][:, 0:n * P], w[:, k, cols], x[:, k, 0:n, :].rearrange("p a n -> p (a n)"),
                                                  start=(k == 0 and m == 0), stop=(k == KT - 1 and m == 2))
                    mm.then_inc(projected[j], 1)

            groups(pe, step)


def merged(first, second):
    runs = [first, second]
    at = [next(r, None) for r in runs]
    while at != [None, None]:
        i = 1 if at[0] is None or (at[1] is not None and at[1] < at[0]) else 0
        at[i] = next(runs[i], None)


def rwkv_phase(nc, io):
    with ExitStack() as ctx:
        def sb(name, shape, dt=F32):
            return ctx.enter_context(nc.sbuf_tensor("r_" + name, shape, dt))

        held = []

        def sem(name):
            held.append(ctx.enter_context(nc.semaphore("r_" + name)))
            return held[-1]

        def sb2(name, shape):
            return [sb(f"{name}{i}", shape) for i in range(2)]

        def sems2(name):
            return [sem(f"{name}{i}") for i in range(2)]

        CT = SHIFT_TILES
        PW = PAIRS * P
        KAPPA = 0.6065306597126334
        GN_EPS = 64e-5
        LN_UP = 65536.0
        NCH = P // CH
        consts = sb("consts", [P, CONST_W])
        per_ch = sb("per_ch", [P, CT + 6 * PAIRS])
        lora_w = sb("lora_w", [P, AW])
        gn = sb("gn", [P, 2, AW])
        cur = sb2("cur", [P, CT, NS * (SL + 1)])
        xs = sb("xs", [P, CT, P])
        th = sb("tanh", [HD, P])
        sig, acc, inv_g, a_gate = (sb(n, [P, PW]) for n in ("sig", "acc", "inv_g", "a_gate"))
        g_run = sb("g_run", [P, PAIRS, NS * (SL + 1)])
        kk, kk_sq, kk_n, fac, kmod, bmul, rk = (sb(n, [P, PW]) for n in ("kk", "kk_sq", "kk_n", "fac", "kmod", "bmul", "rk"))
        bt, kt = sb("bt", [P, PW]), sb("kt", [P, PW])
        ar = sb2("ar", [P, PAIRS, 2, P])
        g_last = sb2("g_last", [P, PAIRS, NS])
        v_tok, k_tok, b_tok = sb2("v_tok", [P, AW]), sb2("k_tok", [P, AW]), sb2("b_tok", [P, AW])
        a_mat = sb2("a_mat", [P, 2, PAIRS, P])
        ak_T = sb2("ak_T", [P, 2, PAIRS, 2, P])
        rb_T = sb2("rb_T", [P, 2, PAIRS, P])
        bonus = sb2("bonus", [P, H])
        x_mat = sb("x_mat", [P, 2, PAIRS, P])
        y_mat, q_mat = sb("y_mat", [P, 2, PAIRS, CH]), sb("q_mat", [P, 2, PAIRS, CH])
        rhs, u_tok = sb("rhs", [P, AW]), sb("u_tok", [P, AW])
        state = sb("state", [P, PAIRS, P])
        states = sb("states", [P, PAIRS, NS, HD])
        st_nat = sb("st_nat", [HD, NS, AW])
        st_shift, shift_T = sb("st_shift", [NS, SHIFT_COLS]), sb("shift_T", [P, CT, NS])
        y_tok, y_sq = sb("y_tok", [P, AW]), sb("y_sq", [P, AW])
        small = sb("small", [P, 40])
        y_sum, y_mean, y_var, y_rstd = (small[:, 8 * i:8 * i + 8] for i in range(4))
        gn_eps, ln_back = small[:, 32:33], small[:, 33:34]
        spread_s, spread_u = sb2("spread", [P, NS, HD]), sb2("spread_u", [P, NS, HD])
        dec_cols = sb("dec_cols", [P, CT, P])
        state_back = sb("state_back", [P, PAIRS, P])
        from_state = [sb(f"from_state{i}", [P, AW]) for i in range(2)]

        def bank(name):
            return ctx.enter_context(nc.psum_tensor("r_ps_" + name, [P, 512], F32))

        ps_job = [bank("job0"), bank("job1")]
        ps_inv = [bank("inv0"), bank("inv1")]
        ps_rhs, ps_u, ps_y, ps_s = bank("rhs"), bank("u"), bank("y"), bank("s")
        ps_turn = [ps_rhs, ps_u]

        def const(name, mode=None):
            at, n = CONST_AT[name if mode is None else f"{name}_{mode}"]
            return consts[:, at:at + n]

        ident = const("ident")

        def chan(i):
            return per_ch[:, CT + i * PAIRS:CT + (i + 1) * PAIRS]

        DECAY, ICLR, REMOVE, KICLR, BONUS, KICLR_REST = range(6)

        def spread(ap, n):
            return ap.rearrange("p (k o) -> p k o", o=1).broadcast_to([P, ap.shape[1], n])

        def c4(ap):
            return ap.rearrange("p (c n) -> p c n", c=PAIRS)

        def heads(ap):
            return ap.rearrange("p (h d) -> p h d", h=H)

        def head_cols(g, c):
            return slice((2 * c + g) * HD, (2 * c + g + 1) * HD)

        def pair_cols(c):
            return slice(c * P, (c + 1) * P)

        def half(i):
            return slice(i * HD, (i + 1) * HD)

        params_loaded, cur_loaded, states_loaded = sem("params_loaded"), sems2("cur_loaded"), sem("states_loaded")
        set_up, states_turned, states_read = sem("set_up"), sem("states_turned"), sem("states_read")
        job_written, job_read = sems2("job_written"), sems2("job_read")
        ready = {n: sem(n + "_ready") for n in (
            "delta", "lora_in", "xs", "tanh", "acc", "g_run", "inv_g", "g_last", "kk", "kk_sq", "kk_log", "rnorm", "kk_n",
            "ahat", "rhat", "fac", "kmod", "bmul", "bt", "kt", "rk", "rkr",
            "y_sum", "y_mean", "y_centred", "y_sq", "y_var", "y_log", "y_rstd", "y_scaled", "y_gained", "y_based",
            "v_bonus", "out", "ps_y")}
        turn_written = sems2("turn_written")
        inv_written, q_ready, y_ready, x_ready = sems2("inv_written"), sems2("q_ready"), sems2("y_ready"), sems2("x_ready")
        rhs_written, rhs_ready, u_written, u_ready = sem("rhs_written"), sem("rhs_ready"), sem("u_written"), sem("u_ready")
        s_written, s_added, state_ready, o_stored = sem("s_written"), sem("s_added"), sem("state_ready"), sem("o_stored")
        dec_written, dec_masked, dec_summed = sems2("dec_written"), sems2("dec_masked"), sems2("dec_summed")
        dec_spread_v, dec_spread_u, dec_added, dec_state = sems2("dec_spread_v"), sems2("dec_spread_u"), sems2("dec_added"), sems2("dec_state")
        y_raw_ready, turned_back, nat_ready, stored = sem("y_raw_ready"), sem("turned_back"), sem("nat_ready"), sem("stored")
        state_turned, state_out, dec_copied = sem("state_turned"), sem("state_out"), sem("dec_copied")

        JOBS = ["decay", "iclr", "kk_sum", "v_tok", "k_tok", "b_tok", "A0", "A1", "AK00", "AK10", "AK01", "AK11",
                "RB0", "RB1", "bonus"]
        JOBS_OF = (len(JOBS) - len(JOBS) // 2, len(JOBS) // 2)
        LEVELS = {"p": 6, "s": 4}
        LP = LEVELS["p"]

        def job_count(t, name):
            j = JOBS.index(name)
            return j % 2, JOBS_OF[j % 2] * t + j // 2

        def free_bank(t, name):
            b, n = job_count(t, name)
            wait(nc.tensor, job_read[b], n)
            return ps_job[b], job_written[b]

        def written(eng, t, name):
            b, n = job_count(t, name)
            eng.wait_ge(job_written[b], n + 1)
            return ps_job[b], job_read[b]

        def was_written(eng, t, name):
            b, n = job_count(t, name)
            wait(eng, job_written[b], n + 1 - JOBS_OF[b])

        def was_read(eng, t, name):
            b, n = job_count(t, name)
            eng.wait_ge(job_read[b], n + 1)

        def need(eng, t, *names):
            for n in names:
                eng.wait_ge(ready[n], t + 1)

        def past(eng, t, *names):
            for n in names:
                wait(eng, ready[n], t)

        def tiles(eng, front, back):
            def both(t, u, mode_next="p"):
                merged(front(t + 1, 1 - u, mode_next) if mode_next else iter(()), back(t, u, "p" if mode_next else "s"))

            for _ in front(0, 0, "p"):
                pass
            both(0, 0)
            both(1, 1)
            with eng.Fori(1, (TILES - 2) // 2) as i:
                both(i * 2, 0)
                both(i * 2 + 1, 1)
            both(TILES - 2, 0)
            both(TILES - 1, 1, "s")
            both(DEC, 0, None)

        def runs(ap, mode):
            n, size = (NCH, CH) if mode == "p" else (NS, SL)
            return ap[:, :, 0:n * (size + 1)].rearrange("p c (n l) -> p c n l", n=n)

        def by_run(ap, mode):
            return ap.rearrange("p c (n l) -> p c n l", n=NCH if mode == "p" else NS)

        def cur_views(u, mode):
            if mode == "p":
                return cur[u][:, :, 1:P + 1], cur[u][:, :, 0:P]
            v = runs(cur[u], mode)
            return v[:, :, :, 1:], v[:, :, :, 0:SL]

        ctx.callback(clear_semaphores, nc, held)
        block = ctx.enter_context(nc.Block())

        @block.sync
        def _(sp):
            def load_cur(t, u):
                sp.dma_start(cur[u][:, :, 0:P + 1], io["proj_T"][:, :, bass.ds(t * P, P + 1)].rearrange("c p n -> p c n")).then_inc(cur_loaded[u], 16)

            sp.dma_start(cur[0][:, :, 1:P + 1], io["proj_T"][:, :, 1:P + 1].rearrange("c p n -> p c n")).then_inc(cur_loaded[0], 16)
            sp.dma_start(consts[:], io["shape_consts"]).then_inc(params_loaded, 16)

            def column(dst, src):
                sp.dma_start(dst, src.rearrange("(c p) -> p c", p=P), allow_slow_non_contiguous=True).then_inc(params_loaded, 16)

            column(per_ch[:, 0:CT], io["shift_mix"][0])
            column(chan(DECAY), io["decay_base"][0])
            column(chan(ICLR), io["iclr_base"][0])
            column(chan(REMOVE), io["key_remove_scale"][0])
            column(chan(KICLR), io["key_iclr_scale"][0])
            column(chan(BONUS), io["bonus_scale"][0].rearrange("h d -> (h d)"))
            sp.dma_start(lora_w[0:HD, :], io["decay_lora_up"][0]).then_inc(params_loaded, 16)
            sp.dma_start(lora_w[HD:P, :], io["iclr_lora_up"][0]).then_inc(params_loaded, 16)
            sp.dma_start(gn[:, 0, :], io["out_norm_gain"][0].partition_broadcast(P)).then_inc(params_loaded, 16)
            sp.dma_start(gn[:, 1, :], io["out_norm_bias"][0].partition_broadcast(P)).then_inc(params_loaded, 16)
            load_cur(1, 1)
            sp.dma_start(st_shift[:], io["state_rwkv_shift"][0].rearrange("b o n -> (b o) n")).then_inc(states_loaded, 16)
            sp.dma_start(st_nat[:].rearrange("v b (h k) -> v (b h) k", h=H),
                         io["state_rwkv_wkv"][0].rearrange("b h v k -> v (b h) k")).then_inc(states_loaded, 16)

            def load_front(t, u, mode):
                yield 8
                if t_known(t) and t >= TILES - 1:
                    return
                need(sp, t, "xs")
                if t_known(t) and t == DEC - 2:
                    sp.dma_start(dec_cols[:], io["proj_T"][:, :, 1 + DEC * P:1 + (DEC + 1) * P].rearrange("c p n -> p c n")).then_inc(cur_loaded[0], 16)
                else:
                    load_cur(t + 2, u)

            def store_back(t, u, mode):
                yield 60
                need(sp, t, "out")
                sp.dma_start(io["o_rwkv"][bass.ds(t * P, P), :], y_tok[:]).then_inc(o_stored, 16)

            for _ in load_front(0, 0, "p"):
                pass
            with sp.Fori(0, (TILES - 2) // 2 - 1) as i:
                merged(load_front(i * 2 + 1, 1, "p"), store_back(i * 2, 0, "p"))
                merged(load_front(i * 2 + 2, 0, "p"), store_back(i * 2 + 1, 1, "p"))
            for t in range(TILES - 4, TILES):
                merged(load_front(t + 1, 1 - t % 2, "p"), store_back(t, t % 2, "p"))
            sp.dma_start(io["shift_prompt_new"].rearrange("a b c (k p) -> p (a b c k)", p=P), cur[1][:, :, P],
                         allow_slow_non_contiguous=True).then_inc(stored, 16)
            for b in range(NS):
                sp.dma_start(io["shift_sample_new"][0, b].rearrange("o (k p) -> p (o k)", p=P), dec_cols[:, :, (b + 1) * SL - 1],
                             allow_slow_non_contiguous=True).then_inc(stored, 16)
            sp.wait_ge(state_out, 1)
            for g in range(2):
                sp.dma_start(io["wkv_prompt_new"][0, 0].rearrange("(c g) v k -> g v c k", g=2)[g],
                             state_back[half(g), :, half(g)]).then_inc(stored, 16)
            for _ in store_back(DEC, 0, "s"):
                pass
            sp.wait_ge(nat_ready, NS)
            sp.dma_start(io["wkv_sample_new"][0].rearrange("b h v k -> v (b h) k"),
                         st_nat[:].rearrange("v b (h k) -> v (b h) k", h=H)).then_inc(stored, 16)
            sp.wait_ge(stored, 16 * (NS + 4))
            sp.wait_ge(o_stored, 16 * (TILES + 1))

        @block.gpsimd
        def _(pool):
            nc.gpsimd.memset(cur[0][:, :, 0:1], 0.0).then_inc(set_up, 1)
            nc.gpsimd.memset(g_run[:], 1.0).then_inc(set_up, 1)
            nc.gpsimd.memset(state[:], 0.0).then_inc(set_up, 1)
            nc.gpsimd.memset(x_mat[:], 0.0).then_inc(set_up, 1)
            nc.gpsimd.memset(gn_eps, GN_EPS).then_inc(set_up, 1)
            nc.gpsimd.memset(ln_back, 8 * 0.6931471805599453).then_inc(set_up, 1)
            pool.wait_ge(params_loaded, 16 * 11)
            nc.gpsimd.tensor_scalar(chan(KICLR_REST), chan(KICLR), -1.0, 1.0, ALU.mult, ALU.add).then_inc(set_up, 1)
            pool.wait_ge(set_up, 7)

            def front(t, u, mode):
                yield 0
                pool.wait_ge(cur_loaded[u], 8 * t + 16 - 8 * u)
                now, before = cur_views(u, mode)
                if mode == "s":
                    pool.wait_ge(dec_copied, 2)
                    pool.wait_ge(states_read, 1)
                past(pool, t, "tanh", "xs")
                was_written(pool, t, "iclr")
                was_written(pool, t, "v_tok")
                past(pool, t, "kk", "kmod", "rhat", "rk")
                nc.gpsimd.tensor_tensor(by_run(xs[:], mode) if mode == "s" else xs[:], before, now, ALU.subtract).then_inc(ready["delta"], 1)
                yield 10
                need(pool, t, "xs")
                past(pool, t, "kk_sq", "kk_n")
                nc.gpsimd.tensor_tensor(c4(kk[:]), xs[:, 4:8], spread(chan(REMOVE), P), ALU.mult).then_inc(ready["kk"], 1)
                yield 12
                past(pool, t, "rkr")
                was_written(pool, t, "bonus")
                nc.gpsimd.tensor_tensor(c4(rk[:]), xs[:, 0:4], spread(chan(BONUS), P), ALU.mult).then_inc(ready["rk"], 1)
                yield 14
                need(pool, t, "fac")
                past(pool, t, "kt", "rkr")
                nc.gpsimd.tensor_tensor(c4(kmod[:]), xs[:, 4:8], c4(fac[:]), ALU.mult).then_inc(ready["kmod"], 1)
                yield 17
                need(pool, t, "g_run")
                wait(pool, ready["ps_y"], t - 1)
                nc.gpsimd.tensor_tensor(by_run(ar[u][:, :, 1, :], mode), by_run(xs[:, 0:4], mode), runs(g_run, mode)[:, :, :, 1:],
                                        ALU.mult).then_inc(ready["rhat"], 1)
                yield 19
                need(pool, t, "rk", "kmod")
                nc.gpsimd.tensor_tensor(rk[:], rk[:], kmod[:], ALU.mult).then_inc(ready["rkr"], 1)

            def back(t, u, mode):
                if mode == "s":
                    yield 47
                    for g, c in [(g, c) for c in range(PAIRS) for g in range(2)]:
                        n = c
                        pool.wait_ge(u_ready, 2 * DEC + 2)
                        wait(pool, dec_added[g], n)
                        nc.gpsimd.tensor_tensor(spread_u[g][:], u_tok[:, head_cols(g, c)].rearrange("p (o d) -> p o d", o=1).broadcast_to([P, NS, HD]),
                                                spread(const("stream_of"), HD), ALU.mult).then_inc(dec_spread_u[g], 1)
                yield 55
                need(pool, t, "y_rstd", "y_centred")
                nc.gpsimd.tensor_tensor(heads(y_tok[:]), heads(y_tok[:]), spread(y_rstd, HD), ALU.mult).then_inc(ready["y_scaled"], 1)
                was_read(pool, t, "bonus")
                past(pool, t, "out")
                need(pool, t, "y_var")
                nc.gpsimd.tensor_tensor(heads(y_sq[:]), heads(v_tok[u][:]), spread(bonus[u][:], HD), ALU.mult).then_inc(ready["v_bonus"], 1)
                need(pool, t, "y_scaled")
                nc.gpsimd.tensor_tensor(y_tok[:], y_tok[:], gn[:, 0, :], ALU.mult).then_inc(ready["y_gained"], 1)
                need(pool, t, "y_gained")
                nc.gpsimd.tensor_tensor(y_tok[:], y_tok[:], gn[:, 1, :], ALU.add).then_inc(ready["y_based"], 1)
                need(pool, t, "y_based", "v_bonus")
                nc.gpsimd.tensor_tensor(y_tok[:], y_tok[:], y_sq[:], ALU.add).then_inc(ready["out"], 1)

            tiles(pool, front, back)

        @block.scalar
        def _(act):
            act.wait_ge(set_up, 7)
            act.wait_ge(states_turned, PAIRS + 1)
            nc.scalar.activation(shift_T[:].rearrange("p c b -> p (c b)"), ps_y[:, 0:CT * NS], ACT.Copy).then_inc(states_read, 1)
            for c, src in enumerate((ps_rhs, ps_u, ps_s, ps_inv[0])):
                nc.scalar.activation(states[:, c].rearrange("p b i -> p (b i)"), src[:], ACT.Copy).then_inc(states_read, 1)

            def front(t, u, mode):
                yield 5
                act.preload_act_table_set("sigmoid_and_others")
                need(act, t, "lora_in")
                was_written(act, t, "decay")
                nc.scalar.activation(th[:], xs[0:HD, CT - 1, :], ACT.Tanh).then_inc(ready["tanh"], 1)
                yield 8
                ps, read = written(act, t, "decay")
                past(act, t, "acc")
                for c in range(PAIRS):
                    last = nc.scalar.activation(sig[:, pair_cols(c)], ps[:, pair_cols(c)], ACT.Sigmoid, bias=chan(DECAY)[:, c:c + 1])
                last.then_inc(read, 1)
                ps, read = written(act, t, "iclr")
                past(act, t, "fac", "bmul")
                for c in range(PAIRS):
                    last = nc.scalar.activation(a_gate[:, pair_cols(c)], ps[:, pair_cols(c)], ACT.Sigmoid, bias=chan(ICLR)[:, c:c + 1])
                last.then_inc(read, 1)
                act.preload_act_table_set(ACT_TABLES)
                yield 12
                need(act, t, "kk")
                was_written(act, t, "kk_sum")
                nc.scalar.activation(kk_sq[:], kk[:], ACT.Square).then_inc(ready["kk_sq"], 1)
                yield 14
                need(act, t, "acc")
                past(act, t, "rhat", "ahat", "g_last")
                if mode == "s":
                    act.wait_ge(dec_copied, 3)
                nc.scalar.activation(runs(g_run, mode)[:, :, :, 1:], by_run(c4(acc[:]), mode), ACT.Exp, scale=-KAPPA).then_inc(ready["g_run"], 1)
                yield 15
                past(act, t, "bt", "kt")
                nc.scalar.activation(inv_g[:], acc[:], ACT.Exp, scale=KAPPA).then_inc(ready["inv_g"], 1)
                yield 17
                was_read(act, t, "kk_sum")
                nc.scalar.activation(kk_n[:], kk_n[:], ACT.Ln, scale=LN_UP).then_inc(ready["kk_log"], 1)
                need(act, t, "kk_log")
                nc.scalar.activation(kk_n[:], kk_n[:], ACT.Exp, scale=-0.5, bias=ln_back).then_inc(ready["rnorm"], 1)
                yield 21
                wait(act, ready["ps_y"], t - 1)
                wait(act, ready["v_bonus"], t - 1)
                for name, buf in (("v_tok", v_tok), ("k_tok", k_tok), ("b_tok", b_tok)):
                    ps, read = written(act, t, name)
                    nc.scalar.activation(buf[u][:], ps[:], ACT.Copy).then_inc(read, 1)
                yield 36
                ps, read = written(act, t, "bonus")
                nc.scalar.activation(bonus[u][:], ps[:, 0:H], ACT.Copy).then_inc(read, 1)

            def back(t, u, mode):
                for l in range(LEVELS[mode] - 1):
                    for g in range(2):
                        yield 3.5 * (l + 1) + 0.2 + g
                        act.wait_ge(turn_written[g], (LP - 1) * t + l + 1)
                        for i in range(2):
                            nc.scalar.activation(x_mat[half(i), g, :, half(i)], ps_turn[g][0:HD, :].rearrange("p (c n) -> p c n", c=PAIRS)[:, :, half(i)],
                                                 ACT.Copy).then_inc(x_ready[g], 1)
                if mode == "p":
                    for n in range(NCH):
                        yield 27 + 8 * n
                        act.wait_ge(rhs_written, 2 * t + n + 1)
                        nc.scalar.activation(rhs[half(n), :], ps_rhs[half(n), :], ACT.Copy).then_inc(rhs_ready, 1)
                        yield 29 + 8 * n
                        act.wait_ge(u_written, 2 * t + n + 1)
                        nc.scalar.activation(u_tok[half(n), :], ps_u[half(n), :], ACT.Copy).then_inc(u_ready, 1)
                else:
                    yield 27
                    act.wait_ge(state_turned, 1)
                    nc.scalar.activation(state_back[:].rearrange("p c n -> p (c n)"), ps_s[:], ACT.Copy).then_inc(state_out, 1)
                    yield 29
                    for n, ps in enumerate((ps_u, ps_s)):
                        act.wait_ge(u_written, 2 * t + n + 1)
                        nc.scalar.activation(u_tok[half(n), :], ps[half(n), :], ACT.Copy).then_inc(u_ready, 1)
                yield 47
                need(act, t, "y_centred")
                past(act, t, "out")
                nc.scalar.activation(y_sq[:], y_tok[:], ACT.Square).then_inc(ready["y_sq"], 1)
                yield 50
                need(act, t, "y_var")
                nc.scalar.activation(y_rstd, y_var, ACT.Ln, scale=1.0 / HD, bias=gn_eps).then_inc(ready["y_log"], 1)
                need(act, t, "y_log")
                nc.scalar.activation(y_rstd, y_rstd, ACT.Exp, scale=-0.5).then_inc(ready["y_rstd"], 1)
                if mode == "s":
                    for b in range(NS):
                        act.wait_ge(turned_back, b + 1)
                        nc.scalar.activation(st_nat[:, b, :], ps_inv[b % 2][0:HD, :], ACT.Copy).then_inc(nat_ready, 1)

            tiles(act, front, back)

        @block.vector
        def _(dve):
            dve.wait_ge(set_up, 7)

            def masked(out, ps, mask, n, read):
                m = mask.rearrange("p (o w) -> p o w", o=1).broadcast_to([P, n, mask.shape[1]])
                nc.vector.tensor_tensor(out, ps[:].rearrange("p (c w) -> p c w", c=n), m, ALU.mult).then_inc(read, 1)

            def front(t, u, mode):
                yield -1
                if mode == "s":
                    dve.wait_ge(cur_loaded[u], 8 * t + 16)
                    dve.wait_ge(states_read, PAIRS + 1)
                    past(dve, t, "g_last", "ahat", "rhat")
                    v = runs(cur[u], mode)
                    nc.vector.tensor_copy(v[:, :, :, 1:], by_run(dec_cols[:], mode)).then_inc(dec_copied, 1)
                    nc.vector.tensor_copy(v[:, :, :, 0], shift_T[:]).then_inc(dec_copied, 1)
                    nc.vector.memset(runs(g_run, mode)[:, :, :, 0], 1.0).then_inc(dec_copied, 1)
                yield 3
                need(dve, t, "delta")
                now, _ = cur_views(u, mode)
                for ct in [CT - 1] + list(range(CT - 1)):
                    x = xs[:, ct] if mode == "p" else xs[:, ct].rearrange("p (n l) -> p n l", n=NS)
                    op = nc.vector.scalar_tensor_tensor(out=x, in0=x, scalar=per_ch[:, ct:ct + 1], in1=now[:, ct],
                                                        op0=ALU.mult, op1=ALU.add)
                    if ct == CT - 1:
                        op.then_inc(ready["lora_in"], 1)
                op.then_inc(ready["xs"], 1)
                yield 11
                was_read(dve, t, "decay")
                past(dve, t, "g_run", "inv_g")
                nc.vector.tensor_tensor_scan(acc[:], const("run", mode), sig[:], 0.0, ALU.mult, ALU.add).then_inc(ready["acc"], 1)
                yield 13
                was_read(dve, t, "iclr")
                past(dve, t, "kmod")
                for c in range(PAIRS):
                    last = nc.vector.tensor_scalar(fac[:, pair_cols(c)], a_gate[:, pair_cols(c)], chan(KICLR)[:, c:c + 1],
                                                   chan(KICLR_REST)[:, c:c + 1], ALU.mult, ALU.add)
                last.then_inc(ready["fac"], 1)
                yield 16
                ps, read = written(dve, t, "kk_sum")
                past(dve, t, "ahat", "bmul")
                nc.vector.tensor_scalar(kk_n[:], ps[:], 1e-24, None, ALU.max).then_inc(read, 1)
                yield 18
                need(dve, t, "rnorm", "kk")
                nc.vector.scalar_tensor_tensor(out=kk_n[:], in0=kk[:], scalar=-1.0, in1=kk_n[:], op0=ALU.mult,
                                               op1=ALU.mult).then_inc(ready["kk_n"], 1)
                need(dve, t, "kk_n", "g_run")
                wait(dve, ready["ps_y"], t - 1)
                nc.vector.tensor_tensor(by_run(ar[u][:, :, 0, :], mode), by_run(c4(kk_n[:]), mode),
                                        runs(g_run, mode)[:, :, :, 0:CH if mode == "p" else SL], ALU.mult).then_inc(ready["ahat"], 1)
                past(dve, t, "bt")
                nc.vector.scalar_tensor_tensor(out=bmul[:], in0=kk_n[:], scalar=-1.0, in1=a_gate[:], op0=ALU.mult,
                                               op1=ALU.mult).then_inc(ready["bmul"], 1)
                need(dve, t, "bmul", "inv_g")
                was_written(dve, t, "RB1")
                nc.vector.tensor_tensor(bt[:], bmul[:], inv_g[:], ALU.mult).then_inc(ready["bt"], 1)
                need(dve, t, "kmod")
                was_written(dve, t, "AK11")
                nc.vector.tensor_tensor(kt[:], kmod[:], inv_g[:], ALU.mult).then_inc(ready["kt"], 1)
                wait(dve, state_ready, 2 * (t - 1))
                k = NCH if mode == "p" else NS
                nc.vector.tensor_copy(g_last[u][:, :, 0:k], runs(g_run, mode)[:, :, :, CH if mode == "p" else SL]).then_inc(ready["g_last"], 1)
                wait(dve, ready["ps_y"], t - 1)
                for name, out, mask, n in (
                        [(f"A{g}", a_mat[u][:, g], const("lower", mode), PAIRS) for g in range(2)]
                        + [(f"AK{g}{i}", ak_T[u][:, g, 2 * i:2 * i + 2].rearrange("p c k n -> p c (k n)"), const("upper", mode), 2)
                           for i in range(2) for g in range(2)]
                        + [(f"RB{g}", rb_T[u][:, g], const("upper", mode)[:, P:2 * P], PAIRS) for g in range(2)]):
                    yield 25 + 1.3 * (JOBS.index(name) - 6)
                    ps, read = written(dve, t, name)
                    masked(out, ps, mask, n, read)

            def back(t, u, mode):
                ident_c = const("ident_c").rearrange("p (o n) -> p o n", o=1).broadcast_to([P, PAIRS, CH])
                for l in range(LEVELS[mode]):
                    level = const("levels", mode)[:, l * CH:(l + 1) * CH].rearrange("p (o n) -> p o n", o=1).broadcast_to([P, PAIRS, CH])
                    base = (2 * LP - 1) * t
                    for g in range(2):
                        yield 3.5 * l + 0.5 + g
                        dve.wait_ge(inv_written[g], base + (1 if l == 0 else 2 * l))
                        if l == 0 and g == 0:
                            wait(dve, u_written, 2 * t)
                        nc.vector.tensor_tensor(q_mat[:, g], ps_inv[g][:, 0:PAIRS * CH].rearrange("p (c n) -> p c n", c=PAIRS),
                                                level, ALU.mult).then_inc(q_ready[g], 1)
                        yield 3.5 * l + 1.5 + g
                        if l == 0:
                            dve.wait_ge(q_ready[g], LP * t + 1)
                            nc.vector.tensor_tensor(y_mat[:, g], q_mat[:, g], ident_c, ALU.add).then_inc(y_ready[g], 1)
                        else:
                            dve.wait_ge(inv_written[g], base + 2 * l + 1)
                            nc.vector.tensor_tensor(y_mat[:, g], y_mat[:, g],
                                                    ps_inv[g][:, PAIRS * CH:].rearrange("p (c n) -> p c n", c=PAIRS),
                                                    ALU.add).then_inc(y_ready[g], 1)
                if mode == "p":
                    y_src, DIV = ps_y, None
                    for n in range(NCH):
                        yield 32 + 8 * n
                        dve.wait_ge(s_written, 2 * t + n + 1)
                        need(dve, t, "g_last")
                        for i in range(2):
                            last = nc.vector.tensor_tensor(state[half(i), :, half(i)], state[half(i), :, half(i)],
                                                           ps_s[half(i), :].rearrange("p (c n) -> p c n", c=PAIRS)[:, :, half(i)], ALU.add)
                        last.then_inc(s_added, 1)
                        dve.wait_ge(s_added, 2 * t + n + 1)
                        for i in range(2):
                            g_l = g_last[u][half(i), :, n:n + 1].broadcast_to([HD, PAIRS, HD])
                            last = nc.vector.tensor_tensor(state[half(i), :, half(i)], state[half(i), :, half(i)], g_l, ALU.mult)
                        last.then_inc(state_ready, 1)
                    yield 44
                    need(dve, t, "ps_y")
                else:
                    yield 24
                    for i in range(2 * PAIRS):
                        for g in range(2):
                            dve.wait_ge(dec_written[g], i + 1)
                            nc.vector.tensor_tensor(spread_s[g][:], ps_inv[g][:].rearrange("p (b d) -> p b d", b=NS),
                                                    spread(const("stream_of"), HD), ALU.mult).then_inc(dec_masked[g], 1)
                            dve.wait_ge(dec_masked[g], i + 1)
                            nc.vector.tensor_reduce(from_state[i % 2][:, head_cols(g, i // 2)],
                                                    spread_s[g][:].rearrange("p b d -> p d b"), AX_X, ALU.add).then_inc(dec_summed[g], 1)
                    yield 27
                    dve.wait_ge(rhs_written, 2 * t + 1)
                    for g in range(2):
                        dve.wait_ge(dec_summed[g], 2 * PAIRS)
                    nc.vector.tensor_tensor(rhs[:], ps_rhs[:], from_state[0][:], ALU.add).then_inc(rhs_ready, 1)
                    yield 44
                    need(dve, t, "ps_y")
                    nc.vector.tensor_tensor(from_state[1][:], ps_y[:], from_state[1][:], ALU.add).then_inc(y_raw_ready, 1)
                    dve.wait_ge(y_raw_ready, 1)
                    y_src = from_state[1]
                past(dve, t, "y_centred")
                nc.vector.tensor_reduce(y_sum, heads(y_src[:]), AX_X, ALU.add).then_inc(ready["y_sum"], 1)
                need(dve, t, "y_sum")
                nc.vector.tensor_scalar(y_mean, y_sum, 1.0 / HD, None, ALU.mult).then_inc(ready["y_mean"], 1)
                need(dve, t, "y_mean")
                wait(dve, o_stored, 16 * t)
                nc.vector.tensor_tensor(heads(y_tok[:]), heads(y_src[:]), spread(y_mean, HD), ALU.subtract).then_inc(ready["y_centred"], 1)
                if mode == "s":
                    need(dve, t, "g_last")
                    for c in range(PAIRS):
                        for g in range(2):
                            wait(dve, dec_added[g], c)
                            nc.vector.tensor_tensor(spread_s[g][:], v_tok[u][:, head_cols(g, c)].rearrange("p (o d) -> p o d", o=1).broadcast_to([P, NS, HD]),
                                                    spread(const("stream_of"), HD), ALU.mult).then_inc(dec_spread_v[g], 1)
                            dve.wait_ge(dec_written[g], 2 * PAIRS + c + 1)
                            nc.vector.tensor_tensor(states[half(g), c], states[half(g), c],
                                                    ps_inv[g][half(g), :].rearrange("p (b d) -> p b d", b=NS), ALU.add).then_inc(dec_added[g], 1)
                            dve.wait_ge(dec_added[g], c + 1)
                            g_l = g_last[u][half(g), c, :].rearrange("p (b o) -> p b o", o=1).broadcast_to([HD, NS, HD])
                            nc.vector.tensor_tensor(states[half(g), c], states[half(g), c], g_l, ALU.mult).then_inc(dec_state[g], 1)
                yield 48
                need(dve, t, "y_sq")
                nc.vector.tensor_reduce(y_var, heads(y_sq[:]), AX_X, ALU.add).then_inc(ready["y_var"], 1)

            tiles(dve, front, back)

        @block.tensor
        def _(pe):
            pe.wait_ge(states_loaded, 32)
            pe.wait_ge(params_loaded, 16 * 11)
            for ct in range(CT):
                last = nc.tensor.transpose(ps_y[:, ct * NS:(ct + 1) * NS], st_shift[:, ct * P:(ct + 1) * P], ident[0:NS, 0:NS])
            last.then_inc(states_turned, 1)
            for c, out in enumerate((ps_rhs, ps_u, ps_s, ps_inv[0])):
                for b in range(NS):
                    last = nc.tensor.transpose(out[:, b * HD:(b + 1) * HD], st_nat[:, b, pair_cols(c)], ident[0:HD, 0:HD])
                last.then_inc(states_turned, 1)
            pe.wait_ge(states_read, PAIRS + 1)
            pe.wait_ge(set_up, 7)

            def front(t, u, mode):
                yield 7
                need(pe, t, "tanh")
                ps, done = free_bank(t, "decay")
                for c in range(PAIRS):
                    last = nc.tensor.matmul(ps[:, pair_cols(c)], lora_w[0:HD, pair_cols(c)], th[:], start=True, stop=True)
                last.then_inc(done, 1)
                ps, done = free_bank(t, "iclr")
                for c in range(PAIRS):
                    last = nc.tensor.matmul(ps[:, pair_cols(c)], lora_w[HD:P, pair_cols(c)], xs[HD:P, CT - 1, :], start=True, stop=True)
                last.then_inc(done, 1)
                yield 14
                need(pe, t, "kk_sq")
                ps, done = free_bank(t, "kk_sum")
                nc.tensor.matmul(ps[:], const("head_ones"), kk_sq[:], start=True, stop=True).then_inc(done, 1)
                yield 15
                for name, src, k in (("v_tok", xs[:, 8:12], "xs"), ("k_tok", c4(kt[:]), "kt"), ("b_tok", c4(bt[:]), "bt")):
                    if k == "kt":
                        yield 21
                    need(pe, t, k)
                    ps, done = free_bank(t, name)
                    for c in range(PAIRS):
                        last = nc.tensor.transpose(ps[:, pair_cols(c)], src[:, c], ident)
                    last.then_inc(done, 1)
                need(pe, t, "ahat", "rhat")
                for g in range(2):
                    yield 24 + g
                    ps, done = free_bank(t, f"A{g}")
                    for c in range(PAIRS):
                        last = nc.tensor.matmul(ps[:, pair_cols(c)], ar[u][half(g), c, 0, :], bt[half(g), pair_cols(c)], start=True, stop=True)
                    last.then_inc(done, 1)
                for i in range(2):
                    for g in range(2):
                        yield 27 + 2 * i + g
                        ps, done = free_bank(t, f"AK{g}{i}")
                        for c in (2 * i, 2 * i + 1):
                            last = nc.tensor.matmul(ps[:, (c - 2 * i) * 2 * P:(c - 2 * i + 1) * 2 * P], kt[half(g), pair_cols(c)],
                                                    ar[u][half(g), c].rearrange("p k n -> p (k n)"), start=True, stop=True)
                        last.then_inc(done, 1)
                for g in range(2):
                    yield 32 + g
                    ps, done = free_bank(t, f"RB{g}")
                    for c in range(PAIRS):
                        last = nc.tensor.matmul(ps[:, pair_cols(c)], bt[half(g), pair_cols(c)], ar[u][half(g), c, 1, :], start=True, stop=True)
                    last.then_inc(done, 1)
                yield 35
                need(pe, t, "rkr")
                ps, done = free_bank(t, "bonus")
                for c in range(PAIRS):
                    last = nc.tensor.matmul(ps[:, 2 * c:2 * c + 2], rk[:, pair_cols(c)], const("head_of"), start=True, stop=True)
                last.then_inc(done, 1)

            def back(t, u, mode):
                for l in range(LEVELS[mode]):
                    for g in range(2):
                        yield 3.5 * l + g
                        if l == 0:
                            was_read(pe, t, f"A{g}")
                        else:
                            pe.wait_ge(y_ready[g], LP * t + l)
                            if l == 1:
                                wait(pe, (rhs_ready, u_ready)[g], 2 * t)
                        for c in range(PAIRS):
                            last = nc.tensor.matmul(ps_inv[g][:, c * CH:(c + 1) * CH], a_mat[u][:, g, c, :],
                                                    const("ident_c") if l == 0 else y_mat[:, g, c, :], start=True, stop=True)
                        last.then_inc(inv_written[g], 1)
                        if l > 0:
                            for c in range(PAIRS):
                                last = nc.tensor.transpose(ps_turn[g][0:HD, pair_cols(c)], y_mat[:, g, c, :], ident)
                            last.then_inc(turn_written[g], 1)
                    for g in range(2):
                        if l > 0:
                            yield 3.5 * l + 1 + g
                            pe.wait_ge(x_ready[g], 2 * (LP - 1) * t + 2 * l)
                            pe.wait_ge(q_ready[g], LP * t + l + 1)
                            for c in range(PAIRS):
                                last = nc.tensor.matmul(ps_inv[g][:, (PAIRS + c) * CH:(PAIRS + c + 1) * CH], x_mat[:, g, c, :],
                                                        q_mat[:, g, c, :], start=True, stop=True)
                            last.then_inc(inv_written[g], 1)
                yield 21
                for g in range(2):
                    pe.wait_ge(x_ready[g], 2 * (LP - 1) * t + 2 * (LEVELS[mode] - 1))
                    b, n = job_count(t, f"RB{g}")
                    pe.wait_ge(job_read[b], n + 1)
                wait(pe, ready["y_centred"], t)
                all_heads = [(g, c) for c in range(PAIRS) for g in range(2)]
                for kind, out in ((0, ps_rhs), (1, ps_y)):
                    for g, c in all_heads:
                        last = nc.tensor.matmul(out[:, head_cols(g, c)], ak_T[u][:, g, c, kind, :], v_tok[u][:, head_cols(g, c)],
                                                start=(g == 0 and c == 0), stop=(mode == "s" and kind == 0 and (g, c) == all_heads[-1]))
                    if mode == "s" and kind == 0:
                        last.then_inc(rhs_written, 1)

                def solve(n, out):
                    for g, c in all_heads:
                        last = nc.tensor.matmul(out[half(n), head_cols(g, c)], y_mat[half(n), g, c, :], rhs[half(n), head_cols(g, c)],
                                                start=True, stop=True)
                    last.then_inc(u_written, 1)

                if mode == "p":
                    for n in range(NCH):
                        yield 26 + 8 * n
                        tokens = slice(n * CH, (n + 1) * CH)
                        wait(pe, state_ready, 2 * t + n)
                        for c in range(PAIRS):
                            last = nc.tensor.matmul(ps_rhs[half(n), pair_cols(c)], ar[u][:, c, 0, tokens], state[:, c, :], start=False, stop=(c == PAIRS - 1))
                        last.then_inc(rhs_written, 1)
                        for c in range(PAIRS - 1):
                            nc.tensor.matmul(ps_y[half(n), pair_cols(c)], ar[u][:, c, 1, tokens], state[:, c, :], start=False, stop=False)
                        for c in range(PAIRS):
                            nc.tensor.matmul(ps_s[:, pair_cols(c)], k_tok[u][half(n), pair_cols(c)], v_tok[u][half(n), pair_cols(c)],
                                             start=(c == 0), stop=False)
                        yield 28 + 8 * n
                        pe.wait_ge(rhs_ready, 2 * t + n + 1)
                        c = PAIRS - 1
                        nc.tensor.matmul(ps_y[half(n), pair_cols(c)], ar[u][:, c, 1, tokens], state[:, c, :], start=False, stop=False)
                        solve(n, ps_u)
                        yield 30 + 8 * n
                        pe.wait_ge(u_ready, 2 * t + n + 1)
                        for c in range(PAIRS):
                            last = nc.tensor.matmul(ps_s[:, pair_cols(c)], b_tok[u][half(n), pair_cols(c)], u_tok[half(n), pair_cols(c)],
                                                    start=False, stop=(c == PAIRS - 1))
                        last.then_inc(s_written, 1)
                else:
                    yield 22
                    pe.wait_ge(state_ready, NCH * TILES)
                    for c in range(PAIRS):
                        last = nc.tensor.transpose(ps_s[:, pair_cols(c)], state[:, c, :], ident)
                    last.then_inc(state_turned, 1)
                    for g in range(2):
                        pe.wait_ge(y_ready[g], LP * t + LEVELS[mode])
                    for i in range(2 * PAIRS):
                        for g in range(2):
                            wait(pe, dec_masked[g], i)
                            nc.tensor.matmul(ps_inv[g][:], ar[u][half(g), i // 2, i % 2, :], states[half(g), i // 2].rearrange("p b i -> p (b i)"),
                                             start=True, stop=True).then_inc(dec_written[g], 1)
                    yield 28
                    pe.wait_ge(rhs_ready, 2 * t + 1)
                    pe.wait_ge(state_out, 1)
                    solve(0, ps_u)
                    solve(1, ps_s)
                    pe.wait_ge(u_ready, 2 * t + 2)
                yield 43
                for g, c in all_heads:
                    last = nc.tensor.matmul(ps_y[:, head_cols(g, c)], rb_T[u][:, g, c, :], u_tok[:, head_cols(g, c)], start=False,
                                            stop=((g, c) == all_heads[-1]))
                last.then_inc(ready["ps_y"], 1)
                if mode == "s":
                    for c in range(PAIRS):
                        for g in range(2):
                            pe.wait_ge(dec_masked[g], 2 * PAIRS)
                            wait(pe, dec_added[g], c)
                            pe.wait_ge(dec_spread_v[g], c + 1)
                            nc.tensor.matmul(ps_inv[g][half(g), :], k_tok[u][:, head_cols(g, c)], spread_s[g][:].rearrange("p b d -> p (b d)"),
                                             start=True, stop=False)
                            pe.wait_ge(dec_spread_u[g], c + 1)
                            nc.tensor.matmul(ps_inv[g][half(g), :], b_tok[u][:, head_cols(g, c)], spread_u[g][:].rearrange("p b d -> p (b d)"),
                                             start=False, stop=True).then_inc(dec_written[g], 1)
                    pe.wait_ge(dec_state[0], PAIRS)
                    pe.wait_ge(dec_state[1], PAIRS)
                    for b in range(NS):
                        wait(pe, nat_ready, b - 1)
                        for c in range(PAIRS):
                            last = nc.tensor.transpose(ps_inv[b % 2][0:HD, pair_cols(c)], states[:, c, b, :], ident)
                        last.then_inc(turned_back, 1)

            tiles(pe, front, back)


def output_phase(nc, io):
    with ExitStack() as ctx:
        def sb(name, shape, dt=F32):
            return ctx.enter_context(nc.sbuf_tensor(name, shape, dt))

        def sem(name):
            return ctx.enter_context(nc.semaphore(name))

        w_hi, w_lo = sb("o_w_hi", [P, KT, 2 * D], F32R), sb("o_w_lo", [P, KT, 2 * D], F32R)
        w_raw = [sb(f"o_w_raw{i}", [P, KT, P]) for i in range(2)]
        xT = [sb(f"o_xT{i}", [P, KT, P]) for i in range(2)]
        x_hi, x_lo = sb("o_x_hi", [P, KT, P], F32R), sb("o_x_lo", [P, KT, P], F32R)
        o_tok = [sb(f"o_o{i}", [P, 2, AW]) for i in range(2)]
        gate, z = sb("o_gate", [P, 2, AW]), sb("o_z", [P, 2, AW])
        z_hi, z_lo = sb("o_z_hi", [P, KT, P], F32R), sb("o_z_lo", [P, KT, P], F32R)
        x_tok = [sb(f"o_x{i}", [P, D]) for i in range(2)]
        y_tok = sb("o_y", [P, D])
        ident = sb("o_ident", [P, P])
        ps_gate = [ctx.enter_context(nc.psum_tensor(f"o_ps_gate{i}", [P, D], F32)) for i in range(2)]
        ps_zT = ctx.enter_context(nc.psum_tensor("o_ps_zT", [P, D], F32))
        ps_y = ctx.enter_context(nc.psum_tensor("o_ps_y", [P, D], F32))

        ident_zero, ident_ready = sem("o_ident_zero"), sem("o_ident_ready")
        w_loaded = [sem(f"o_w_loaded{i}") for i in range(2)]
        w_hi_ready, w_lo_ready = sem("o_w_hi_ready"), sem("o_w_lo_ready")
        xT_loaded = [sem(f"o_xT_loaded{i}") for i in range(2)]
        o_loaded = [sem(f"o_o_loaded{i}") for i in range(2)]
        x_loaded = [sem(f"o_x_loaded{i}") for i in range(2)]
        x_hi_ready, x_lo_ready, gate_ready = sem("o_x_hi_ready"), sem("o_x_lo_ready"), sem("o_gate_ready")
        gate_silu, z_ready = sem("o_gate_silu"), sem("o_z_ready")
        z_turned, z_hi_ready, z_lo_ready = sem("o_z_turned"), sem("o_z_hi_ready"), sem("o_z_lo_ready")
        y_summed, y_ready, y_stored = sem("o_y_summed"), sem("o_y_ready"), sem("o_y_stored")

        N = TILES + 1
        w_in = io["w_in"][0].rearrange("(k p) n -> p k n", p=P)
        w_out = io["w_out"][0].rearrange("(k p) n -> p k n", p=P)
        GATE_ATT, GATE_RWKV = 3 * AW, 4 * AW + SHIFT_COLS
        blocks = ([w_in[:, :, GATE_ATT + i * P:GATE_ATT + (i + 1) * P] for i in range(4)]
                  + [w_in[:, :, GATE_RWKV + i * P:GATE_RWKV + (i + 1) * P] for i in range(4)]
                  + [w_out[:, :, i * P:(i + 1) * P] for i in range(8)])
        block = ctx.enter_context(nc.Block())

        def tiles(eng, step):
            step(0, 0)
            step(1, 1)
            with eng.Fori(1, TILES // 2) as i:
                step(i * 2, 0)
                step(i * 2 + 1, 1)
            step(DEC, 0)

        def loads(t, u):
            return 8 * t + 16 - 8 * u

        @block.sync
        def _(sp):
            for b, w in enumerate(blocks[:2]):
                sp.dma_start(w_raw[b % 2][:], w).then_inc(w_loaded[b % 2], 16)
            for u in range(2):
                sp.dma_start(xT[u][:], io["xT"][u]).then_inc(xT_loaded[u], 16)
            for b, w in enumerate(blocks):
                if b >= 2:
                    sp.wait_ge(w_lo_ready, b - 1)
                    sp.dma_start(w_raw[b % 2][:], w).then_inc(w_loaded[b % 2], 16)
            for u in range(2):
                sp.dma_start(o_tok[u][:, 0, :], io["o_att"][u * P:(u + 1) * P, :]).then_inc(o_loaded[u], 16)
                sp.dma_start(o_tok[u][:, 1, :], io["o_rwkv"][u * P:(u + 1) * P, :]).then_inc(o_loaded[u], 16)
                sp.dma_start(x_tok[u][:], rows_of(io["x_prompt"], D)[u * P:(u + 1) * P, :]).then_inc(x_loaded[u], 16)

            def store(t):
                last = t_known(t) and t == DEC
                y = rows_of(io["y_sample"], D) if last else rows_of(io["y_prompt"], D)[bass.ds(t * P, P), :]
                sp.wait_ge(y_ready, 2 * t + 2)
                sp.dma_start(y, y_tok[:]).then_inc(y_stored, 16)

            def move(t, u, nxt):
                sp.wait_ge(x_lo_ready, t + 1)
                sp.dma_start(xT[u][:], io["xT"][bass.ds(nxt, 1)].rearrange("a p k n -> (a p) k n")).then_inc(xT_loaded[u], 16)
                sp.wait_ge(z_ready, t + 1)
                sp.dma_start(o_tok[u][:, 0, :], io["o_att"][bass.ds(nxt * P, P), :]).then_inc(o_loaded[u], 16)
                sp.dma_start(o_tok[u][:, 1, :], io["o_rwkv"][bass.ds(nxt * P, P), :]).then_inc(o_loaded[u], 16)
                store(t)
                last = t_known(nxt) and nxt == DEC
                x = rows_of(io["x_sample"], D) if last else rows_of(io["x_prompt"], D)[bass.ds(nxt * P, P), :]
                sp.dma_start(x_tok[u][:], x).then_inc(x_loaded[u], 16)

            with sp.Fori(0, TILES // 2 - 1) as i:
                move(i * 2, 0, i * 2 + 2)
                move(i * 2 + 1, 1, i * 2 + 3)
            move(TILES - 2, 0, DEC)
            store(TILES - 1)
            store(DEC)
            sp.wait_ge(y_stored, 16 * N)

        @block.gpsimd
        def _(pool):
            nc.gpsimd.memset(ident[:], 0.0).then_inc(ident_zero, 1)
            pool.wait_ge(ident_zero, 1)
            nc.gpsimd.affine_select(out=ident[:], in_=ident[:], compare_op=ALU.not_equal, fill=1.0, base=0,
                                    pattern=[[-1, P]], channel_multiplier=1).then_inc(ident_ready, 1)

            def split_lo(t, u):
                pool.wait_ge(x_hi_ready, t + 1)
                nc.gpsimd.tensor_tensor(x_lo[:], xT[u][:], x_hi[:].bitcast(F32), ALU.subtract).then_inc(x_lo_ready, 1)

            tiles(pool, split_lo)

        @block.scalar
        def _(act):
            def split_hi(t, u):
                act.wait_ge(xT_loaded[u], loads(t, u))
                wait(act, gate_ready, t)
                wait(act, x_lo_ready, t)
                nc.scalar.activation(x_hi[:], xT[u][:], ACT.Copy).then_inc(x_hi_ready, 1)

            split_hi(0, 0)
            for b in range(len(blocks)):
                act.wait_ge(w_loaded[b % 2], 16 * (b // 2 + 1))
                nc.scalar.activation(w_hi[:, :, b * P:(b + 1) * P], w_raw[b % 2][:], ACT.Copy).then_inc(w_hi_ready, 1)

            def step(t, u):
                act.wait_ge(gate_ready, t + 1)
                wait(act, z_ready, t)
                nc.scalar.activation(gate[:].rearrange("p g d -> p (g d)"), ps_gate[u][:], ACT.Silu).then_inc(gate_silu, 1)
                if not (t_known(t) and t == DEC):
                    split_hi(t + 1, 1 - u)
                act.wait_ge(z_turned, t + 1)
                wait(act, y_summed, 2 * t)
                nc.scalar.activation(z_hi[:].rearrange("p k n -> p (k n)"), ps_zT[:], ACT.Copy).then_inc(z_hi_ready, 1)

            tiles(act, step)

        @block.vector
        def _(dve):
            for b in range(len(blocks)):
                dve.wait_ge(w_hi_ready, b + 1)
                nc.vector.tensor_tensor(w_lo[:, :, b * P:(b + 1) * P], w_raw[b % 2][:],
                                        w_hi[:, :, b * P:(b + 1) * P].bitcast(F32), ALU.subtract).then_inc(w_lo_ready, 1)

            def step(t, u):
                dve.wait_ge(gate_silu, t + 1)
                dve.wait_ge(o_loaded[u], 2 * loads(t, u))
                wait(dve, z_turned, t)
                nc.vector.tensor_tensor(z[:], o_tok[u][:], gate[:], ALU.mult).then_inc(z_ready, 1)
                dve.wait_ge(z_hi_ready, t + 1)
                nc.vector.tensor_tensor(z_lo[:].rearrange("p k n -> p (k n)"), ps_zT[:],
                                        z_hi[:].rearrange("p k n -> p (k n)").bitcast(F32), ALU.subtract).then_inc(z_lo_ready, 1)
                dve.wait_ge(x_loaded[u], loads(t, u))
                wait(dve, y_stored, 16 * t)
                for j in range(2):
                    cols = slice(j * 512, (j + 1) * 512)
                    dve.wait_ge(y_summed, 2 * t + j + 1)
                    nc.vector.tensor_tensor(y_tok[:, cols], ps_y[:, cols], x_tok[u][:, cols], ALU.add).then_inc(y_ready, 1)

            tiles(dve, step)

        @block.tensor
        def _(pe):
            def passes(out, hi, lo, cols):
                for k in range(KT):
                    for i, (a, w) in enumerate(((hi, w_hi), (hi, w_lo), (lo, w_hi))):
                        mm = nc.tensor.matmul(out, a[:, k, :], w[:, k, cols], start=(k == 0 and i == 0),
                                              stop=(k == KT - 1 and i == 2))
                return mm

            def gates(t, u, j):
                if j == 0:
                    pe.wait_ge(x_lo_ready, t + 1)
                    wait(pe, gate_silu, t - 1)
                if t_known(t) and t == 0:
                    pe.wait_ge(w_lo_ready, 4 * (j + 1))
                last = passes(ps_gate[u][:, j * 512:(j + 1) * 512], x_hi, x_lo, slice(j * 512, (j + 1) * 512))
                if j == 1:
                    last.then_inc(gate_ready, 1)

            pe.wait_ge(ident_ready, 1)
            gates(0, 0, 0)
            gates(0, 0, 1)
            pe.wait_ge(w_lo_ready, len(blocks))

            def step(t, u):
                more = not (t_known(t) and t == DEC)
                if more:
                    gates(t + 1, 1 - u, 0)
                pe.wait_ge(z_ready, t + 1)
                wait(pe, z_lo_ready, t)
                for k in range(KT):
                    last = nc.tensor.transpose(ps_zT[:, k * P:(k + 1) * P], z[:].rearrange("p g d -> p (g d)")[:, k * P:(k + 1) * P],
                                               ident[:])
                last.then_inc(z_turned, 1)
                if more:
                    gates(t + 1, 1 - u, 1)
                pe.wait_ge(z_lo_ready, t + 1)
                wait(pe, y_ready, 2 * t)
                for j in range(2):
                    passes(ps_y[:, j * 512:(j + 1) * 512], z_hi, z_lo, slice(D + j * 512, D + (j + 1) * 512)).then_inc(y_summed, 1)

            tiles(pe, step)



_INS = ["x_prompt", "x_sample", "cache_attn_k", "cache_attn_v", "state_rwkv_wkv", "state_rwkv_shift", "norm_gain",
        "w_in", "q_norm_gain", "k_norm_gain", "rel_pos_bias", "shift_mix", "decay_base", "decay_lora_up", "iclr_base",
        "iclr_lora_up", "key_remove_scale", "key_iclr_scale", "bonus_scale", "out_norm_gain", "out_norm_bias", "w_out"]
_OUTS = [("y_prompt", (1, TILES * P, D)), ("y_sample", (NS, SL, D)),
         ("k_prompt_new", (1, 1, H, 512, HD)), ("v_prompt_new", (1, 1, H, 512, HD)),
         ("k_sample_new", (1, NS, H, SL, HD)), ("v_sample_new", (1, NS, H, SL, HD)),
         ("wkv_prompt_new", (1, 1, H, HD, HD)), ("wkv_sample_new", (1, NS, H, HD, HD)),
         ("shift_prompt_new", (1, 1, 1, SHIFT_COLS)), ("shift_sample_new", (1, NS, 1, SHIFT_COLS))]
_SCRATCH = [("xT", (TILES + 1, P, KT, P)), ("o_att", ((TILES + 1) * P, AW)), ("o_rwkv", ((TILES + 1) * P, AW)),
            ("proj_T", (SHIFT_TILES, P, 1 + (TILES + 1) * P)), ("rev_table", (H, P, 3 * P)), ("qT_new", (P, PAIRS, P)), ("kT_new", (P, PAIRS, P)), ("v_new", (P, AW))]


def program(nc, io):
    attention_phase(nc, io)
    cached_attention_phase(nc, io)
    rwkv_projection_phase(nc, io)
    rwkv_phase(nc, io)
    output_phase(nc, io)


def kernel(**inputs):
    import numpy as _np
    import concourse.bacc as _bacc
    from concourse.bass_utils import run_bass_kernel_spmd as _run

    nc = _bacc.Bacc("TRN2", target_bir_lowering=False, num_devices=1)
    arrays, io = {}, {}
    for name in _INS:
        a = _np.ascontiguousarray(inputs[name])
        arrays[f"in_{name}"] = a
        io[name] = nc.dram_tensor(f"in_{name}", a.shape, F32, kind="ExternalInput").ap()
    arrays["shape_consts"] = _np.ascontiguousarray(_np.concatenate(list(shape_constants().values()), 1))
    io["shape_consts"] = nc.dram_tensor("shape_consts", (P, CONST_W), F32, kind="ExternalInput").ap()
    for name, shape in _OUTS:
        io[name] = nc.dram_tensor(f"out_{name}", shape, F32, kind="ExternalOutput").ap()
    for name, shape in _SCRATCH:
        io[name] = nc.dram_tensor(f"scratch_{name}", shape, F32, kind="Internal").ap()
    program(nc, io)
    r = _run(nc, [arrays], core_ids=[0])
    return tuple(r.results[0][f"out_{name}"] for name, _ in _OUTS)
```

```python
from contextlib import ExitStack

import concourse.bass as bass
from concourse import mybir

F32 = mybir.dt.float32
F32R = mybir.dt.float32r
ACT = mybir.ActivationFunctionType
ALU = mybir.AluOpType
AX_X = mybir.AxisListType.X

P = 128
D = 1024
KT = D // P
HD = 64
H = 8
PAIRS = H // 2
AW = H * HD
TILES = 16
DEC = TILES
NS, SL = 8, 16
PAST = 256
SLOTS = 5
WIN = SLOTS * P
NEAR = 2 * P
FAR = WIN - NEAR
MAXREL = 128
CH = 64
MASKED = -3.0e38
SCALE = HD ** -0.5
EPS = 1e-6
SHIFT_COLS = 3 * AW + 128
ACT_TABLES = "natural_log_exp_and_others"


def wait(eng, sem, value):
    if isinstance(value, int) and value <= 0:
        return
    eng.wait_ge(sem, value)


def t_known(t):
    return isinstance(t, int)


def rows_of(dram, width):
    return dram.rearrange("b s d -> (b s) d")


def prompt_steps(eng, step):
    for t in range(4):
        step(t, t % 2)
    with eng.Fori(4, 12, 2) as t:
        step(t, 0)
        step(t + 1, 1)
    for t in range(12, TILES):
        step(t, t % 2)


def clear_semaphores(nc, held):
    with nc.Block() as block:
        @block.gpsimd
        def _(pool):
            numbers = sorted(sem.num for sem in held)
            if numbers[-1] - numbers[0] == len(numbers) - 1:
                pool.sem_clear(range(numbers[0], numbers[-1] + 1))
            else:
                for sem in held:
                    pool.sem_clear(sem)


def attention_phase(nc, io):
    with ExitStack() as ctx:
        def sb(name, shape, dt=F32):
            return ctx.enter_context(nc.sbuf_tensor(name, shape, dt))

        held = []

        def sem(name):
            held.append(ctx.enter_context(nc.semaphore(name)))
            return held[-1]

        QKV = 3 * AW
        w_hi = sb("a_w_hi", [P, KT, QKV], F32R)
        w_lo = sb("a_w_lo", [P, KT, QKV], F32R)
        w_raw = [sb(f"a_w_raw{i}", [P, KT, P]) for i in range(2)]
        x_tok = [sb(f"a_x{i}", [P, D]) for i in range(2)]
        xT = sb("a_xT", [P, KT, P])
        x_hi = [sb(f"a_x_hi{i}", [P, KT, P], F32R) for i in range(2)]
        x_lo = [sb(f"a_x_lo{i}", [P, KT, P], F32R) for i in range(2)]
        ident = sb("a_ident", [P, P])
        gainT = sb("a_gainT", [P, KT])
        qk_gain = sb("a_qk_gain", [P, 2, HD])
        near_bias = sb("a_near_bias", [P, H, NEAR])
        far_mask = sb("a_far_mask", [P, FAR])
        far_value = sb("a_far_value", [P, H])
        qk = sb("a_qk", [P, 2, AW])
        qk_n = sb("a_qk_n", [P, 2, AW])
        qT = sb("a_qT", [P, PAIRS, P])
        kT = [sb(f"a_kT{i}", [P, PAIRS, WIN]) for i in range(2)]
        v = [sb(f"a_v{i}", [P, SLOTS, AW]) for i in range(2)]
        probs = [sb(f"a_probs{i}", [P, WIN]) for i in range(2)]
        pT = [sb(f"a_pT{i}", [P, WIN]) for i in range(2)]
        o_tok = sb("a_o", [P, H, HD])
        small = sb("a_small", [P, 64])
        sumsq, rstd, logms = small[:, 0:1], small[:, 1:2], small[:, 2:3]
        neg_max = [small[:, 3:4], small[:, 4:5]]
        row_sum = small[:, 8:16]
        row_inv = small[:, 16:24]
        qk_ss, qk_rstd, eps = small[:, 24:40], small[:, 40:56], small[:, 5:6]

        ps_proj = [ctx.enter_context(nc.psum_tensor(f"a_ps_proj{i}", [P, 512], F32)) for i in range(2)]
        ps_score = [ctx.enter_context(nc.psum_tensor(f"a_ps_score{i}", [P, 1024], F32)) for i in range(2)]
        ps_turn = ctx.enter_context(nc.psum_tensor("a_ps_turn", [P, 512], F32))
        ps_out = ctx.enter_context(nc.psum_tensor("a_ps_out", [P, 512], F32))

        consts_loaded = sem("a_consts_loaded")
        ident_zero, ident_ready = sem("a_ident_zero"), sem("a_ident_ready")
        eps_ready = sem("a_eps_ready")
        rev_zero, rev_ready, table_stored = sem("a_rev_zero"), sem("a_rev_ready"), sem("a_table_stored")
        bias_loaded, bias_near, bias_ready = sem("a_bias_loaded"), sem("a_bias_near"), sem("a_bias_ready")
        w_loaded = [sem(f"a_w_loaded{i}") for i in range(2)]
        w_hi_ready, w_lo_ready = sem("a_w_hi_ready"), sem("a_w_lo_ready")
        x_loaded = [sem(f"a_x_loaded{i}") for i in range(2)]
        x_sumsq, x_logms, x_rstd, x_scaled = sem("a_x_sumsq"), sem("a_x_logms"), sem("a_x_rstd"), sem("a_x_scaled")
        x_turned, xT_ready, xT_stored = sem("a_x_turned"), sem("a_xT_ready"), sem("a_xT_stored")
        x_hi_ready, x_lo_ready = sem("a_x_hi_ready"), sem("a_x_lo_ready")
        proj_ready, proj_read = sem("a_proj_ready"), sem("a_proj_read")
        qk_sq, qk_summed, qk_logms = sem("a_qk_sq"), sem("a_qk_summed"), sem("a_qk_logms")
        qk_rstd_ready, qk_scaled, qk_normed = sem("a_qk_rstd"), sem("a_qk_scaled"), sem("a_qk_normed")
        qk_turned, qkT_ready, shifted = sem("a_qk_turned"), sem("a_qkT_ready"), sem("a_shifted")
        score_ready, biased, max_ready = sem("a_score_ready"), sem("a_biased"), sem("a_max_ready")
        p_ready, p_turned, pT_ready, pv_done = sem("a_p_ready"), sem("a_p_turned"), sem("a_pT_ready"), sem("a_pv_done")
        inv_ready, out_ready, out_stored = sem("a_inv_ready"), sem("a_out_ready"), sem("a_out_stored")
        kv_stored = sem("a_kv_stored")

        xp, xs = rows_of(io["x_prompt"], D), rows_of(io["x_sample"], D)
        w_in = io["w_in"][0].rearrange("(k p) n -> p k n", p=P)
        table = io["rel_pos_bias"][0]
        rev = w_raw[0][0:H, :, :].rearrange("h a b -> h (a b)")[:, 0:3 * P]
        tab = w_raw[1][0:H, :, :].rearrange("h a b -> h (a b)")[:, 0:2 * MAXREL + 1]
        rev_d = io["rev_table"]
        WB = QKV // P

        PAR = [0]

        def half_count(n, u):
            return 8 * n + 16 - 8 * u

        ctx.callback(clear_semaphores, nc, held)
        block = ctx.enter_context(nc.Block())

        def x_rows(t):
            return xs if isinstance(t, int) and t == DEC else xp[bass.ds(t * P, P), :]

        def first_slot(t):
            return SLOTS - 1 - t if isinstance(t, int) and t < SLOTS - 1 else 0

        @block.sync
        def _(sp):
            sp.dma_start(tab, table).then_inc(consts_loaded, 16)
            sp.dma_start(x_tok[0][:], x_rows(0)).then_inc(x_loaded[0], 16)
            sp.dma_start(x_tok[1][:], x_rows(1)).then_inc(x_loaded[1], 16)
            sp.dma_start(gainT[:], io["norm_gain"][0].rearrange("(k p) -> p k", p=P),
                         allow_slow_non_contiguous=True).then_inc(consts_loaded, 16)
            sp.dma_start(qk_gain[:, 0, :], io["q_norm_gain"][0].partition_broadcast(P)).then_inc(consts_loaded, 16)
            sp.dma_start(qk_gain[:, 1, :], io["k_norm_gain"][0].partition_broadcast(P)).then_inc(consts_loaded, 16)
            sp.wait_ge(rev_ready, 2)
            sp.dma_start(rev_d, rev.rearrange("h (o n) -> h o n", o=1).broadcast_to([H, P, 3 * P])).then_inc(table_stored, 16)
            sp.wait_ge(table_stored, 16)
            for h in range(H):
                src = bass.AP(rev_d.tensor, h * P * 3 * P + P - 1, [[3 * P - 1, P], [1, NEAR]])
                sp.dma_start(near_bias[:, h, :], src).then_inc(bias_loaded, 16)
            sp.dma_start(far_value[:], bass.AP(rev_d.tensor, 0, [[0, P], [P * 3 * P, H]]),
                         allow_slow_non_contiguous=True).then_inc(bias_loaded, 16)
            def store_xT(n):
                sp.wait_ge(xT_ready, 2 * n + 2)
                sp.dma_start(io["xT"][bass.ds(n, 1)].rearrange("a p k n -> (a p) k n"), xT[:]).then_inc(xT_stored, 16)

            for b in range(WB):
                if b == 2:
                    store_xT(0)
                    store_xT(1)
                if b >= 2:
                    sp.wait_ge(w_lo_ready, b - 1)
                sp.dma_start(w_raw[b % 2][:], w_in[:, :, b * P:(b + 1) * P]).then_inc(w_loaded[b % 2], 16)

            def step(t, u):
                if t_known(t) and t >= 12:
                    rows = slice((t - 12) * P, (t - 11) * P)
                    sp.wait_ge(qk_normed, t + 1)
                    sp.dma_start(io["k_prompt_new"][0, 0, :, rows, :].rearrange("h s d -> s h d"),
                                 qk_n[:, 1, :].rearrange("p (h d) -> p h d", h=H)).then_inc(kv_stored, 16)
                    sp.wait_ge(proj_read, 3 * (t + 1))
                    sp.dma_start(io["v_prompt_new"][0, 0, :, rows, :].rearrange("h s d -> s h d"),
                                 v[u][:, SLOTS - 1, :].rearrange("p (h d) -> p h d", h=H)).then_inc(kv_stored, 16)
                if not (t_known(t) and t + 2 > DEC):
                    sp.wait_ge(x_turned, 2 * t + 2)
                    sp.dma_start(x_tok[u][:], x_rows(t + 2)).then_inc(x_loaded[u], 16)
                    store_xT(t + 2)
                sp.wait_ge(out_ready, t + 1)
                sp.dma_start(io["o_att"][bass.ds(t * P, P), :],
                             o_tok[:].rearrange("p h d -> p (h d)")).then_inc(out_stored, 16)

            prompt_steps(sp, step)
            sp.wait_ge(qk_normed, DEC + 1)
            sp.wait_ge(proj_read, 3 * (DEC + 1))
            sp.dma_start(io["k_new"], qk_n[:, 1, :]).then_inc(kv_stored, 16)
            sp.wait_ge(qkT_ready, 2 * (DEC + 1))
            sp.dma_start(io["qT_new"], qT[:]).then_inc(kv_stored, 16)
            sp.dma_start(io["kT_new"], kT[0][:, :, FAR + P:WIN]).then_inc(kv_stored, 16)
            sp.dma_start(io["v_new"], v[0][:, SLOTS - 1, :]).then_inc(kv_stored, 16)
            sp.wait_ge(kv_stored, 16 * (2 * 4 + 4))
            sp.wait_ge(xT_stored, 16 * (TILES + 1))
            sp.wait_ge(out_stored, 16 * TILES)

        @block.gpsimd
        def _(pool):
            nc.gpsimd.memset(ident[:], 0.0).then_inc(ident_zero, 1)
            pool.wait_ge(ident_zero, 1)
            nc.gpsimd.affine_select(out=ident[:], in_=ident[:], compare_op=ALU.not_equal, fill=1.0, base=0,
                                    pattern=[[-1, P]], channel_multiplier=1).then_inc(ident_ready, 1)

            def split_lo(n, u):
                pool.wait_ge(x_hi_ready, n + 1)
                wait(pool, proj_ready, 3 * (n - 1))
                nc.gpsimd.tensor_tensor(x_lo[u][:], xT[:], x_hi[u][:].bitcast(F32), ALU.subtract).then_inc(x_lo_ready, 1)

            def apply_gain(n):
                pool.wait_ge(qk_scaled, n + 1)
                gain = qk_gain[:].rearrange("p g (o d) -> p g o d", o=1).broadcast_to([P, 2, H, HD])
                nc.gpsimd.tensor_tensor(qk_n[:].rearrange("p g (h d) -> p g h d", h=H),
                                        qk[:].rearrange("p g (h d) -> p g h d", h=H), gain,
                                        ALU.mult).then_inc(qk_normed, 1)

            pool.wait_ge(consts_loaded, 64)
            split_lo(0, 0)
            split_lo(1, 1)
            apply_gain(0)

            def step(t, u):
                apply_gain(t + 1)
                if not t_known(t) or t < TILES - 1:
                    split_lo(t + 2, u)

            prompt_steps(pool, step)

        @block.scalar
        def _(act):
            act.preload_act_table_set(ACT_TABLES)

            def norm_stats(n, u):
                act.wait_ge(x_loaded[u], half_count(n, u))
                wait(act, xT_ready, 2 * n)
                wait(act, x_lo_ready, n)
                wait(act, xT_stored, 16 * n)
                nc.scalar.activation(xT[:].rearrange("p k n -> p (k n)"), x_tok[u][:], ACT.Square,
                                     accum_out=sumsq).then_inc(x_sumsq, 1)
                act.wait_ge(x_sumsq, n + 1)
                act.wait_ge(eps_ready, 1)
                nc.scalar.activation(logms, sumsq, ACT.Ln, scale=1.0 / D, bias=eps).then_inc(x_logms, 1)
                act.wait_ge(x_logms, n + 1)
                wait(act, x_scaled, n)
                nc.scalar.activation(rstd, logms, ACT.Exp, scale=-0.5).then_inc(x_rstd, 1)

            def split_hi(n, u):
                act.wait_ge(xT_ready, 2 * n + 2)
                wait(act, proj_ready, 3 * (n - 1))
                nc.scalar.activation(x_hi[u][:], xT[:], ACT.Copy).then_inc(x_hi_ready, 1)

            def read_qk(n, g):
                act.wait_ge(proj_ready, 3 * n + g + 1)
                wait(act, qk_normed, n)
                nc.scalar.activation(qk[:, g, :], ps_proj[(n + g) % 2 if t_known(n) else g ^ PAR[0]][:], ACT.Copy).then_inc(proj_read, 1)

            def read_v(n, u):
                act.wait_ge(proj_ready, 3 * n + 3)
                wait(act, pv_done, H * (n - 1))
                wait(act, shifted, 2 * (n - 1))
                nc.scalar.activation(v[u][:, SLOTS - 1, :], ps_proj[u][:], ACT.Copy).then_inc(proj_read, 1)

            def square_qk(n):
                act.wait_ge(proj_read, 3 * n + 2)
                wait(act, qk_turned, 2 * n)
                if t_known(n) and n > 12:
                    act.wait_ge(kv_stored, 32 * (n - 12))
                nc.scalar.activation(qk_n[:], qk[:], ACT.Square).then_inc(qk_sq, 1)

            def qk_stats(n):
                act.wait_ge(qk_summed, n + 1)
                nc.scalar.activation(qk_rstd, qk_ss, ACT.Ln, scale=1.0 / HD, bias=eps).then_inc(qk_logms, 1)
                act.wait_ge(qk_logms, n + 1)
                nc.scalar.activation(qk_rstd, qk_rstd, ACT.Exp, scale=-0.5).then_inc(qk_rstd_ready, 1)

            def read_qT(n):
                act.wait_ge(qk_turned, 2 * n + 1)
                wait(act, score_ready, H * n)
                nc.scalar.activation(qT[:], ps_turn[:].rearrange("p (g n) -> p g n", g=PAIRS), ACT.Copy).then_inc(qkT_ready, 1)

            def read_kT(n, u):
                act.wait_ge(qk_turned, 2 * n + 2)
                wait(act, shifted, 2 * (n - 1))
                nc.scalar.activation(kT[u][:, :, FAR + P:WIN], ps_turn[:].rearrange("p (g n) -> p g n", g=PAIRS),
                                     ACT.Copy).then_inc(qkT_ready, 1)

            def exps(t, h, lo):
                act.wait_ge(max_ready, H * t + h + 1)
                if h == 0:
                    wait(act, inv_ready, t)
                nc.scalar.activation(probs[h % 2][:, lo * P:WIN], probs[h % 2][:, lo * P:WIN], ACT.Exp,
                                     bias=neg_max[h % 2], accum_out=row_sum[:, h:h + 1]).then_inc(p_ready, 1)

            def read_pT(t, h, lo):
                act.wait_ge(p_turned, H * t + h + 1)
                wait(act, pv_done, H * t + h - 1)
                nc.scalar.activation(pT[h % 2][:, lo * P:WIN], ps_score[h % 2][:, lo * P:WIN], ACT.Copy).then_inc(pT_ready, 1)

            norm_stats(0, 0)
            split_hi(0, 0)
            norm_stats(1, 1)
            split_hi(1, 1)
            for b in range(WB):
                act.wait_ge(w_loaded[b % 2], 16 * (b // 2 + 1))
                nc.scalar.activation(w_hi[:, :, b * P:(b + 1) * P], w_raw[b % 2][:], ACT.Copy).then_inc(w_hi_ready, 1)
            PAR[0] = 0
            read_qk(0, 0)
            read_qk(0, 1)
            square_qk(0)
            qk_stats(0)
            read_v(0, 0)
            read_qT(0)
            read_kT(0, 0)

            def step(t, u):
                PAR[0] = 1 - u
                lo = first_slot(t)
                more = not t_known(t) or t < TILES - 1
                for h in range(H):
                    if h >= 1:
                        read_pT(t, h - 1, lo)
                    exps(t, h, lo)
                    if h == 2:
                        read_qk(t + 1, 0)
                        if more:
                            norm_stats(t + 2, u)
                    if h == 4:
                        read_qk(t + 1, 1)
                        square_qk(t + 1)
                    if h == 5:
                        qk_stats(t + 1)
                    if h == 6 and more:
                        split_hi(t + 2, u)
                read_v(t + 1, 1 - u)
                read_qT(t + 1)
                read_pT(t, H - 1, lo)
                read_kT(t + 1, 1 - u)

            prompt_steps(act, step)

        @block.vector
        def _(dve):
            def norm_x(n, u):
                dve.wait_ge(x_rstd, n + 1)
                nc.vector.tensor_scalar(x_tok[u][:], x_tok[u][:], rstd, None, ALU.mult).then_inc(x_scaled, 1)

            def read_xT(n, j):
                dve.wait_ge(x_turned, 2 * n + j + 1)
                gain = gainT[:, 4 * j:4 * j + 4].rearrange("p (k o) -> p k o", o=1).broadcast_to([P, 4, P])
                nc.vector.tensor_tensor(xT[:, 4 * j:4 * j + 4, :], ps_turn[:].rearrange("p (k n) -> p k n", k=4),
                                        gain, ALU.mult).then_inc(xT_ready, 1)

            def sum_qk(n):
                dve.wait_ge(qk_sq, n + 1)
                nc.vector.tensor_reduce(qk_ss, qk_n[:].rearrange("p g (h d) -> p (g h) d", h=H), AX_X,
                                        ALU.add).then_inc(qk_summed, 1)

            def scale_qk(n):
                dve.wait_ge(qk_rstd_ready, n + 1)
                r = qk_rstd.rearrange("p (g o) -> p g o", o=1).broadcast_to([P, 2 * H, HD])
                x = qk[:].rearrange("p g (h d) -> p (g h) d", h=H)
                nc.vector.tensor_tensor(x, x, r, ALU.mult).then_inc(qk_scaled, 1)

            def bias_and_max(t, h, lo):
                dve.wait_ge(score_ready, H * t + h + 1)
                wait(dve, p_turned, H * t + h - 1)
                s, out = ps_score[h % 2], probs[h % 2]
                if lo * P < FAR:
                    nc.vector.scalar_tensor_tensor(out=out[:, lo * P:FAR], in0=s[:, lo * P:FAR], scalar=SCALE,
                                                   in1=far_mask[:, lo * P:FAR], op0=ALU.mult, op1=ALU.add)
                near = max(lo * P, FAR)
                nc.vector.scalar_tensor_tensor(out=out[:, near:WIN], in0=s[:, near:WIN], scalar=SCALE,
                                               in1=near_bias[:, h, near - FAR:NEAR], op0=ALU.mult,
                                               op1=ALU.add).then_inc(biased, 1)
                dve.wait_ge(biased, H * t + h + 1)
                nc.vector.tensor_reduce(neg_max[h % 2], out[:, lo * P:WIN], AX_X, ALU.max,
                                        negate=True).then_inc(max_ready, 1)

            def shift_window(n, u):
                lo = first_slot(n)
                dve.wait_ge(qkT_ready, 2 * n)
                wait(dve, score_ready, H * (n - 1))
                wait(dve, shifted, 2 * (n - 1))
                nc.vector.tensor_copy(kT[u][:, :, lo * P:FAR + P], kT[1 - u][:, :, (lo + 1) * P:WIN]).then_inc(shifted, 1)
                dve.wait_ge(proj_read, 3 * n)
                wait(dve, pv_done, H * (n - 1))
                nc.vector.tensor_copy(v[u][:, lo:SLOTS - 1, :], v[1 - u][:, lo + 1:SLOTS, :]).then_inc(shifted, 1)

            nc.vector.memset(eps, EPS).then_inc(eps_ready, 1)
            dve.wait_ge(consts_loaded, 64)
            last = tab[:, 2 * MAXREL:2 * MAXREL + 1]
            nc.vector.tensor_copy(rev[:, 0:P], last.broadcast_to([H, P])).then_inc(rev_ready, 1)
            nc.vector.tensor_copy(rev[:, P:3 * P], tab[:, 0:2 * MAXREL][:, ::-1]).then_inc(rev_ready, 1)
            nc.vector.memset(far_mask[:], 0.0).then_inc(rev_zero, 1)
            dve.wait_ge(rev_zero, 1)
            nc.vector.memset(far_mask[CH:P, 0:CH], MASKED).then_inc(bias_near, 1)
            norm_x(0, 0)
            read_xT(0, 0)
            read_xT(0, 1)
            norm_x(1, 1)
            wait(dve, x_lo_ready, 1)
            wait(dve, xT_stored, 16)
            read_xT(1, 0)
            read_xT(1, 1)
            dve.wait_ge(bias_loaded, 16 * (H + 1))
            far = far_value[:].rearrange("p (h o) -> p h o", o=1).broadcast_to([P, H, NEAR])
            nc.vector.tensor_tensor(near_bias[:], near_bias[:], far, ALU.subtract).then_inc(bias_near, 1)
            dve.wait_ge(bias_near, 2)
            nc.vector.memset(near_bias[0:CH, :, NEAR - CH:NEAR], MASKED).then_inc(bias_ready, 1)
            for b in range(WB):
                dve.wait_ge(w_hi_ready, b + 1)
                nc.vector.tensor_tensor(w_lo[:, :, b * P:(b + 1) * P], w_raw[b % 2][:],
                                        w_hi[:, :, b * P:(b + 1) * P].bitcast(F32), ALU.subtract).then_inc(w_lo_ready, 1)
            sum_qk(0)
            scale_qk(0)
            dve.wait_ge(bias_ready, 1)

            def step(t, u):
                lo = first_slot(t)
                more = not t_known(t) or t < TILES - 1
                for h in range(H):
                    bias_and_max(t, h, lo)
                    if h == 1 and more:
                        shift_window(t + 1, 1 - u)
                    if h == 3 and more:
                        norm_x(t + 2, u)
                    if more and h in (4, 5):
                        read_xT(t + 2, h - 4)
                    if h == 5:
                        sum_qk(t + 1)
                    if h == 6:
                        scale_qk(t + 1)
                dve.wait_ge(p_ready, H * (t + 1))
                nc.vector.reciprocal(row_inv, row_sum).then_inc(inv_ready, 1)
                dve.wait_ge(inv_ready, t + 1)
                dve.wait_ge(pv_done, H * (t + 1))
                wait(dve, out_stored, 16 * t)
                inv = row_inv.rearrange("p (h o) -> p h o", o=1).broadcast_to([P, H, HD])
                nc.vector.tensor_tensor(o_tok[:], ps_out[:].rearrange("p (h d) -> p h d", h=H), inv,
                                        ALU.mult).then_inc(out_ready, 1)

            prompt_steps(dve, step)

        @block.tensor
        def _(pe):
            def turn_x(n, u, j):
                pe.wait_ge(x_scaled, n + 1)
                if j == 0:
                    wait(pe, qkT_ready, 2 * (n - 1))
                wait(pe, xT_ready, 2 * n + j)
                for k in range(4):
                    last = nc.tensor.transpose(ps_turn[:, k * P:(k + 1) * P],
                                               x_tok[u][:, (4 * j + k) * P:(4 * j + k + 1) * P], ident[:])
                last.then_inc(x_turned, 1)

            def projection(n, u):
                for g in range(3):
                    out = ps_proj[(u + g) % 2]
                    for k in range(KT):
                        for i, (a, w) in enumerate(((x_hi, w_hi), (x_hi, w_lo), (x_lo, w_hi))):
                            if k == 0 and i == 0:
                                if g == 0:
                                    pe.wait_ge(x_hi_ready, n + 1)
                                    pe.wait_ge(x_lo_ready, n + 1)
                                wait(pe, proj_read, 3 * n + g - 1)
                                if t_known(n) and n == 0:
                                    pe.wait_ge(w_lo_ready, 4 * (g + 1))
                            mm = nc.tensor.matmul(out[:], a[u][:, k, :], w[:, k, g * AW:(g + 1) * AW],
                                                  start=(k == 0 and i == 0), stop=(k == KT - 1 and i == 2))
                            if k == KT - 1 and i == 2:
                                mm.then_inc(proj_ready, 1)
                            yield

            def turn_qk(n, g):
                if g == 0:
                    pe.wait_ge(qk_normed, n + 1)
                    pe.wait_ge(xT_ready, 2 * (DEC + 1) if t_known(n) and n == DEC else 2 * n + 4)
                wait(pe, qkT_ready, 2 * n + g)
                for c in range(PAIRS):
                    last = nc.tensor.transpose(ps_turn[:, c * P:(c + 1) * P], qk_n[:, g, c * P:(c + 1) * P], ident[:])
                last.then_inc(qk_turned, 1)

            def scores(t, u, h, lo):
                c, o = h // 2, HD * (h % 2)
                if h == 0:
                    pe.wait_ge(qkT_ready, 2 * t + 2)
                    wait(pe, shifted, 2 * t - 1)
                wait(pe, pT_ready, H * t + h - 1)
                for a, b in ((lo * P, 512), (512, WIN)):
                    if a < b:
                        mm = nc.tensor.matmul(ps_score[h % 2][:, a:b], qT[o:o + HD, c, :], kT[u][o:o + HD, c, a:b],
                                              start=True, stop=True)
                mm.then_inc(score_ready, 1)

            def turn_probs(t, h, lo):
                pe.wait_ge(p_ready, H * t + h + 1)
                for s in range(lo, SLOTS):
                    last = nc.tensor.transpose(ps_score[h % 2][:, s * P:(s + 1) * P], probs[h % 2][:, s * P:(s + 1) * P],
                                               ident[:])
                last.then_inc(p_turned, 1)

            def weigh_values(t, u, h, lo):
                pe.wait_ge(pT_ready, H * t + h + 1)
                if h == 0:
                    wait(pe, out_ready, t)
                    wait(pe, shifted, 2 * t)
                    pe.wait_ge(proj_read, 3 * (t + 1))
                for s in range(lo, SLOTS):
                    mm = nc.tensor.matmul(ps_out[:, h * HD:(h + 1) * HD], pT[h % 2][:, s * P:(s + 1) * P],
                                          v[u][:, s, h * HD:(h + 1) * HD], start=(s == lo), stop=(s == SLOTS - 1))
                mm.then_inc(pv_done, 1)

            pe.wait_ge(ident_ready, 1)
            for n in (0, 1):
                turn_x(n, n, 0)
                turn_x(n, n, 1)
            for _ in projection(0, 0):
                pass
            turn_qk(0, 0)
            turn_qk(0, 1)

            def step(t, u):
                lo = first_slot(t)
                more = not t_known(t) or t < TILES - 1
                ahead = projection(t + 1, 1 - u)

                def fill(n):
                    for _ in range(n):
                        next(ahead, None)

                for h in range(H):
                    scores(t, u, h, lo)
                    fill(4 if h < 4 else 2)
                    if h >= 1:
                        turn_probs(t, h - 1, lo)
                    fill(4 if h < 4 else 2)
                    if h >= 1:
                        weigh_values(t, u, h - 1, lo)
                    fill(4 if h < 4 else 2)
                    if more and h in (4, 5):
                        turn_x(t + 2, u, h - 4)
                turn_qk(t + 1, 0)
                turn_probs(t, H - 1, lo)
                turn_qk(t + 1, 1)
                weigh_values(t, u, H - 1, lo)

            prompt_steps(pe, step)


def cached_attention_phase(nc, io):
    with ExitStack() as ctx:
        def sb(name, shape, dt=F32):
            return ctx.enter_context(nc.sbuf_tensor(name, shape, dt))

        held = []

        def sem(name):
            held.append(ctx.enter_context(nc.semaphore(name)))
            return held[-1]

        DK = PAST // P
        DW = PAST + P
        BW = DW + P - SL
        G2 = 2 * SL
        k_c = [sb(f"c_k{i}", [P, DK, AW]) for i in range(4)]
        v_c = [sb(f"c_v{i}", [P, DK, AW]) for i in range(4)]
        kcT = [sb(f"c_kT{i}", [P, DK, PAIRS, P]) for i in range(2)]
        q_blocks = [sb(f"c_q{i}", [P, PAIRS, 2, SL]) for i in range(2)]
        qT, knT, v_n = sb("c_qT", [P, PAIRS, P]), sb("c_knT", [P, PAIRS, P]), sb("c_vn", [P, AW])
        bias = sb("c_bias", [P, BW])
        probs = [sb(f"c_probs{i}", [P, DW]) for i in range(2)]
        pT = [sb(f"c_pT{i}", [P, DK + 1, P]) for i in range(2)]
        oT, o_tok = sb("c_oT", [P, PAIRS, P]), sb("c_o", [P, AW])
        ident = sb("c_ident", [P, P])
        small = sb("c_small", [P, 8])
        ps_k = ctx.enter_context(nc.psum_tensor("c_ps_k", [P, DK * AW], F32))
        ps_s = [ctx.enter_context(nc.psum_tensor(f"c_ps_s{i}", [P, 512], F32)) for i in range(2)]
        ps_p = [ctx.enter_context(nc.psum_tensor(f"c_ps_p{i}", [P, 512], F32)) for i in range(2)]
        ps_o = [ctx.enter_context(nc.psum_tensor(f"c_ps_o{i}", [P, 512], F32)) for i in range(2)]

        new_loaded, bias_loaded, kv_stored = sem("c_new_loaded"), sem("c_bias_loaded"), sem("c_kv_stored")
        kv_loaded = [sem(f"c_kv_loaded{i}") for i in range(4)]
        ident_zero, ident_ready, bias_masked, q_zero = sem("c_ident_zero"), sem("c_ident_ready"), sem("c_bias_masked"), sem("c_q_zero")
        q_ready, k_turned, kcT_ready = sem("c_q_ready"), sem("c_k_turned"), sem("c_kcT_ready")
        score_ready, biased, max_ready, p_exp = sem("c_score_ready"), sem("c_biased"), sem("c_max_ready"), sem("c_p_exp")
        inv_ready, p_ready, p_turned, pT_ready = sem("c_inv_ready"), sem("c_p_ready"), sem("c_p_turned"), sem("c_pT_ready")
        pv_done, oT_ready, o_turned, o_ready, o_stored = sem("c_pv_done"), sem("c_oT_ready"), sem("c_o_turned"), sem("c_o_ready"), sem("c_o_stored")

        ctx.callback(clear_semaphores, nc, held)
        block = ctx.enter_context(nc.Block())

        def streams(eng, first, second):
            def two_pairs(b):
                for q in range(2):
                    for half in (first, second):
                        for u in range(2):
                            half(b + (2 * q + u), u, 2 * q + u)

            two_pairs(0)
            with eng.Fori(1, NS // 4) as i:
                two_pairs(i * 4)

        @block.sync
        def _(sp):
            sp.dma_start(qT[:], io["qT_new"]).then_inc(new_loaded, 16)
            sp.dma_start(knT[:], io["kT_new"]).then_inc(new_loaded, 16)
            sp.dma_start(v_n[:], io["v_new"]).then_inc(new_loaded, 16)
            rev = io["rev_table"].tensor

            def load(b, i):
                wait(sp, pv_done, b - 3)
                for s in range(DK):
                    for buf, cache in ((k_c, "cache_attn_k"), (v_c, "cache_attn_v")):
                        src = io[cache][0, bass.ds(b, 1), :, s * P:(s + 1) * P, :].rearrange("o h s d -> s (o h) d")
                        sp.dma_start(buf[i][:, s, :].rearrange("p (h d) -> p h d", h=H), src).then_inc(kv_loaded[i], 16)

            load(0, 0)
            sp.wait_ge(bias_masked, 1)
            for lo, hi, at, back in ((0, P, 0, 0), (P, PAST, P - 1, 1), (DW - SL, DW, PAST - 1, 1)):
                src = bass.AP(rev, at, [[P * 3 * P, H], [(3 * P - 1) * back, SL], [1, hi - lo]])
                sp.dma_start(bias[:, lo:hi], src).then_inc(bias_loaded, 16)
            for i in range(1, 4):
                load(i, i)
            with sp.Fori(1, NS // 4) as i:
                for k in range(4):
                    load(i * 4 + k, k)
            for src, dst in (("k_new", "k_sample_new"), ("v_new", "v_sample_new")):
                for b in range(NS):
                    sp.dma_start(io[dst][0, b].rearrange("h s d -> s h d"),
                                 io[src][b * SL:(b + 1) * SL].rearrange("s (h d) -> s h d", h=H)).then_inc(kv_stored, 16)
            sp.wait_ge(o_ready, 1)
            sp.dma_start(io["o_att"][DEC * P:(DEC + 1) * P, :], o_tok[:]).then_inc(o_stored, 16)
            sp.wait_ge(o_stored, 16)
            sp.wait_ge(kv_stored, 16 * 2 * NS)

        @block.gpsimd
        def _(pool):
            nc.gpsimd.memset(bias[:], MASKED).then_inc(bias_masked, 1)
            nc.gpsimd.memset(q_blocks[0][:], 0.0).then_inc(q_zero, 1)
            nc.gpsimd.memset(q_blocks[1][:], 0.0).then_inc(q_zero, 1)
            nc.gpsimd.memset(ident[:], 0.0).then_inc(ident_zero, 1)
            pool.wait_ge(ident_zero, 1)
            nc.gpsimd.affine_select(out=ident[:], in_=ident[:], compare_op=ALU.not_equal, fill=1.0, base=0,
                                    pattern=[[-1, P]], channel_multiplier=1).then_inc(ident_ready, 1)

        @block.scalar
        def _(act):
            act.preload_act_table_set(ACT_TABLES)

            def keys_and_exp(b, u, i4):
                act.wait_ge(k_turned, b + 1)
                wait(act, score_ready, b - u)
                nc.scalar.activation(kcT[u][:], ps_k[:].rearrange("p (s c n) -> p s c n", s=DK, c=PAIRS),
                                     ACT.Copy).then_inc(kcT_ready, 1)
                act.wait_ge(max_ready, b + 1)
                nc.scalar.activation(probs[u][:], probs[u][:], ACT.Exp, bias=small[:, u:u + 1],
                                     accum_out=small[:, 2 + u:3 + u]).then_inc(p_exp, 1)

            def read_pT(b, u, i4):
                act.wait_ge(p_turned, b + 1)
                wait(act, pv_done, b - u)
                nc.scalar.activation(pT[u][:], ps_p[u][:, 0:DW].rearrange("p (s n) -> p s n", n=P),
                                     ACT.Copy).then_inc(pT_ready, 1)

            streams(act, keys_and_exp, read_pT)
            act.wait_ge(o_turned, 1)
            nc.scalar.activation(o_tok[:], ps_p[0][:], ACT.Copy).then_inc(o_ready, 1)

        @block.vector
        def _(dve):
            dve.wait_ge(new_loaded, 48)
            dve.wait_ge(q_zero, 2)
            dve.wait_ge(bias_loaded, 16 * 3)

            def queries_and_max(b, u, i4):
                wait(dve, score_ready, b - u)
                for i in range(2):
                    nc.vector.tensor_copy(q_blocks[u][i * HD:(i + 1) * HD, :, i, :],
                                          qT[i * HD:(i + 1) * HD, :, bass.ds(b * SL, SL)]).then_inc(q_ready, 1)
                dve.wait_ge(score_ready, b + 1)
                wait(dve, p_turned, b - u)
                nc.vector.scalar_tensor_tensor(out=probs[u][:, 0:PAST], in0=ps_s[u][:, 0:PAST], scalar=SCALE,
                                               in1=bias[:, 0:PAST], op0=ALU.mult, op1=ALU.add)
                nc.vector.scalar_tensor_tensor(out=probs[u][:, PAST:DW], in0=ps_s[u][:, PAST:DW], scalar=SCALE,
                                               in1=bias[:, bass.ds(DW - SL - b * SL, P)], op0=ALU.mult,
                                               op1=ALU.add).then_inc(biased, 1)
                dve.wait_ge(biased, b + 1)
                nc.vector.tensor_reduce(small[:, u:u + 1], probs[u][:], AX_X, ALU.max, negate=True).then_inc(max_ready, 1)

            def normalise_and_keep(b, u, i4):
                dve.wait_ge(p_exp, b + 1)
                nc.vector.reciprocal(small[:, 4 + u:5 + u], small[:, 2 + u:3 + u]).then_inc(inv_ready, 1)
                dve.wait_ge(inv_ready, b + 1)
                nc.vector.tensor_scalar(probs[u][:], probs[u][:], small[:, 4 + u:5 + u], None, ALU.mult).then_inc(p_ready, 1)
                dve.wait_ge(pv_done, b + 1)
                for i in range(2):
                    half = slice(i * HD, (i + 1) * HD)
                    src = ps_o[u][half, 0:P].rearrange("p (c i q) -> p c i q", c=PAIRS, i=2)[:, :, i, :]
                    nc.vector.tensor_copy(oT[half, :, bass.ds(b * SL, SL)], src).then_inc(oT_ready, 1)

            streams(dve, queries_and_max, normalise_and_keep)

        @block.tensor
        def _(pe):
            pe.wait_ge(ident_ready, 1)
            pe.wait_ge(new_loaded, 48)

            def turn_and_score(b, u, i4):
                pe.wait_ge(kv_loaded[i4], 16 * b + (64 - 16 * i4))
                wait(pe, kcT_ready, b)
                for s in range(DK):
                    for c in range(PAIRS):
                        last = nc.tensor.transpose(ps_k[:, (s * PAIRS + c) * P:(s * PAIRS + c + 1) * P],
                                                   k_c[i4][:, s, c * P:(c + 1) * P], ident[:])
                last.then_inc(k_turned, 1)
                pe.wait_ge(q_ready, 2 * b + 2)
                wait(pe, biased, b - u)
                pe.wait_ge(kcT_ready, b + 1)
                for c in range(PAIRS):
                    lhs = q_blocks[u][:, c, :, :].rearrange("p i q -> p (i q)")
                    nc.tensor.matmul(ps_s[u][c * G2:(c + 1) * G2, 0:PAST], lhs, kcT[u][:, :, c, :], start=True, stop=True)
                    last = nc.tensor.matmul(ps_s[u][c * G2:(c + 1) * G2, PAST:DW], lhs, knT[:, c, :], start=True, stop=True)
                last.then_inc(score_ready, 1)

            def turn_and_weigh(b, u, i4):
                wait(pe, pT_ready, b - u)
                pe.wait_ge(p_ready, b + 1)
                for s in range(DK + 1):
                    last = nc.tensor.transpose(ps_p[u][:, s * P:(s + 1) * P], probs[u][:, s * P:(s + 1) * P], ident[:])
                last.then_inc(p_turned, 1)
                wait(pe, oT_ready, 2 * (b - u))
                pe.wait_ge(pT_ready, b + 1)
                for c in range(PAIRS):
                    cols = slice(c * P, (c + 1) * P)
                    for s in range(DK + 1):
                        vs = v_c[i4][:, s, cols] if s < DK else v_n[:, cols]
                        last = nc.tensor.matmul(ps_o[u][:, c * G2:(c + 1) * G2], vs, pT[u][:, s, c * G2:(c + 1) * G2],
                                                start=(s == 0), stop=(s == DK))
                last.then_inc(pv_done, 1)

            streams(pe, turn_and_score, turn_and_weigh)
            pe.wait_ge(oT_ready, 2 * NS)
            pe.wait_ge(pT_ready, NS)
            for c in range(PAIRS):
                last = nc.tensor.transpose(ps_p[0][:, c * P:(c + 1) * P], oT[:, c, :], ident[:])
            last.then_inc(o_turned, 1)


def shape_constants():
    import numpy as np

    p = np.arange(P)[:, None]
    c = np.arange(P)[None, :]
    out = {"ident": p == c, "head_ones": p // HD == c // HD, "head_of": p // HD == np.arange(2)[None, :],
           "stream_of": p // SL == np.arange(NS)[None, :]}
    for mode, size in (("p", CH), ("s", SL)):
        same = p // size == c // size
        out[f"lower_{mode}"] = same & (p > c)
        out[f"upper_{mode}"] = np.concatenate([same & (p < c), same & (p <= c)], 1)
        out[f"run_{mode}"] = np.broadcast_to(np.arange(PAIRS * P)[None, :] % size != 0, (P, PAIRS * P))
    out["levels"] = np.concatenate([(p // w == c // w) & (p % w < w // 2) & (c % w >= w // 2)
                                    for w in (2 ** (i + 1) for i in range(CH.bit_length() - 1))], 1)
    return {k: np.ascontiguousarray(v, np.float32) for k, v in out.items()}


CONST_AT, CONST_W = {}, 0
for _name, _v in shape_constants().items():
    CONST_AT[_name] = (CONST_W, _v.shape[1])
    CONST_W += _v.shape[1]


SHIFT_TILES = SHIFT_COLS // P
GT = 4


def rwkv_projection_phase(nc, io):
    with ExitStack() as ctx:
        def sb(name, shape, dt=F32):
            return ctx.enter_context(nc.sbuf_tensor("j_" + name, shape, dt))

        held = []

        def sem(name):
            held.append(ctx.enter_context(nc.semaphore("j_" + name)))
            return held[-1]

        w_hi, w_lo = sb("w_hi", [P, KT, SHIFT_COLS], F32R), sb("w_lo", [P, KT, SHIFT_COLS], F32R)
        w_raw = [sb(f"w_raw{i}", [P, KT, P]) for i in range(2)]
        xT = sb("xT", [P, GT, KT, P])
        x_hi, x_lo = sb("x_hi", [P, KT, GT, P], F32R), sb("x_lo", [P, KT, GT, P], F32R)
        out = [sb(f"out{i}", [P, GT * P]) for i in range(2)]
        ps = [ctx.enter_context(nc.psum_tensor(f"j_ps{i}", [P, GT * P], F32)) for i in range(2)]

        w_loaded = [sem(f"w_loaded{i}") for i in range(2)]
        w_hi_ready, w_lo_ready = sem("w_hi_ready"), sem("w_lo_ready")
        x_loaded, x_hi_ready, x_lo_ready, x_used = sem("x_loaded"), sem("x_hi_ready"), sem("x_lo_ready"), sem("x_used")
        projected, copied, stored = ([sem(f"{n}{i}") for i in range(2)] for n in ("projected", "copied", "stored"))

        w_in = io["w_in"][0].rearrange("(k p) n -> p k n", p=P)
        COL0 = 4 * AW
        GROUPS = TILES // GT
        OF = (SHIFT_TILES - SHIFT_TILES // 2, SHIFT_TILES // 2)
        ctx.callback(clear_semaphores, nc, held)
        block = ctx.enter_context(nc.Block())

        def groups(eng, step):
            step(0, GT)
            with eng.Fori(1, GROUPS) as g:
                step(g, GT)
            step(GROUPS, 1)

        def blocks(g):
            for c in range(SHIFT_TILES):
                yield c, c % 2, g * OF[c % 2] + c // 2

        @block.sync
        def _(sp):
            def load_w(b):
                sp.dma_start(w_raw[b % 2][:], w_in[:, :, COL0 + b * P:COL0 + (b + 1) * P]).then_inc(w_loaded[b % 2], 16)

            def load_x(g, n):
                src = io["xT"][bass.ds(g * GT, n)].rearrange("a p k n -> p a (k n)")
                sp.dma_start(xT[:, 0:n].rearrange("p a k n -> p a (k n)"), src).then_inc(x_loaded, 16)

            load_w(0)
            load_x(0, GT)
            load_w(1)

            def step(g, n):
                if not (t_known(g) and g == GROUPS):
                    sp.wait_ge(x_lo_ready, KT * (g + 1))
                    load_x(g + 1, GT) if not (t_known(g) and g == GROUPS - 1) else load_x(GROUPS, 1)
                for c, j, i in blocks(g):
                    if t_known(g) and g == 0 and c + 2 < SHIFT_TILES:
                        sp.wait_ge(w_lo_ready, c + 1)
                        load_w(c + 2)
                    sp.wait_ge(copied[j], i + 1)
                    sp.dma_start(io["proj_T"][c, :, bass.ds(1 + g * (GT * P), n * P)], out[j][:, 0:n * P]).then_inc(stored[j], 16)

            step(0, GT)
            with sp.Fori(1, GROUPS - 1) as g:
                step(g, GT)
            step(GROUPS - 1, GT)
            step(GROUPS, 1)
            for j in range(2):
                sp.wait_ge(stored[j], 16 * OF[j] * (GROUPS + 1))

        @block.scalar
        def _(act):
            def split(g, n):
                act.wait_ge(x_loaded, 16 * (g + 1))
                for k in range(KT):
                    if not (t_known(g) and g == 0):
                        if k < KT - 1:
                            act.wait_ge(x_used, (KT - 1) * (g - 1) + k + 1)
                        else:
                            act.wait_ge(projected[(SHIFT_TILES - 1) % 2], OF[0] * g)
                    nc.scalar.activation(x_hi[:, k, 0:n, :], xT[:, 0:n, k, :], ACT.Copy).then_inc(x_hi_ready, 1)

            act.wait_ge(w_loaded[0], 16)
            nc.scalar.activation(w_hi[:, :, 0:P], w_raw[0][:], ACT.Copy).then_inc(w_hi_ready, 1)
            split(0, GT)
            for b in range(1, SHIFT_TILES):
                act.wait_ge(w_loaded[b % 2], 16 * (b // 2 + 1))
                nc.scalar.activation(w_hi[:, :, b * P:(b + 1) * P], w_raw[b % 2][:], ACT.Copy).then_inc(w_hi_ready, 1)
            with act.Fori(1, GROUPS) as g:
                split(g, GT)
            split(GROUPS, 1)

        @block.vector
        def _(dve):
            def split_w(b):
                dve.wait_ge(w_hi_ready, b + 1)
                nc.vector.tensor_tensor(w_lo[:, :, b * P:(b + 1) * P], w_raw[b % 2][:],
                                        w_hi[:, :, b * P:(b + 1) * P].bitcast(F32), ALU.subtract).then_inc(w_lo_ready, 1)

            def split(g, n):
                for k in range(KT):
                    dve.wait_ge(x_hi_ready, KT * g + k + 1)
                    nc.vector.tensor_tensor(x_lo[:, k, 0:n, :], xT[:, 0:n, k, :], x_hi[:, k, 0:n, :].bitcast(F32),
                                            ALU.subtract).then_inc(x_lo_ready, 1)

            split_w(0)

            def step(g, n):
                split(g, n)
                for c, j, i in blocks(g):
                    if t_known(g) and g == 0 and c + 1 < SHIFT_TILES:
                        split_w(c + 1)
                    dve.wait_ge(projected[j], i + 1)
                    wait(dve, stored[j], 16 * i)
                    nc.vector.tensor_copy(out[j][:, 0:n * P], ps[j][:, 0:n * P]).then_inc(copied[j], 1)

            groups(dve, step)

        @block.tensor
        def _(pe):
            def step(g, n):
                for c, j, i in blocks(g):
                    wait(pe, copied[j], i)
                    if t_known(g) and g == 0:
                        pe.wait_ge(w_lo_ready, c + 1)
                    cols = slice(c * P, (c + 1) * P)
                    for k in range(KT):
                        if c == 0:
                            pe.wait_ge(x_lo_ready, KT * g + k + 1)
                        for m, (w, x) in enumerate(((w_hi, x_hi), (w_lo, x_hi), (w_hi, x_lo))):
                            mm = nc.tensor.matmul(ps[j][:, 0:n * P], w[:, k, cols], x[:, k, 0:n, :].rearrange("p a n -> p (a n)"),
                                                  start=(k == 0 and m == 0), stop=(k == KT - 1 and m == 2))
                        if c == SHIFT_TILES - 1:
                            mm.then_inc(x_used if k < KT - 1 else projected[j], 1)
                    if c < SHIFT_TILES - 1:
                        mm.then_inc(projected[j], 1)

            groups(pe, step)


def merged(*runs):
    at = [next(r, None) for r in runs]
    while any(a is not None for a in at):
        i = min((a, i) for i, a in enumerate(at) if a is not None)[1]
        at[i] = next(runs[i], None)


def rwkv_phase(nc, io):
    with ExitStack() as ctx:
        def sb(name, shape, dt=F32):
            return ctx.enter_context(nc.sbuf_tensor("r_" + name, shape, dt))

        held = []

        def sem(name):
            held.append(ctx.enter_context(nc.semaphore("r_" + name)))
            return held[-1]

        def sb2(name, shape):
            return [sb(f"{name}{i}", shape) for i in range(2)]

        def sems2(name):
            return [sem(f"{name}{i}") for i in range(2)]

        CT = SHIFT_TILES
        PW = PAIRS * P
        KAPPA = 0.6065306597126334
        GN_EPS = 64e-5
        LN_UP = 65536.0
        NCH = P // CH
        consts = sb("consts", [P, CONST_W])
        per_ch = sb("per_ch", [P, CT + 6 * PAIRS])
        lora_w = sb("lora_w", [P, AW])
        gn = sb("gn", [P, 2, AW])
        cur = sb2("cur", [P, CT, NS * (SL + 1)])
        xs = sb("xs", [P, CT, P])
        th = sb("tanh", [HD, P])
        sig, acc, inv_g, a_gate = (sb(n, [P, PW]) for n in ("sig", "acc", "inv_g", "a_gate"))
        g_run = sb("g_run", [P, PAIRS, NS * (SL + 1)])
        kk, kk_sq, kk_n, fac, kmod, bmul, rk = (sb(n, [P, PW]) for n in ("kk", "kk_sq", "kk_n", "fac", "kmod", "bmul", "rk"))
        bt, kt = sb("bt", [P, PW]), sb("kt", [P, PW])
        ar = sb2("ar", [P, PAIRS, 2, 2, P])
        g_last = sb2("g_last", [P, PAIRS, NS])
        v_tok, k_tok, b_tok = sb2("v_tok", [P, AW]), sb2("k_tok", [P, AW]), sb2("b_tok", [P, AW])
        a_mat = sb2("a_mat", [P, 2, PAIRS, P])
        ak_T = sb2("ak_T", [P, PAIRS, 2, 2, P])
        rb_T = sb2("rb_T", [P, PAIRS, 2, P])
        bonus = sb2("bonus", [P, H])
        x_mat = sb("x_mat", [P, 2, PAIRS, P])
        y_mat, q_mat = sb("y_mat", [P, 2, PAIRS, P]), sb("q_mat", [P, 2, PAIRS, P])
        rhs, u_tok = sb("rhs", [P, AW]), sb("u_tok", [P, AW])
        state = sb("state", [P, PAIRS, P])
        states = sb("states", [P, PAIRS, NS, HD])
        shift_T = sb("shift_T", [P, CT, NS])
        gate_w = sb("gate_w", [P, KT * D])
        gate_x = sb("gate_x", [P, 2 * D])
        gate_out = sb2("gate_out", [P, AW])
        st_nat = gate_w[0:HD, 0:NS * AW].rearrange("v (b n) -> v b n", b=NS)
        st_shift = gate_x[0:NS, 0:SHIFT_COLS]
        y_tok, y_sq = sb("y_tok", [P, AW]), sb("y_sq", [P, AW])
        small = sb("small", [P, 40])
        y_sum, y_mean, y_var, y_rstd = (small[:, 8 * i:8 * i + 8] for i in range(4))
        gn_eps, ln_back = small[:, 32:33], small[:, 33:34]
        late = [gate_w[:, NS * AW + i * AW:NS * AW + (i + 1) * AW] for i in range(6)]
        spread_s, spread_u = ([late[2 * j + i].rearrange("p (b d) -> p b d", b=NS) for i in range(2)] for j in range(2))
        dec_cols = sb("dec_cols", [P, CT, P])
        state_back = acc[:].rearrange("p (c n) -> p c n", c=PAIRS)
        from_state = late[4:6]

        def bank(name):
            return ctx.enter_context(nc.psum_tensor("r_ps_" + name, [P, 512], F32))

        ps_job = [bank("job0"), bank("job1")]
        ps_inv = [bank("inv0"), bank("inv1")]
        ps_rhs, ps_u, ps_y, ps_gate = bank("rhs"), bank("u"), bank("y"), bank("gate")
        ps_s = ps_inv[0]
        ps_turn = [ps_u, ps_u]

        def const(name, mode=None):
            at, n = CONST_AT[name if mode is None else f"{name}_{mode}"]
            return consts[:, at:at + n]

        ident = const("ident")

        def chan(i):
            return per_ch[:, CT + i * PAIRS:CT + (i + 1) * PAIRS]

        DECAY, ICLR, REMOVE, KICLR, BONUS, KICLR_REST = range(6)

        def spread(ap, n):
            return ap.rearrange("p (k o) -> p k o", o=1).broadcast_to([P, ap.shape[1], n])

        def c4(ap):
            return ap.rearrange("p (c n) -> p c n", c=PAIRS)

        def heads(ap):
            return ap.rearrange("p (h d) -> p h d", h=H)

        def head_cols(g, c):
            return slice((2 * c + g) * HD, (2 * c + g + 1) * HD)

        def pair_cols(c):
            return slice(c * P, (c + 1) * P)

        def half(i):
            return slice(i * HD, (i + 1) * HD)

        params_loaded, cur_loaded, states_loaded = sem("params_loaded"), sems2("cur_loaded"), sem("states_loaded")
        gate_w_loaded, gate_x_loaded, gate_written, gate_copied = sem("gate_w_loaded"), sems2("gate_x_loaded"), sem("gate_written"), sem("gate_copied")
        gate_stored = sems2("gate_stored")
        set_up, states_turned, states_read = sem("set_up"), sem("states_turned"), sem("states_read")
        job_written, job_read = sems2("job_written"), sems2("job_read")
        ready = {n: sem(n + "_ready") for n in (
            "delta", "lora_in", "xs", "tanh", "acc", "g_run", "inv_g", "g_last", "kk", "kk_sq", "kk_log", "rnorm", "kk_n",
            "ahat", "rhat", "fac", "kmod", "bmul", "bt", "kt", "rk", "rkr",
            "y_sum", "y_mean", "y_centred", "y_sq", "y_var", "y_log", "y_rstd", "y_scaled", "y_gained", "y_based",
            "v_bonus", "out", "ps_y")}
        turn_written = sems2("turn_written")
        inv_written, q_ready, y_ready, x_ready = sems2("inv_written"), sems2("q_ready"), sems2("y_ready"), sems2("x_ready")
        rhs_written, rhs_ready, u_written, u_ready = sem("rhs_written"), sem("rhs_ready"), sem("u_written"), sem("u_ready")
        s_written, s_added, state_ready, o_stored = sem("s_written"), sem("s_added"), sem("state_ready"), sem("o_stored")
        dec_written, dec_masked, dec_summed = sems2("dec_written"), sems2("dec_masked"), sems2("dec_summed")
        dec_spread_v, dec_spread_u, dec_added, dec_state = sems2("dec_spread_v"), sems2("dec_spread_u"), sems2("dec_added"), sems2("dec_state")
        y_raw_ready, turned_back, nat_ready, stored = sem("y_raw_ready"), sem("turned_back"), sem("nat_ready"), sem("stored")
        state_turned, state_out, dec_copied = sem("state_turned"), sem("state_out"), sem("dec_copied")

        JOBS = ["decay", "iclr", "kk_sum", "v_tok", "k_tok", "b_tok", "A0", "A1", "AK0", "AK1", "AK2", "AK3",
                "RB0", "RB1", "bonus"]
        GRAM_STAGES = dict(zip(JOBS[6:14], (7, 7.5, 8, 9, 10, 11, 12, 13)))
        JOBS_OF = (len(JOBS) - len(JOBS) // 2, len(JOBS) // 2)
        LEVELS = {"p": 6, "s": 4}
        LP = LEVELS["p"]

        def job_count(t, name):
            j = JOBS.index(name)
            return j % 2, JOBS_OF[j % 2] * t + j // 2

        def free_bank(t, name):
            b, n = job_count(t, name)
            wait(nc.tensor, job_read[b], n)
            return ps_job[b], job_written[b]

        def written(eng, t, name):
            b, n = job_count(t, name)
            eng.wait_ge(job_written[b], n + 1)
            return ps_job[b], job_read[b]

        def was_written(eng, t, name):
            b, n = job_count(t, name)
            wait(eng, job_written[b], n + 1 - JOBS_OF[b])

        def was_read(eng, t, name):
            b, n = job_count(t, name)
            eng.wait_ge(job_read[b], n + 1)

        def need(eng, t, *names):
            for n in names:
                eng.wait_ge(ready[n], t + 1)

        def past(eng, t, *names):
            for n in names:
                wait(eng, ready[n], t)

        def nothing(t, u, mode):
            return iter(())

        def tiles(eng, front, back, mix=nothing, tail=nothing, gates=nothing, loop_end=(TILES - 2) // 2):
            def iteration(t, u):
                fixed = t_known(t)
                runs = []
                if not fixed or t > 0:
                    runs.append(tail(t - 1, 1 - u, "p"))
                runs.append(back(t, u, "s" if fixed and t == DEC else "p"))
                if not fixed or t < DEC:
                    runs.append(front(t + 1, 1 - u, "s" if fixed and t + 1 == DEC else "p"))
                    runs.append(gates(t, u, "p"))
                if not fixed or t < DEC - 1:
                    runs.append(mix(t + 2, u, "s" if fixed and t + 2 == DEC else "p"))
                merged(*runs)

            merged(mix(0, 0, "p"))
            merged(front(0, 0, "p"), mix(1, 1, "p"), gates(-1, 1, "s"))
            iteration(0, 0)
            iteration(1, 1)
            with eng.Fori(1, loop_end) as i:
                iteration(i * 2, 0)
                iteration(i * 2 + 1, 1)
            for t in range(2 * loop_end, DEC + 1):
                iteration(t, t % 2)
            merged(tail(DEC, 0, "s"))

        def runs(ap, mode):
            n, size = (NCH, CH) if mode == "p" else (NS, SL)
            return ap[:, :, 0:n * (size + 1)].rearrange("p c (n l) -> p c n l", n=n)

        def by_run(ap, mode):
            return ap.rearrange("p c (n l) -> p c n l", n=NCH if mode == "p" else NS)

        def cur_views(u, mode):
            if mode == "p":
                return cur[u][:, :, 1:P + 1], cur[u][:, :, 0:P]
            v = runs(cur[u], mode)
            return v[:, :, :, 1:], v[:, :, :, 0:SL]

        ctx.callback(clear_semaphores, nc, held)
        block = ctx.enter_context(nc.Block())

        @block.sync
        def _(sp):
            def load_cur(t, u):
                sp.dma_start(cur[u][:, :, 0:P + 1], io["proj_T"][:, :, bass.ds(t * P, P + 1)].rearrange("c p n -> p c n")).then_inc(cur_loaded[u], 16)

            sp.dma_start(cur[0][:, :, 1:P + 1], io["proj_T"][:, :, 1:P + 1].rearrange("c p n -> p c n")).then_inc(cur_loaded[0], 16)
            sp.dma_start(consts[:], io["shape_consts"]).then_inc(params_loaded, 16)

            def column(dst, src):
                sp.dma_start(dst, src.rearrange("(c p) -> p c", p=P), allow_slow_non_contiguous=True).then_inc(params_loaded, 16)

            column(per_ch[:, 0:CT], io["shift_mix"][0])
            column(chan(DECAY), io["decay_base"][0])
            column(chan(ICLR), io["iclr_base"][0])
            column(chan(REMOVE), io["key_remove_scale"][0])
            column(chan(KICLR), io["key_iclr_scale"][0])
            column(chan(BONUS), io["bonus_scale"][0].rearrange("h d -> (h d)"))
            sp.dma_start(lora_w[0:HD, :], io["decay_lora_up"][0]).then_inc(params_loaded, 16)
            sp.dma_start(lora_w[HD:P, :], io["iclr_lora_up"][0]).then_inc(params_loaded, 16)
            sp.dma_start(gn[:, 0, :], io["out_norm_gain"][0].partition_broadcast(P)).then_inc(params_loaded, 16)
            sp.dma_start(gn[:, 1, :], io["out_norm_bias"][0].partition_broadcast(P)).then_inc(params_loaded, 16)
            load_cur(1, 1)
            sp.dma_start(st_shift, io["state_rwkv_shift"][0].rearrange("b o n -> (b o) n")).then_inc(states_loaded, 16)
            sp.dma_start(st_nat.rearrange("v b (h k) -> v (b h) k", h=H),
                         io["state_rwkv_wkv"][0].rearrange("b h v k -> v (b h) k")).then_inc(states_loaded, 16)

            GATE_ATT, GATE_RWKV = 3 * AW, 4 * AW + SHIFT_COLS
            w_in = io["w_in"][0].rearrange("(k p) n -> p k n", p=P)
            sp.wait_ge(states_turned, PAIRS + 1)
            for j, at in enumerate((GATE_ATT, GATE_RWKV)):
                sp.dma_start(gate_w[:].rearrange("p (j k n) -> p j k n", j=2, k=KT)[:, j], w_in[:, :, at:at + AW]).then_inc(gate_w_loaded, 16)

            def load_gate_x(n, b):
                tile = DEC if t_known(n) and n < 0 else n
                sp.dma_start(gate_x[:, b * D:(b + 1) * D], io["xT"][bass.ds(tile, 1)].rearrange("a p k n -> (a p) (k n)")).then_inc(gate_x_loaded[b], 16)

            load_gate_x(-1, 0)
            load_gate_x(0, 1)

            sp.dma_start(io["shift_prompt_new"].rearrange("a b c (k p) -> k p (a b c)", p=P), io["proj_T"][:, :, TILES * P:TILES * P + 1],
                         allow_slow_non_contiguous=True).then_inc(stored, 16)
            sp.dma_start(io["shift_sample_new"][0].rearrange("b o (k p) -> k p (b o)", p=P),
                         io["proj_T"][:, :, 1 + DEC * P:].rearrange("k p (b l) -> k p b l", b=NS)[:, :, :, SL - 1],
                         allow_slow_non_contiguous=True).then_inc(stored, 16)

            def gates(t, u, mode):
                yield 0.5
                if not t_known(t) or 0 <= t < TILES - 1:
                    sp.wait_ge(gate_written, 2 * t + 2)
                    load_gate_x(t + 1, u)
                for j in range(2):
                    yield (21 + 1, 44 + 1)[j]
                    rows = DEC if t_known(t) and t < 0 else t
                    sp.wait_ge(gate_copied, 2 * t + 3 + j)
                    sp.dma_start(io["gates"][bass.ds(rows * P, P), j * AW:(j + 1) * AW], gate_out[j][:]).then_inc(gate_stored[j], 16)

            def mix(t, u, mode):
                yield 16
                if t_known(t) and t + 2 > DEC:
                    return
                need(sp, t, "xs")
                if t_known(t) and t + 2 == DEC:
                    sp.dma_start(dec_cols[:], io["proj_T"][:, :, 1 + DEC * P:1 + (DEC + 1) * P].rearrange("c p n -> p c n")).then_inc(cur_loaded[0], 16)
                else:
                    load_cur(t + 2, u)

            def tail(t, u, mode):
                yield 9
                need(sp, t, "out")
                sp.dma_start(io["o_rwkv"][bass.ds(t * P, P), :], y_tok[:]).then_inc(o_stored, 16)

            tiles(sp, nothing, nothing, mix, tail, gates, (TILES - 4) // 2)
            sp.wait_ge(state_out, 1)
            for g in range(2):
                sp.dma_start(io["wkv_prompt_new"][0, 0].rearrange("(c g) v k -> g v c k", g=2)[g],
                             state_back[half(g), :, half(g)]).then_inc(stored, 16)
            sp.wait_ge(stored, 16 * 6)
            sp.wait_ge(o_stored, 16 * (TILES + 1))
            for j in range(2):
                sp.wait_ge(gate_stored[j], 16 * (TILES + 1))

        @block.gpsimd
        def _(pool):
            nc.gpsimd.memset(cur[0][:, :, 0:1], 0.0).then_inc(set_up, 1)
            nc.gpsimd.memset(g_run[:], 1.0).then_inc(set_up, 1)
            nc.gpsimd.memset(state[:], 0.0).then_inc(set_up, 1)
            for i in range(2):
                nc.gpsimd.memset(ar[i][:], 0.0).then_inc(set_up, 1)
            nc.gpsimd.memset(gn_eps, GN_EPS).then_inc(set_up, 1)
            nc.gpsimd.memset(ln_back, 8 * 0.6931471805599453).then_inc(set_up, 1)
            pool.wait_ge(params_loaded, 16 * 11)
            nc.gpsimd.tensor_scalar(chan(KICLR_REST), chan(KICLR), -1.0, 1.0, ALU.mult, ALU.add).then_inc(set_up, 1)
            pool.wait_ge(set_up, 8)

            def mix(t, u, mode):
                yield 10
                pool.wait_ge(cur_loaded[u], 8 * t + 16 - 8 * u)
                now, before = cur_views(u, mode)
                if mode == "s":
                    pool.wait_ge(dec_copied, 2)
                    pool.wait_ge(states_read, 1)
                past(pool, t, "tanh", "xs")
                was_written(pool, t, "iclr")
                was_written(pool, t, "v_tok")
                past(pool, t, "kk", "kmod", "rhat", "rk")
                nc.gpsimd.tensor_tensor(by_run(xs[:], mode) if mode == "s" else xs[:], before, now, ALU.subtract).then_inc(ready["delta"], 1)
                yield 16
                need(pool, t, "xs")
                past(pool, t, "kk_sq", "kk_n")
                nc.gpsimd.tensor_tensor(c4(kk[:]), xs[:, 4:8], spread(chan(REMOVE), P), ALU.mult).then_inc(ready["kk"], 1)
                yield 19
                past(pool, t, "rkr")
                was_written(pool, t, "bonus")
                nc.gpsimd.tensor_tensor(c4(rk[:]), xs[:, 0:4], spread(chan(BONUS), P), ALU.mult).then_inc(ready["rk"], 1)

            def front(t, u, mode):
                yield 0
                need(pool, t, "fac")
                past(pool, t, "kt", "rkr")
                nc.gpsimd.tensor_tensor(c4(kmod[:]), xs[:, 4:8], c4(fac[:]), ALU.mult).then_inc(ready["kmod"], 1)
                yield 2
                need(pool, t, "kk_n")
                past(pool, t, "bt")
                nc.gpsimd.tensor_tensor(bmul[:], kk_n[:], a_gate[:], ALU.mult).then_inc(ready["bmul"], 1)
                yield 3
                need(pool, t, "rk", "kmod")
                nc.gpsimd.tensor_tensor(rk[:], rk[:], kmod[:], ALU.mult).then_inc(ready["rkr"], 1)

            def back(t, u, mode):
                if mode == "s":
                    yield 47
                    for g, c in [(g, c) for c in range(PAIRS) for g in range(2)]:
                        n = c
                        pool.wait_ge(u_ready, 2 * DEC + 2)
                        pool.wait_ge(gate_written, 2 * (TILES + 1))
                        wait(pool, dec_added[g], n)
                        nc.gpsimd.tensor_tensor(spread_u[g], u_tok[:, head_cols(g, c)].rearrange("p (o d) -> p o d", o=1).broadcast_to([P, NS, HD]),
                                                spread(const("stream_of"), HD), ALU.mult).then_inc(dec_spread_u[g], 1)

            def tail(t, u, mode):
                yield 4
                was_read(pool, t, "bonus")
                past(pool, t, "out")
                need(pool, t, "y_var")
                nc.gpsimd.tensor_tensor(heads(y_sq[:]), heads(v_tok[u][:]), spread(bonus[u][:], HD), ALU.mult).then_inc(ready["v_bonus"], 1)
                yield 5
                need(pool, t, "y_rstd", "y_centred")
                nc.gpsimd.tensor_tensor(heads(y_tok[:]), heads(y_tok[:]), spread(y_rstd, HD), ALU.mult).then_inc(ready["y_scaled"], 1)
                yield 6
                need(pool, t, "y_scaled")
                nc.gpsimd.tensor_tensor(y_tok[:], y_tok[:], gn[:, 0, :], ALU.mult).then_inc(ready["y_gained"], 1)
                yield 7
                need(pool, t, "y_gained")
                nc.gpsimd.tensor_tensor(y_tok[:], y_tok[:], gn[:, 1, :], ALU.add).then_inc(ready["y_based"], 1)
                yield 8
                need(pool, t, "y_based", "v_bonus")
                nc.gpsimd.tensor_tensor(y_tok[:], y_tok[:], y_sq[:], ALU.add).then_inc(ready["out"], 1)

            tiles(pool, front, back, mix, tail)

        @block.scalar
        def _(act):
            act.wait_ge(set_up, 8)
            act.wait_ge(states_turned, PAIRS + 1)
            nc.scalar.activation(shift_T[:].rearrange("p c b -> p (c b)"), ps_y[:, 0:CT * NS], ACT.Copy).then_inc(states_read, 1)
            for c, src in enumerate((ps_rhs, ps_u, ps_gate, ps_inv[0])):
                nc.scalar.activation(states[:, c].rearrange("p b i -> p (b i)"), src[:], ACT.Copy).then_inc(states_read, 1)

            def mix(t, u, mode):
                yield 21
                act.preload_act_table_set("sigmoid_and_others")
                need(act, t, "lora_in")
                was_written(act, t, "decay")
                nc.scalar.activation(th[:], xs[0:HD, CT - 1, :], ACT.Tanh).then_inc(ready["tanh"], 1)
                yield 23
                ps, read = written(act, t, "decay")
                past(act, t, "acc")
                for c in range(PAIRS):
                    last = nc.scalar.activation(sig[:, pair_cols(c)], ps[:, pair_cols(c)], ACT.Sigmoid, bias=chan(DECAY)[:, c:c + 1])
                last.then_inc(read, 1)
                ps, read = written(act, t, "iclr")
                past(act, t, "fac", "bmul")
                for c in range(PAIRS):
                    last = nc.scalar.activation(a_gate[:, pair_cols(c)], ps[:, pair_cols(c)], ACT.Sigmoid, bias=chan(ICLR)[:, c:c + 1])
                last.then_inc(read, 1)
                yield 24
                need(act, t, "kk")
                was_written(act, t, "kk_sum")
                nc.scalar.activation(kk_sq[:], kk[:], ACT.Square).then_inc(ready["kk_sq"], 1)

            def front(t, u, mode):
                yield 0
                act.preload_act_table_set(ACT_TABLES)
                was_read(act, t, "kk_sum")
                nc.scalar.activation(kk_n[:], kk_n[:], ACT.Ln, scale=LN_UP).then_inc(ready["kk_log"], 1)
                need(act, t, "kk_log")
                nc.scalar.activation(kk_n[:], kk_n[:], ACT.Exp, scale=-0.5, bias=ln_back).then_inc(ready["rnorm"], 1)
                yield 1
                need(act, t, "acc")
                past(act, t, "rhat", "ahat", "g_last")
                if mode == "s":
                    act.wait_ge(dec_copied, 3)
                nc.scalar.activation(runs(g_run, mode)[:, :, :, 1:], by_run(c4(acc[:]), mode), ACT.Exp, scale=-KAPPA).then_inc(ready["g_run"], 1)
                yield 2
                past(act, t, "bt", "kt")
                nc.scalar.activation(inv_g[:], acc[:], ACT.Exp, scale=KAPPA).then_inc(ready["inv_g"], 1)
                yield 5
                wait(act, ready["ps_y"], t - 1)
                wait(act, ready["v_bonus"], t - 1)
                for name, buf in (("v_tok", v_tok), ("k_tok", k_tok), ("b_tok", b_tok)):
                    yield 5 if name == "v_tok" else 7
                    ps, read = written(act, t, name)
                    nc.scalar.activation(buf[u][:], ps[:], ACT.Copy).then_inc(read, 1)
                yield 18.5
                ps, read = written(act, t, "bonus")
                nc.scalar.activation(bonus[u][:], ps[:, 0:H], ACT.Copy).then_inc(read, 1)

            def back(t, u, mode):
                for l in range(LEVELS[mode] - 1):
                    for g in range(2):
                        yield 3.5 * (l + 1) + 0.2 + g
                        act.wait_ge(turn_written[g], (LP - 1) * t + l + 1)
                        nc.scalar.activation(x_mat[:, g].rearrange("p c n -> p (c n)"), ps_turn[g][:], ACT.Copy).then_inc(x_ready[g], 1)
                if mode == "p":
                    for n in range(NCH):
                        yield 27 + 8 * n
                        act.wait_ge(rhs_written, 2 * t + n + 1)
                        nc.scalar.activation(rhs[half(n), :], ps_rhs[half(n), :], ACT.Copy).then_inc(rhs_ready, 1)
                        yield 29 + 8 * n
                        act.wait_ge(u_written, 2 * t + n + 1)
                        nc.scalar.activation(u_tok[half(n), :], ps_u[half(n), :], ACT.Copy).then_inc(u_ready, 1)
                else:
                    yield 27
                    act.wait_ge(state_turned, 1)
                    nc.scalar.activation(acc[:], ps_gate[:], ACT.Copy).then_inc(state_out, 1)
                    yield 29
                    for n, ps in enumerate((ps_u, ps_gate)):
                        act.wait_ge(u_written, 2 * t + n + 1)
                        nc.scalar.activation(u_tok[half(n), :], ps[half(n), :], ACT.Copy).then_inc(u_ready, 1)
                yield 47
                need(act, t, "y_centred")
                past(act, t, "out")
                nc.scalar.activation(y_sq[:], y_tok[:], ACT.Square).then_inc(ready["y_sq"], 1)
                if mode == "s":
                    for b in range(NS):
                        act.wait_ge(turned_back, b + 1)
                        act.wait_ge(gate_written, 2 * (TILES + 1))
                        nc.scalar.activation(st_nat[:, b, :], ps_inv[b % 2][0:HD, :], ACT.Copy).then_inc(nat_ready, 1)
                        if b % 4 == 3:
                            act.wait_ge(nat_ready, b + 1)
                            act.dma_start(io["wkv_sample_new"][0, b - 3:b + 1].rearrange("b h v k -> v (b h) k"),
                                          st_nat[:, b - 3:b + 1, :].rearrange("v b (h k) -> v (b h) k", h=H)).then_inc(stored, 16)

            def tail(t, u, mode):
                yield 3
                need(act, t, "y_var")
                nc.scalar.activation(y_rstd, y_var, ACT.Ln, scale=1.0 / HD, bias=gn_eps).then_inc(ready["y_log"], 1)
                need(act, t, "y_log")
                nc.scalar.activation(y_rstd, y_rstd, ACT.Exp, scale=-0.5).then_inc(ready["y_rstd"], 1)

            def gates(t, u, mode):
                for j in range(2):
                    yield (21, 44)[j]
                    act.wait_ge(gate_written, 2 * t + 3 + j)
                    wait(act, gate_stored[j], 16 * t + 16)
                    nc.scalar.activation(gate_out[j][:], ps_gate[:], ACT.Copy).then_inc(gate_copied, 1)

            tiles(act, front, back, mix, tail, gates)

        @block.vector
        def _(dve):
            dve.wait_ge(set_up, 8)

            def masked(out, ps, mask, n, read):
                m = mask.rearrange("p (o w) -> p o w", o=1).broadcast_to([P, n, mask.shape[1]])
                nc.vector.tensor_tensor(out, ps[:].rearrange("p (c w) -> p c w", c=n), m, ALU.mult).then_inc(read, 1)

            def mix(t, u, mode):
                yield 9
                if mode == "s":
                    dve.wait_ge(cur_loaded[u], 8 * t + 16)
                    dve.wait_ge(states_read, PAIRS + 1)
                    v = runs(cur[u], mode)
                    nc.vector.tensor_copy(v[:, :, :, 1:], by_run(dec_cols[:], mode)).then_inc(dec_copied, 1)
                    nc.vector.tensor_copy(v[:, :, :, 0], shift_T[:]).then_inc(dec_copied, 1)
                yield 14
                need(dve, t, "delta")
                now, _ = cur_views(u, mode)
                for ct in [CT - 1] + list(range(CT - 1)):
                    x = xs[:, ct] if mode == "p" else xs[:, ct].rearrange("p (n l) -> p n l", n=NS)
                    op = nc.vector.scalar_tensor_tensor(out=x, in0=x, scalar=per_ch[:, ct:ct + 1], in1=now[:, ct],
                                                        op0=ALU.mult, op1=ALU.add)
                    if ct == CT - 1:
                        op.then_inc(ready["lora_in"], 1)
                op.then_inc(ready["xs"], 1)
                yield 29
                ps, read = written(dve, t, "kk_sum")
                past(dve, t, "ahat", "bmul")
                nc.vector.tensor_scalar(kk_n[:], ps[:], 1e-24, None, ALU.max).then_inc(read, 1)
                yield 31
                was_read(dve, t, "decay")
                past(dve, t, "g_run", "inv_g")
                nc.vector.tensor_tensor_scan(acc[:], const("run", mode), sig[:], 0.0, ALU.mult, ALU.add).then_inc(ready["acc"], 1)
                yield 35
                was_read(dve, t, "iclr")
                past(dve, t, "kmod")
                for c in range(PAIRS):
                    last = nc.vector.tensor_scalar(fac[:, pair_cols(c)], a_gate[:, pair_cols(c)], chan(KICLR)[:, c:c + 1],
                                                   chan(KICLR_REST)[:, c:c + 1], ALU.mult, ALU.add)
                last.then_inc(ready["fac"], 1)

            def front(t, u, mode):
                yield 0
                if mode == "s":
                    past(dve, t, "g_last", "ahat", "rhat")
                    nc.vector.memset(runs(g_run, mode)[:, :, :, 0], 1.0).then_inc(dec_copied, 1)
                yield 2
                need(dve, t, "rnorm", "kk")
                nc.vector.scalar_tensor_tensor(out=kk_n[:], in0=kk[:], scalar=-1.0, in1=kk_n[:], op0=ALU.mult,
                                               op1=ALU.mult).then_inc(ready["kk_n"], 1)
                need(dve, t, "kk_n", "g_run")
                wait(dve, ready["ps_y"], t - 1)
                for g in range(2):
                    last = nc.vector.tensor_tensor(by_run(ar[u][half(g), :, g, 0, :], mode), by_run(c4(kk_n[half(g)]), mode),
                                                   runs(g_run[half(g)], mode)[:, :, :, 0:CH if mode == "p" else SL], ALU.mult)
                last.then_inc(ready["ahat"], 1)
                for g in range(2):
                    last = nc.vector.tensor_tensor(by_run(ar[u][half(g), :, g, 1, :], mode), by_run(xs[half(g), 0:4], mode),
                                                   runs(g_run[half(g)], mode)[:, :, :, 1:], ALU.mult)
                last.then_inc(ready["rhat"], 1)
                yield 3
                need(dve, t, "bmul", "inv_g")
                was_written(dve, t, "RB1")
                nc.vector.scalar_tensor_tensor(out=bt[:], in0=bmul[:], scalar=-1.0, in1=inv_g[:], op0=ALU.mult,
                                               op1=ALU.mult).then_inc(ready["bt"], 1)
                need(dve, t, "kmod")
                was_written(dve, t, "AK3")
                nc.vector.tensor_tensor(kt[:], kmod[:], inv_g[:], ALU.mult).then_inc(ready["kt"], 1)
                wait(dve, state_ready, 2 * (t - 1))
                k = NCH if mode == "p" else NS
                nc.vector.tensor_copy(g_last[u][:, :, 0:k], runs(g_run, mode)[:, :, :, CH if mode == "p" else SL]).then_inc(ready["g_last"], 1)
                wait(dve, ready["ps_y"], t - 1)
                for name, out, mask, n in (
                        [(f"A{g}", a_mat[u][:, g], const("lower", mode), PAIRS) for g in range(2)]
                        + [(f"AK{c}", ak_T[u][:, c].rearrange("p g k n -> p g (k n)"), const("upper", mode), 2) for c in range(PAIRS)]
                        + [(f"RB{i}", rb_T[u][:, 2 * i:2 * i + 2].rearrange("p c g n -> p (c g) n"), const("upper", mode)[:, P:2 * P], PAIRS)
                           for i in range(2)]):
                    yield GRAM_STAGES[name] + 0.5
                    ps, read = written(dve, t, name)
                    masked(out, ps, mask, n, read)

            def back(t, u, mode):
                idents = ident.rearrange("p (o n) -> p o n", o=1).broadcast_to([P, PAIRS, P])
                for l in range(LEVELS[mode]):
                    level = const("levels")[:, l * P:(l + 1) * P].rearrange("p (o n) -> p o n", o=1).broadcast_to([P, PAIRS, P])
                    base = (2 * LP - 1) * t
                    for g in range(2):
                        yield 3.5 * l + 0.5 + g
                        dve.wait_ge(inv_written[g], base + (1 if l == 0 else 2 * l))
                        if l == 0 and g == 0:
                            wait(dve, u_written, 2 * t)
                        nc.vector.tensor_tensor(q_mat[:, g], c4(ps_inv[g][:]),
                                                level, ALU.mult).then_inc(q_ready[g], 1)
                        yield 3.5 * l + 1.5 + g
                        if l == 0:
                            dve.wait_ge(q_ready[g], LP * t + 1)
                            nc.vector.tensor_tensor(y_mat[:, g], q_mat[:, g], idents, ALU.add).then_inc(y_ready[g], 1)
                        else:
                            dve.wait_ge(inv_written[g], base + 2 * l + 1)
                            nc.vector.tensor_tensor(y_mat[:, g], y_mat[:, g],
                                                    c4(ps_inv[g][:]),
                                                    ALU.add).then_inc(y_ready[g], 1)
                if mode == "p":
                    y_src = ps_y
                    for n in range(NCH):
                        yield 32 + 8 * n
                        dve.wait_ge(s_written, 2 * t + n + 1)
                        need(dve, t, "g_last")
                        for i in range(2):
                            last = nc.vector.tensor_tensor(state[half(i), :, half(i)], state[half(i), :, half(i)],
                                                           ps_s[half(i), :].rearrange("p (c n) -> p c n", c=PAIRS)[:, :, half(i)], ALU.add)
                        last.then_inc(s_added, 1)
                        dve.wait_ge(s_added, 2 * t + n + 1)
                        for i in range(2):
                            g_l = g_last[u][half(i), :, n:n + 1].broadcast_to([HD, PAIRS, HD])
                            last = nc.vector.tensor_tensor(state[half(i), :, half(i)], state[half(i), :, half(i)], g_l, ALU.mult)
                        last.then_inc(state_ready, 1)
                    yield 44
                    need(dve, t, "ps_y")
                else:
                    yield 24
                    dve.wait_ge(gate_written, 2 * (TILES + 1))
                    for i in range(2 * PAIRS):
                        for g in range(2):
                            dve.wait_ge(dec_written[g], i + 1)
                            nc.vector.tensor_tensor(spread_s[g], ps_inv[g][:].rearrange("p (b d) -> p b d", b=NS),
                                                    spread(const("stream_of"), HD), ALU.mult).then_inc(dec_masked[g], 1)
                            dve.wait_ge(dec_masked[g], i + 1)
                            nc.vector.tensor_reduce(from_state[i % 2][:, head_cols(g, i // 2)],
                                                    spread_s[g].rearrange("p b d -> p d b"), AX_X, ALU.add).then_inc(dec_summed[g], 1)
                    yield 27
                    dve.wait_ge(rhs_written, 2 * t + 1)
                    for g in range(2):
                        dve.wait_ge(dec_summed[g], 2 * PAIRS)
                    nc.vector.tensor_tensor(rhs[:], ps_rhs[:], from_state[0], ALU.add).then_inc(rhs_ready, 1)
                    yield 44
                    need(dve, t, "ps_y")
                    nc.vector.tensor_tensor(from_state[1], ps_y[:], from_state[1], ALU.add).then_inc(y_raw_ready, 1)
                    dve.wait_ge(y_raw_ready, 1)
                    y_src = from_state[1]
                past(dve, t, "y_centred")
                nc.vector.tensor_reduce(y_sum, heads(y_src[:, :]), AX_X, ALU.add).then_inc(ready["y_sum"], 1)
                need(dve, t, "y_sum")
                nc.vector.tensor_scalar(y_mean, y_sum, 1.0 / HD, None, ALU.mult).then_inc(ready["y_mean"], 1)
                need(dve, t, "y_mean")
                wait(dve, o_stored, 16 * t)
                nc.vector.tensor_tensor(heads(y_tok[:]), heads(y_src[:, :]), spread(y_mean, HD), ALU.subtract).then_inc(ready["y_centred"], 1)
                if mode == "s":
                    need(dve, t, "g_last")
                    for c in range(PAIRS):
                        for g in range(2):
                            wait(dve, dec_added[g], c)
                            nc.vector.tensor_tensor(spread_s[g], v_tok[u][:, head_cols(g, c)].rearrange("p (o d) -> p o d", o=1).broadcast_to([P, NS, HD]),
                                                    spread(const("stream_of"), HD), ALU.mult).then_inc(dec_spread_v[g], 1)
                            dve.wait_ge(dec_written[g], 2 * PAIRS + c + 1)
                            nc.vector.tensor_tensor(states[half(g), c], states[half(g), c],
                                                    ps_inv[g][half(g), :].rearrange("p (b d) -> p b d", b=NS), ALU.add).then_inc(dec_added[g], 1)
                            dve.wait_ge(dec_added[g], c + 1)
                            g_l = g_last[u][half(g), c, :].rearrange("p (b o) -> p b o", o=1).broadcast_to([HD, NS, HD])
                            nc.vector.tensor_tensor(states[half(g), c], states[half(g), c], g_l, ALU.mult).then_inc(dec_state[g], 1)

            def tail(t, u, mode):
                yield 1
                need(dve, t, "y_sq")
                nc.vector.tensor_reduce(y_var, heads(y_sq[:]), AX_X, ALU.add).then_inc(ready["y_var"], 1)

            tiles(dve, front, back, mix, tail)

        @block.tensor
        def _(pe):
            pe.wait_ge(states_loaded, 32)
            pe.wait_ge(params_loaded, 16 * 11)
            for ct in range(CT):
                last = nc.tensor.transpose(ps_y[:, ct * NS:(ct + 1) * NS], st_shift[:, ct * P:(ct + 1) * P], ident[0:NS, 0:NS])
            last.then_inc(states_turned, 1)
            for c, out in enumerate((ps_rhs, ps_u, ps_gate, ps_inv[0])):
                for b in range(NS):
                    last = nc.tensor.transpose(out[:, b * HD:(b + 1) * HD], st_nat[:, b, pair_cols(c)], ident[0:HD, 0:HD])
                last.then_inc(states_turned, 1)
            pe.wait_ge(states_read, PAIRS + 1)
            pe.wait_ge(set_up, 8)

            def mix(t, u, mode):
                yield 22
                need(pe, t, "tanh")
                ps, done = free_bank(t, "decay")
                for c in range(PAIRS):
                    last = nc.tensor.matmul(ps[:, pair_cols(c)], lora_w[0:HD, pair_cols(c)], th[:], start=True, stop=True)
                last.then_inc(done, 1)
                ps, done = free_bank(t, "iclr")
                for c in range(PAIRS):
                    last = nc.tensor.matmul(ps[:, pair_cols(c)], lora_w[HD:P, pair_cols(c)], xs[HD:P, CT - 1, :], start=True, stop=True)
                last.then_inc(done, 1)
                yield 25
                need(pe, t, "kk_sq")
                ps, done = free_bank(t, "kk_sum")
                nc.tensor.matmul(ps[:], const("head_ones"), kk_sq[:], start=True, stop=True).then_inc(done, 1)
                yield 25.5
                turn(t, "v_tok", xs[:, 8:12])

            def turn(t, name, src):
                ps, done = free_bank(t, name)
                for c in range(PAIRS):
                    last = nc.tensor.transpose(ps[:, pair_cols(c)], src[:, c], ident)
                last.then_inc(done, 1)

            def front(t, u, mode):
                yield 6
                need(pe, t, "kt")
                turn(t, "k_tok", c4(kt[:]))
                need(pe, t, "bt")
                turn(t, "b_tok", c4(bt[:]))
                need(pe, t, "ahat", "rhat")
                for g in range(2):
                    yield GRAM_STAGES[f"A{g}"]
                    ps, done = free_bank(t, f"A{g}")
                    for c in range(PAIRS):
                        last = nc.tensor.matmul(ps[:, pair_cols(c)], ar[u][:, c, g, 0, :], bt[:, pair_cols(c)], start=True, stop=True)
                    last.then_inc(done, 1)
                for c in range(PAIRS):
                    yield GRAM_STAGES[f"AK{c}"]
                    ps, done = free_bank(t, f"AK{c}")
                    nc.tensor.matmul(ps[:], kt[:, pair_cols(c)], ar[u][:, c].rearrange("p g k n -> p (g k n)"),
                                     start=True, stop=True).then_inc(done, 1)
                for i in range(2):
                    yield GRAM_STAGES[f"RB{i}"]
                    ps, done = free_bank(t, f"RB{i}")
                    for c in (2 * i, 2 * i + 1):
                        last = nc.tensor.matmul(ps[:, (c - 2 * i) * 2 * P:(c - 2 * i + 1) * 2 * P], bt[:, pair_cols(c)], ar[u][:, c, :, 1, :],
                                                start=True, stop=True)
                    last.then_inc(done, 1)
                yield 18
                need(pe, t, "rkr")
                ps, done = free_bank(t, "bonus")
                for c in range(PAIRS):
                    last = nc.tensor.matmul(ps[:, 2 * c:2 * c + 2], rk[:, pair_cols(c)], const("head_of"), start=True, stop=True)
                last.then_inc(done, 1)

            def back(t, u, mode):
                all_heads = [(g, c) for c in range(PAIRS) for g in range(2)]

                def values(kind, out, head):
                    g, c = head
                    return nc.tensor.matmul(out[:, head_cols(g, c)], ak_T[u][:, c, g, kind, :], v_tok[u][:, head_cols(g, c)],
                                            start=(head == all_heads[0]), stop=(mode == "s" and kind == 0 and head == all_heads[-1]))

                for l in range(LEVELS[mode]):
                    if l > 0:
                        yield 3.5 * l - 0.7
                        if l == 1:
                            for g in range(2):
                                was_read(pe, t, f"RB{g}")
                            wait(pe, ready["y_centred"], t)
                            wait(pe, rhs_ready, 2 * t)
                        k = 2 if mode == "p" else 3
                        for head in all_heads[k * (l - 1):k * l]:
                            values(1, ps_y, head)
                            last = values(0, ps_rhs, head)
                            if mode == "s" and head == all_heads[-1]:
                                last.then_inc(rhs_written, 1)
                    for g in range(2):
                        yield 3.5 * l + g
                        if l == 0:
                            was_read(pe, t, f"A{g}")
                            if g == 0:
                                wait(pe, s_added, 2 * t)
                        else:
                            pe.wait_ge(y_ready[g], LP * t + l)
                        for c in range(PAIRS):
                            last = nc.tensor.matmul(ps_inv[g][:, pair_cols(c)], a_mat[u][:, g, c, :],
                                                    ident if l == 0 else y_mat[:, g, c, :], start=True, stop=True)
                        last.then_inc(inv_written[g], 1)
                        if l > 0:
                            if g == 1:
                                pe.wait_ge(x_ready[0], (LP - 1) * t + l)
                            elif l == 1:
                                wait(pe, u_ready, 2 * t)
                            for c in range(PAIRS):
                                last = nc.tensor.transpose(ps_turn[g][:, pair_cols(c)], y_mat[:, g, c, :], ident)
                            last.then_inc(turn_written[g], 1)
                    for g in range(2):
                        if l > 0:
                            yield 3.5 * l + 1 + g
                            pe.wait_ge(x_ready[g], (LP - 1) * t + l)
                            pe.wait_ge(q_ready[g], LP * t + l + 1)
                            for c in range(PAIRS):
                                last = nc.tensor.matmul(ps_inv[g][:, pair_cols(c)], x_mat[:, g, c, :],
                                                        q_mat[:, g, c, :], start=True, stop=True)
                            last.then_inc(inv_written[g], 1)
                def solve(n, out):
                    for g, c in all_heads:
                        last = nc.tensor.matmul(out[half(n), head_cols(g, c)], y_mat[half(n), g, c, half(n)], rhs[half(n), head_cols(g, c)],
                                                start=True, stop=True)
                    last.then_inc(u_written, 1)

                if mode == "p":
                    for n in range(NCH):
                        yield 26 + 8 * n
                        tokens = slice(n * CH, (n + 1) * CH)
                        wait(pe, state_ready, 2 * t + n)
                        for g, c in all_heads:
                            last = nc.tensor.matmul(ps_rhs[half(n), head_cols(g, c)], ar[u][:, c, g, 0, tokens], state[:, c, half(g)],
                                                    start=False, stop=((g, c) == all_heads[-1]))
                        last.then_inc(rhs_written, 1)
                        for g, c in all_heads[:-1]:
                            nc.tensor.matmul(ps_y[half(n), head_cols(g, c)], ar[u][:, c, g, 1, tokens], state[:, c, half(g)], start=False, stop=False)
                        if n == 0:
                            pe.wait_ge(y_ready[0], LP * t + LP)
                        for c in range(PAIRS):
                            nc.tensor.matmul(ps_s[:, pair_cols(c)], k_tok[u][half(n), pair_cols(c)], v_tok[u][half(n), pair_cols(c)],
                                             start=(c == 0), stop=False)
                        yield 28 + 8 * n
                        pe.wait_ge(rhs_ready, 2 * t + n + 1)
                        if n == 0:
                            pe.wait_ge(y_ready[1], LP * t + LP)
                        g, c = all_heads[-1]
                        nc.tensor.matmul(ps_y[half(n), head_cols(g, c)], ar[u][:, c, g, 1, tokens], state[:, c, half(g)], start=False, stop=False)
                        solve(n, ps_u)
                        yield 30 + 8 * n
                        pe.wait_ge(u_ready, 2 * t + n + 1)
                        for c in range(PAIRS):
                            last = nc.tensor.matmul(ps_s[:, pair_cols(c)], b_tok[u][half(n), pair_cols(c)], u_tok[half(n), pair_cols(c)],
                                                    start=False, stop=(c == PAIRS - 1))
                        last.then_inc(s_written, 1)
                else:
                    yield 22
                    pe.wait_ge(state_ready, NCH * TILES)
                    pe.wait_ge(gate_copied, 2 * (TILES + 1))
                    for c in range(PAIRS):
                        last = nc.tensor.transpose(ps_gate[:, pair_cols(c)], state[:, c, :], ident)
                    last.then_inc(state_turned, 1)
                    for g in range(2):
                        pe.wait_ge(y_ready[g], LP * t + LEVELS[mode])
                    for i in range(2 * PAIRS):
                        for g in range(2):
                            wait(pe, dec_masked[g], i)
                            nc.tensor.matmul(ps_inv[g][:], ar[u][half(g), i // 2, g, i % 2, :], states[half(g), i // 2].rearrange("p b i -> p (b i)"),
                                             start=True, stop=True).then_inc(dec_written[g], 1)
                    yield 28
                    pe.wait_ge(rhs_ready, 2 * t + 1)
                    pe.wait_ge(state_out, 1)
                    solve(0, ps_u)
                    solve(1, ps_gate)
                    pe.wait_ge(u_ready, 2 * t + 2)
                yield 43
                for g, c in all_heads:
                    last = nc.tensor.matmul(ps_y[:, head_cols(g, c)], rb_T[u][:, c, g, :], u_tok[:, head_cols(g, c)], start=False,
                                            stop=((g, c) == all_heads[-1]))
                last.then_inc(ready["ps_y"], 1)
                if mode == "s":
                    for c in range(PAIRS):
                        for g in range(2):
                            pe.wait_ge(dec_masked[g], 2 * PAIRS)
                            wait(pe, dec_added[g], c)
                            pe.wait_ge(dec_spread_v[g], c + 1)
                            nc.tensor.matmul(ps_inv[g][half(g), :], k_tok[u][:, head_cols(g, c)], spread_s[g].rearrange("p b d -> p (b d)"),
                                             start=True, stop=False)
                            pe.wait_ge(dec_spread_u[g], c + 1)
                            nc.tensor.matmul(ps_inv[g][half(g), :], b_tok[u][:, head_cols(g, c)], spread_u[g].rearrange("p b d -> p (b d)"),
                                             start=False, stop=True).then_inc(dec_written[g], 1)
                    pe.wait_ge(dec_state[0], PAIRS)
                    pe.wait_ge(dec_state[1], PAIRS)
                    for b in range(NS):
                        wait(pe, nat_ready, b - 1)
                        for c in range(PAIRS):
                            last = nc.tensor.transpose(ps_inv[b % 2][0:HD, pair_cols(c)], states[:, c, b, :], ident)
                        last.then_inc(turned_back, 1)

            def gates(t, u, mode):
                at = ((0.3, 1.3, 2.3, 5.3, 8.8, 12.3, 15.8, 18.3), (26.5, 28.5, 30.5, 34.5, 36.5, 38.5, 42.9, 43.1))
                w = gate_w[:].rearrange("p (j k n) -> p j k n", j=2, k=KT)
                for j in range(2):
                    for k in range(KT):
                        yield at[j][k]
                        if k == 0:
                            pe.wait_ge(gate_x_loaded[1 - u], 8 * t + 16 + 8 * u)
                            if t_known(t) and t < 0:
                                pe.wait_ge(gate_w_loaded, 32)
                            wait(pe, gate_copied, 2 * t + 2 + j)
                        x = gate_x[:, (1 - u) * D + k * P:(1 - u) * D + (k + 1) * P]
                        mm = nc.tensor.matmul(ps_gate[:], x, w[:, j, k, :], start=(k == 0), stop=(k == KT - 1))
                    mm.then_inc(gate_written, 1)

            tiles(pe, front, back, mix, gates=gates)


def output_phase(nc, io):
    with ExitStack() as ctx:
        def sb(name, shape, dt=F32):
            return ctx.enter_context(nc.sbuf_tensor(name, shape, dt))

        def sem(name):
            return ctx.enter_context(nc.semaphore(name))

        w_hi, w_lo = sb("o_w_hi", [P, KT, D], F32R), sb("o_w_lo", [P, KT, D], F32R)
        w_raw = [sb(f"o_w_raw{i}", [P, D]) for i in range(4)]
        g_tok = [sb(f"o_g{i}", [P, 2, AW]) for i in range(2)]
        o_tok = [sb(f"o_o{i}", [P, 2, AW]) for i in range(2)]
        z = [sb(f"o_z{i}", [P, 2, AW]) for i in range(2)]
        z_hi, z_lo = ([sb(f"o_z_{n}{i}", [P, KT, P], F32R) for i in range(2)] for n in ("hi", "lo"))
        x_tok = [sb(f"o_x{i}", [P, D]) for i in range(2)]
        y_tok = [sb(f"o_y{i}", [P, D]) for i in range(2)]
        ident = sb("o_ident", [P, P])
        ps_zT = [ctx.enter_context(nc.psum_tensor(f"o_ps_zT{i}", [P, D], F32)) for i in range(2)]
        ps_y = [ctx.enter_context(nc.psum_tensor(f"o_ps_y{i}", [P, D], F32)) for i in range(2)]

        ident_zero, ident_ready = sem("o_ident_zero"), sem("o_ident_ready")
        w_loaded = [sem(f"o_w_loaded{i}") for i in range(4)]
        w_hi_ready, w_lo_ready = sem("o_w_hi_ready"), sem("o_w_lo_ready")
        g_loaded, o_loaded, x_loaded = ([sem(f"o_{n}_loaded{i}") for i in range(2)] for n in ("g", "o", "x"))
        gate_ready, z_ready = sem("o_gate_ready"), sem("o_z_ready")
        z_turned, z_hi_ready, z_lo_ready = sem("o_z_turned"), sem("o_z_hi_ready"), sem("o_z_lo_ready")
        y_summed, y_ready = sem("o_y_summed"), sem("o_y_ready")
        y_stored = [sem(f"o_y_stored{i}") for i in range(2)]

        w_out = io["w_out"][0].rearrange("(k p) n -> p k n", p=P)
        block = ctx.enter_context(nc.Block())

        def tiles(eng, step):
            step(0, 0)
            step(1, 1)
            with eng.Fori(1, TILES // 2) as i:
                step(i * 2, 0)
                step(i * 2 + 1, 1)
            step(DEC, 0)

        def loads(t, u):
            return 8 * t + 16 - 8 * u

        @block.sync
        def _(sp):
            def load(n, u):
                last = t_known(n) and n == DEC
                sp.dma_start(g_tok[u][:].rearrange("p g n -> p (g n)"), io["gates"][bass.ds(n * P, P), :]).then_inc(g_loaded[u], 16)
                sp.dma_start(o_tok[u][:, 0, :], io["o_att"][bass.ds(n * P, P), :]).then_inc(o_loaded[u], 16)
                sp.dma_start(o_tok[u][:, 1, :], io["o_rwkv"][bass.ds(n * P, P), :]).then_inc(o_loaded[u], 16)
                if not (t_known(n) and n < 2):
                    sp.wait_ge(y_ready, 2 * n - 2)
                x = rows_of(io["x_sample"], D) if last else rows_of(io["x_prompt"], D)[bass.ds(n * P, P), :]
                sp.dma_start(x_tok[u][:], x).then_inc(x_loaded[u], 16)

            for k in range(KT):
                if k >= 4:
                    sp.wait_ge(w_lo_ready, k - 3)
                sp.dma_start(w_raw[k % 4][:], w_out[:, k, :]).then_inc(w_loaded[k % 4], 16)
                if k < 2:
                    load(k, k)

            def store(t, u):
                last = t_known(t) and t == DEC
                y = rows_of(io["y_sample"], D) if last else rows_of(io["y_prompt"], D)[bass.ds(t * P, P), :]
                sp.wait_ge(y_ready, 2 * t + 2)
                sp.dma_start(y, y_tok[u][:]).then_inc(y_stored[u], 16)

            def move(t, u, nxt):
                sp.wait_ge(z_ready, t + 1)
                load(nxt, u)
                store(t, u)

            with sp.Fori(0, TILES // 2 - 1) as i:
                move(i * 2, 0, i * 2 + 2)
                move(i * 2 + 1, 1, i * 2 + 3)
            move(TILES - 2, 0, DEC)
            store(TILES - 1, 1)
            store(DEC, 0)
            sp.wait_ge(y_stored[0], 16 * (TILES // 2 + 1))
            sp.wait_ge(y_stored[1], 16 * (TILES // 2))

        @block.gpsimd
        def _(pool):
            nc.gpsimd.memset(ident[:], 0.0).then_inc(ident_zero, 1)
            pool.wait_ge(ident_zero, 1)
            nc.gpsimd.affine_select(out=ident[:], in_=ident[:], compare_op=ALU.not_equal, fill=1.0, base=0,
                                    pattern=[[-1, P]], channel_multiplier=1).then_inc(ident_ready, 1)

        @block.scalar
        def _(act):
            def silu(t, u):
                act.wait_ge(g_loaded[u], loads(t, u))
                nc.scalar.activation(g_tok[u][:], g_tok[u][:], ACT.Silu).then_inc(gate_ready, 1)

            def z_part(t, u):
                act.wait_ge(z_turned, t + 1)
                wait(act, y_summed, 2 * (t - 1))
                nc.scalar.activation(z_hi[u][:].rearrange("p k n -> p (k n)"), ps_zT[u][:], ACT.Copy).then_inc(z_hi_ready, 1)

            silu(0, 0)
            silu(1, 1)
            z_part(0, 0)
            for k in range(KT):
                act.wait_ge(w_loaded[k % 4], 16 * (k // 4 + 1))
                nc.scalar.activation(w_hi[:, k, :], w_raw[k % 4][:], ACT.Copy).then_inc(w_hi_ready, 1)

            def step(t, u):
                if not (t_known(t) and t == 0):
                    z_part(t, u)
                if not (t_known(t) and t + 2 > DEC):
                    silu(t + 2, u)

            step(0, 0)
            step(1, 1)
            with act.Fori(1, TILES // 2 - 1) as i:
                step(i * 2, 0)
                step(i * 2 + 1, 1)
            for t in range(TILES - 2, DEC + 1):
                step(t, t % 2)

        @block.vector
        def _(dve):
            def split_w(k):
                dve.wait_ge(w_hi_ready, k + 1)
                nc.vector.tensor_tensor(w_lo[:, k, :], w_raw[k % 4][:], w_hi[:, k, :].bitcast(F32), ALU.subtract).then_inc(w_lo_ready, 1)

            def split_z(t, u):
                dve.wait_ge(z_hi_ready, t + 1)
                nc.vector.tensor_tensor(z_lo[u][:].rearrange("p k n -> p (k n)"), ps_zT[u][:],
                                        z_hi[u][:].rearrange("p k n -> p (k n)").bitcast(F32), ALU.subtract).then_inc(z_lo_ready, 1)

            def apply(t, u):
                dve.wait_ge(gate_ready, t + 1)
                dve.wait_ge(o_loaded[u], 2 * loads(t, u))
                wait(dve, z_turned, t - 1)
                nc.vector.tensor_tensor(z[u][:], o_tok[u][:], g_tok[u][:], ALU.mult).then_inc(z_ready, 1)

            apply(0, 0)
            split_z(0, 0)
            for k in range(KT):
                split_w(k)

            def step(t, u):
                if not (t_known(t) and t == DEC):
                    apply(t + 1, 1 - u)
                if not (t_known(t) and t == 0):
                    split_z(t, u)
                    add(t - 1, 1 - u)

            def add(t, u):
                dve.wait_ge(x_loaded[u], loads(t, u))
                wait(dve, y_stored[u], 8 * t - 8 * u)
                for j in range(2):
                    cols = slice(j * 512, (j + 1) * 512)
                    dve.wait_ge(y_summed, 2 * t + j + 1)
                    nc.vector.tensor_tensor(y_tok[u][:, cols], ps_y[u][:, cols], x_tok[u][:, cols], ALU.add).then_inc(y_ready, 1)

            tiles(dve, step)
            add(DEC, 0)

        @block.tensor
        def _(pe):
            def turn(t, u):
                pe.wait_ge(z_ready, t + 1)
                wait(pe, z_lo_ready, t - 1)
                for k in range(KT):
                    last = nc.tensor.transpose(ps_zT[u][:, k * P:(k + 1) * P], z[u][:].rearrange("p g d -> p (g d)")[:, k * P:(k + 1) * P],
                                               ident[:])
                last.then_inc(z_turned, 1)

            pe.wait_ge(ident_ready, 1)
            turn(0, 0)

            def products(u, j, k):
                cols = slice(j * 512, (j + 1) * 512)
                for i, (a, w) in enumerate(((z_hi, w_hi), (z_hi, w_lo), (z_lo, w_hi))):
                    mm = nc.tensor.matmul(ps_y[u][:, cols], a[u][:, k, :], w[:, k, cols], start=(k == 0 and i == 0),
                                          stop=(k == KT - 1 and i == 2))
                if k == KT - 1:
                    mm.then_inc(y_summed, 1)

            def step(t, u):
                if t_known(t) and t == 0:
                    pe.wait_ge(z_lo_ready, 1)
                    for k in range(KT):
                        pe.wait_ge(w_lo_ready, k + 1)
                        for j in range(2):
                            products(u, j, k)
                    turn(1, 1)
                    return
                if not (t_known(t) and t == DEC):
                    turn(t + 1, 1 - u)
                pe.wait_ge(z_lo_ready, t + 1)
                wait(pe, y_ready, 2 * (t - 1))
                for j in range(2):
                    for k in range(KT):
                        products(u, j, k)

            tiles(pe, step)



_INS = ["x_prompt", "x_sample", "cache_attn_k", "cache_attn_v", "state_rwkv_wkv", "state_rwkv_shift", "norm_gain",
        "w_in", "q_norm_gain", "k_norm_gain", "rel_pos_bias", "shift_mix", "decay_base", "decay_lora_up", "iclr_base",
        "iclr_lora_up", "key_remove_scale", "key_iclr_scale", "bonus_scale", "out_norm_gain", "out_norm_bias", "w_out"]
_OUTS = [("y_prompt", (1, TILES * P, D)), ("y_sample", (NS, SL, D)),
         ("k_prompt_new", (1, 1, H, 512, HD)), ("v_prompt_new", (1, 1, H, 512, HD)),
         ("k_sample_new", (1, NS, H, SL, HD)), ("v_sample_new", (1, NS, H, SL, HD)),
         ("wkv_prompt_new", (1, 1, H, HD, HD)), ("wkv_sample_new", (1, NS, H, HD, HD)),
         ("shift_prompt_new", (1, 1, 1, SHIFT_COLS)), ("shift_sample_new", (1, NS, 1, SHIFT_COLS))]
_SCRATCH = [("xT", (TILES + 1, P, KT, P)), ("o_att", ((TILES + 1) * P, AW)), ("o_rwkv", ((TILES + 1) * P, AW)),
            ("gates", ((TILES + 1) * P, D)), ("proj_T", (SHIFT_TILES, P, 1 + (TILES + 1) * P)), ("rev_table", (H, P, 3 * P)), ("qT_new", (P, PAIRS, P)), ("kT_new", (P, PAIRS, P)), ("v_new", (P, AW)), ("k_new", (P, AW))]


def program(nc, io):
    attention_phase(nc, io)
    cached_attention_phase(nc, io)
    rwkv_projection_phase(nc, io)
    rwkv_phase(nc, io)
    output_phase(nc, io)


def kernel(**inputs):
    import numpy as _np
    import concourse.bacc as _bacc
    from concourse.bass_utils import run_bass_kernel_spmd as _run

    nc = _bacc.Bacc("TRN2", target_bir_lowering=False, num_devices=1)
    arrays, io = {}, {}
    for name in _INS:
        a = _np.ascontiguousarray(inputs[name])
        arrays[f"in_{name}"] = a
        io[name] = nc.dram_tensor(f"in_{name}", a.shape, F32, kind="ExternalInput").ap()
    arrays["shape_consts"] = _np.ascontiguousarray(_np.concatenate(list(shape_constants().values()), 1))
    io["shape_consts"] = nc.dram_tensor("shape_consts", (P, CONST_W), F32, kind="ExternalInput").ap()
    for name, shape in _OUTS:
        io[name] = nc.dram_tensor(f"out_{name}", shape, F32, kind="ExternalOutput").ap()
    for name, shape in _SCRATCH:
        io[name] = nc.dram_tensor(f"scratch_{name}", shape, F32, kind="Internal").ap()
    program(nc, io)
    r = _run(nc, [arrays], core_ids=[0])
    return tuple(r.results[0][f"out_{name}"] for name, _ in _OUTS)
```
